# Optimizing a Trainium2 kernel written in Bass

```python
import jax, jax.numpy as jnp
from jax import lax
import numpy as np
import math

D_MODEL = 2048
BATCH = 1
SEQ = 256
DEPTH = 1

CONV_WIDTH = D_MODEL // 2
CONV_K = 3
HEAD_DIM = 128
ATTN_WIDTH = D_MODEL // 2
N_HEADS = ATTN_WIDTH // HEAD_DIM
D_FF = 4 * D_MODEL
BLOCK_Q = 128
EPS = 1e-6

SPLIT_SIZES = (CONV_WIDTH, CONV_WIDTH, CONV_WIDTH,
               ATTN_WIDTH, ATTN_WIDTH, ATTN_WIDTH,
               N_HEADS, D_MODEL, D_MODEL)
IN_COLS = sum(SPLIT_SIZES)
SPLIT_POINTS = tuple(int(v) for v in np.cumsum(SPLIT_SIZES)[:-1])


def rmsnorm(x, g):
    xf = x.astype(jnp.float32)
    y = xf * lax.rsqrt(jnp.mean(xf * xf, axis=-1, keepdims=True) + EPS)
    return (y * g.astype(jnp.float32)).astype(x.dtype)

def causal_dwconv(u, w):
    s = u.shape[1]
    up = jnp.pad(u, ((0, 0), (CONV_K - 1, 0), (0, 0)))
    y = w[0] * up[:, 0:s, :]
    for j in range(1, CONV_K):
        y = y + w[j] * up[:, j:j + s, :]
    return y

def forgetting_attention(q, k, v, log_f):
    b, s, h, d = q.shape
    nb = s // BLOCK_Q
    c = jnp.cumsum(log_f, axis=1).transpose(0, 2, 1)
    qh = q.transpose(0, 2, 1, 3)
    kh = k.transpose(0, 2, 1, 3)
    vh = v.transpose(0, 2, 1, 3)
    scale = float(d) ** -0.5
    q_blocks = qh.reshape(b, h, nb, BLOCK_Q, d).transpose(2, 0, 1, 3, 4)
    c_blocks = c.reshape(b, h, nb, BLOCK_Q).transpose(2, 0, 1, 3)
    k_pos = jnp.arange(s)

    def one_block(args):
        qb, cb, i = args
        logits = jnp.einsum('bhqd,bhkd->bhqk', qb, kh).astype(jnp.float32) * scale
        logits = logits + cb[..., :, None] - c[..., None, :]
        q_pos = i * BLOCK_Q + jnp.arange(BLOCK_Q)
        causal = k_pos[None, :] <= q_pos[:, None]
        logits = jnp.where(causal, logits, -jnp.inf)
        p = jax.nn.softmax(logits, axis=-1)
        return jnp.einsum('bhqk,bhkd->bhqd', p.astype(vh.dtype), vh)

    out = lax.map(one_block, (q_blocks, c_blocks, jnp.arange(nb)))
    return out.transpose(1, 0, 3, 2, 4).reshape(b, s, h * d)

def first_inputs(seed: int = 0) -> dict:
    key = jax.random.key(seed)
    ks = jax.random.split(key, 14)
    nrm = jax.random.normal
    x = nrm(ks[0], (BATCH, SEQ, D_MODEL), jnp.float32)
    g_mix = 1.0 + 0.02 * nrm(ks[1], (DEPTH, D_MODEL), jnp.float32)
    w_in = nrm(ks[2], (DEPTH, D_MODEL, IN_COLS), jnp.float32) * D_MODEL ** -0.5
    b_f = 2.0 + 0.5 * nrm(ks[3], (DEPTH, N_HEADS), jnp.float32)
    b_gate = 0.02 * nrm(ks[4], (DEPTH, 2 * D_MODEL), jnp.float32)
    conv_w = nrm(ks[5], (DEPTH, CONV_K, CONV_WIDTH), jnp.float32) * CONV_K ** -0.5
    w_conv_out = nrm(ks[6], (DEPTH, CONV_WIDTH, D_MODEL), jnp.float32) * CONV_WIDTH ** -0.5
    w_attn_out = nrm(ks[7], (DEPTH, ATTN_WIDTH, D_MODEL), jnp.float32) * ATTN_WIDTH ** -0.5
    w_mix_out = nrm(ks[8], (DEPTH, D_MODEL, D_MODEL), jnp.float32) * D_MODEL ** -0.5
    g_mlp = 1.0 + 0.02 * nrm(ks[9], (DEPTH, D_MODEL), jnp.float32)
    w_ff1 = nrm(ks[10], (DEPTH, D_MODEL, D_FF), jnp.float32) * D_MODEL ** -0.5
    w_ff2 = nrm(ks[11], (DEPTH, D_FF, D_MODEL), jnp.float32) * D_FF ** -0.5
    g_final = 1.0 + 0.02 * nrm(ks[12], (D_MODEL,), jnp.float32)
    return {"x": x, "g_mix": g_mix, "w_in": w_in, "b_f": b_f, "b_gate": b_gate,
            "conv_w": conv_w, "w_conv_out": w_conv_out, "w_attn_out": w_attn_out,
            "w_mix_out": w_mix_out, "g_mlp": g_mlp, "w_ff1": w_ff1, "w_ff2": w_ff2,
            "g_final": g_final}

def first_block(x, g_mix, w_in, b_f, b_gate, conv_w, w_conv_out, w_attn_out,
              w_mix_out, g_mlp, w_ff1, w_ff2, g_final):
    b, s, _ = x.shape
    for l in range(DEPTH):
        h = rmsnorm(x, g_mix[l])
        z = jnp.einsum('bsd,dc->bsc', h, w_in[l])
        cb, cc, cv, q, k, v, f_logit, gate_c, gate_a = jnp.split(z, SPLIT_POINTS, axis=-1)

        conv_y = cb * causal_dwconv(cc * cv, conv_w[l])
        conv_branch = jnp.einsum('bsc,cd->bsd', conv_y, w_conv_out[l])

        log_f = jax.nn.log_sigmoid(f_logit.astype(jnp.float32) + b_f[l].astype(jnp.float32))
        attn = forgetting_attention(q.reshape(b, s, N_HEADS, HEAD_DIM),
                                    k.reshape(b, s, N_HEADS, HEAD_DIM),
                                    v.reshape(b, s, N_HEADS, HEAD_DIM), log_f)
        attn_branch = jnp.einsum('bsc,cd->bsd', attn, w_attn_out[l])

        gc = jax.nn.sigmoid(gate_c + b_gate[l, :D_MODEL])
        ga = jax.nn.sigmoid(gate_a + b_gate[l, D_MODEL:])
        merged = gc * conv_branch + ga * attn_branch
        x = x + jnp.einsum('bsd,de->bse', merged, w_mix_out[l])

        h = rmsnorm(x, g_mlp[l])
        u = jnp.square(jax.nn.relu(jnp.einsum('bsd,df->bsf', h, w_ff1[l])))
        x = x + jnp.einsum('bsf,fd->bsd', u, w_ff2[l])
    return rmsnorm(x, g_final)


ATTN_WIDTH_2 = D_MODEL // 2
ATTN_HEAD_DIM = 128
N_ATTN_HEADS = ATTN_WIDTH_2 // ATTN_HEAD_DIM
SSM_WIDTH = D_MODEL - ATTN_WIDTH_2
SSM_HEAD_DIM = 64
N_SSM_HEADS = SSM_WIDTH // SSM_HEAD_DIM
N_SSM_GROUPS = 2
SSM_HEADS_PER_GROUP = N_SSM_HEADS // N_SSM_GROUPS
D_STATE = 128
SSM_CONV = 4
SSM_CHUNK = 256
SSM_CONV_CH = SSM_WIDTH + 2 * N_SSM_GROUPS * D_STATE
MOBA_BLOCK = 256
MOBA_TOPK = 3
MOBA_Q_CHUNK = 32
REL_BUCKETS = 32
REL_MAX_DIST = 128
FFN_DIM = 5632
FFN_CONV = 3
IN_COLS_2 = 3 * ATTN_WIDTH_2 + 2 * SSM_WIDTH + 2 * N_SSM_GROUPS * D_STATE + N_SSM_HEADS


def rms_norm(x, g):
    xf = x.astype(jnp.float32)
    y = xf * lax.rsqrt(jnp.mean(xf * xf, axis=-1, keepdims=True) + EPS)
    return (y * g.astype(jnp.float32)).astype(x.dtype)

def causal_dwconv_2(x, w, b):
    k = w.shape[0]
    y = lax.conv_general_dilated(x, w[:, None, :].astype(x.dtype), window_strides=(1,),
                                 padding=[(k - 1, 0)], dimension_numbers=('NWC', 'WIO', 'NWC'),
                                 feature_group_count=x.shape[-1])
    return y + b.astype(x.dtype)

def pad_seq(x, mult):
    p = (-x.shape[1]) % mult
    return jnp.pad(x, [(0, 0), (0, p)] + [(0, 0)] * (x.ndim - 2))

def rel_bucket(dist):
    n = jnp.maximum(dist, 0)
    max_exact = REL_BUCKETS // 2
    nf = jnp.maximum(n, max_exact).astype(jnp.float32)
    large = max_exact + (jnp.log(nf / max_exact) / math.log(REL_MAX_DIST / max_exact)
                         * (REL_BUCKETS - max_exact)).astype(jnp.int32)
    large = jnp.minimum(large, REL_BUCKETS - 1)
    return jnp.where(n < max_exact, n, large)

def gather_blocks(blocks, sel):
    return jax.vmap(jax.vmap(lambda kb, s: kb[s]))(blocks, sel)

def moba_attention(q, k, v, rel_bias):
    bsz, s = q.shape[:2]
    q, k, v = [pad_seq(t, MOBA_BLOCK).transpose(0, 2, 1, 3) for t in (q, k, v)]
    sp = q.shape[2]
    nb = sp // MOBA_BLOCK
    n_sel = min(MOBA_TOPK, nb - 1)
    k_blocks = k.reshape(bsz, N_ATTN_HEADS, nb, MOBA_BLOCK, ATTN_HEAD_DIM)
    v_blocks = v.reshape(bsz, N_ATTN_HEADS, nb, MOBA_BLOCK, ATTN_HEAD_DIM)
    k_mean = jnp.mean(k_blocks, axis=3)
    scale = ATTN_HEAD_DIM ** -0.5
    bias_t = rel_bias.T.astype(jnp.float32)
    head_idx = jnp.arange(N_ATTN_HEADS)[:, None, None, None]

    def chunk(ci):
        q0 = ci * MOBA_Q_CHUNK
        blk = q0 // MOBA_BLOCK
        qc = lax.dynamic_slice_in_dim(q, q0, MOBA_Q_CHUNK, axis=2)
        q_pos = q0 + jnp.arange(MOBA_Q_CHUNK)
        k_own = lax.dynamic_index_in_dim(k_blocks, blk, axis=2, keepdims=False)
        v_own = lax.dynamic_index_in_dim(v_blocks, blk, axis=2, keepdims=False)
        dist_own = q_pos[:, None] - (blk * MOBA_BLOCK + jnp.arange(MOBA_BLOCK))[None, :]
        logit_own = (jnp.einsum('bhqd,bhkd->bhqk', qc, k_own).astype(jnp.float32) * scale
                     + bias_t[:, rel_bucket(dist_own)])
        logit_own = jnp.where(dist_own >= 0, logit_own, -jnp.inf)
        if n_sel == 0:
            p_own = jax.nn.softmax(logit_own, axis=-1).astype(v.dtype)
            return jnp.einsum('bhqk,bhkd->bhqd', p_own, v_own)
        gate = jnp.einsum('bhqd,bhnd->bhqn', qc, k_mean).astype(jnp.float32)
        gate = jnp.where(jnp.arange(nb) < blk, gate, -jnp.inf)
        _, sel = lax.top_k(gate, n_sel)
        k_sel = gather_blocks(k_blocks, sel)
        v_sel = gather_blocks(v_blocks, sel)
        sel_pos = sel[..., None] * MOBA_BLOCK + jnp.arange(MOBA_BLOCK)
        dist_sel = q_pos[:, None, None] - sel_pos
        logit_sel = (jnp.einsum('bhqd,bhqtkd->bhqtk', qc, k_sel).astype(jnp.float32) * scale
                     + bias_t[head_idx, rel_bucket(dist_sel)])
        slot_ok = (jnp.arange(n_sel) < blk)[:, None]
        logit_sel = jnp.where(slot_ok, logit_sel, -jnp.inf)
        logits = jnp.concatenate(
            [logit_sel.reshape(bsz, N_ATTN_HEADS, MOBA_Q_CHUNK, n_sel * MOBA_BLOCK), logit_own], axis=-1)
        p = jax.nn.softmax(logits, axis=-1).astype(v.dtype)
        p_sel = p[..., :n_sel * MOBA_BLOCK].reshape(bsz, N_ATTN_HEADS, MOBA_Q_CHUNK, n_sel, MOBA_BLOCK)
        p_own = p[..., n_sel * MOBA_BLOCK:]
        return (jnp.einsum('bhqtk,bhqtkd->bhqd', p_sel, v_sel)
                + jnp.einsum('bhqk,bhkd->bhqd', p_own, v_own))

    out = lax.map(chunk, jnp.arange(sp // MOBA_Q_CHUNK))
    out = out.transpose(1, 0, 3, 2, 4).reshape(bsz, sp, N_ATTN_HEADS * ATTN_HEAD_DIM)
    return out[:, :s]

def segsum(x):
    t = x.shape[-1]
    xe = jnp.broadcast_to(x[..., :, None], x.shape + (t,))
    xe = jnp.where(jnp.tril(jnp.ones((t, t), bool), -1), xe, 0.0)
    xs = jnp.cumsum(xe, axis=-2)
    return jnp.where(jnp.tril(jnp.ones((t, t), bool)), xs, -jnp.inf)

def ssd_mixer(xs, z, bmat, cmat, dt_raw, conv_w, conv_b, dt_bias, a_log, d_skip, norm_g):
    bsz, s = xs.shape[:2]
    gn = N_SSM_GROUPS * D_STATE
    xbc = jax.nn.silu(causal_dwconv_2(jnp.concatenate([xs, bmat, cmat], axis=-1), conv_w, conv_b))
    x_h = xbc[..., :SSM_WIDTH].reshape(bsz, s, N_SSM_HEADS, SSM_HEAD_DIM).astype(jnp.float32)
    bm = xbc[..., SSM_WIDTH:SSM_WIDTH + gn].astype(jnp.float32)
    cm = xbc[..., SSM_WIDTH + gn:].astype(jnp.float32)
    dt = jax.nn.softplus(dt_raw.astype(jnp.float32) + dt_bias.astype(jnp.float32))
    a = -jnp.exp(a_log.astype(jnp.float32))
    xdt = pad_seq(x_h * dt[..., None], SSM_CHUNK)
    adt = pad_seq(dt * a, SSM_CHUNK)
    bm, cm = pad_seq(bm, SSM_CHUNK), pad_seq(cm, SSM_CHUNK)
    sp = xdt.shape[1]
    nc = sp // SSM_CHUNK
    X = xdt.reshape(bsz, nc, SSM_CHUNK, N_SSM_GROUPS, SSM_HEADS_PER_GROUP, SSM_HEAD_DIM)
    A = adt.reshape(bsz, nc, SSM_CHUNK, N_SSM_GROUPS, SSM_HEADS_PER_GROUP).transpose(0, 3, 4, 1, 2)
    Bm = bm.reshape(bsz, nc, SSM_CHUNK, N_SSM_GROUPS, D_STATE)
    Cm = cm.reshape(bsz, nc, SSM_CHUNK, N_SSM_GROUPS, D_STATE)
    A_cs = jnp.cumsum(A, axis=-1)
    Lm = jnp.exp(segsum(A))
    y_diag = jnp.einsum('bclgn,bcsgn,bgrcls,bcsgrp->bclgrp', Cm, Bm, Lm, X)
    decay_states = jnp.exp(A_cs[..., -1:] - A_cs)
    states = jnp.einsum('bclgn,bgrcl,bclgrp->bcgrpn', Bm, decay_states, X)
    states = jnp.concatenate([jnp.zeros_like(states[:, :1]), states], axis=1)
    chunk_tot = jnp.pad(A_cs[..., -1], ((0, 0), (0, 0), (0, 0), (1, 0)))
    decay_chunk = jnp.exp(segsum(chunk_tot))
    new_states = jnp.einsum('bgrzc,bcgrpn->bzgrpn', decay_chunk, states)
    prev_states = new_states[:, :-1]
    y_off = jnp.einsum('bclgn,bcgrpn,bgrcl->bclgrp', Cm, prev_states, jnp.exp(A_cs))
    y = (y_diag + y_off).reshape(bsz, sp, N_SSM_HEADS, SSM_HEAD_DIM)[:, :s]
    y = y + d_skip.astype(jnp.float32)[:, None] * x_h
    y = y.reshape(bsz, s, SSM_WIDTH) * jax.nn.silu(z.astype(jnp.float32))
    yg = y.reshape(bsz, s, N_SSM_GROUPS, SSM_WIDTH // N_SSM_GROUPS)
    yg = yg * lax.rsqrt(jnp.mean(yg * yg, axis=-1, keepdims=True) + EPS)
    return (yg.reshape(bsz, s, SSM_WIDTH) * norm_g.astype(jnp.float32)).astype(xs.dtype)

def conv_ffn(h, w_up, conv_w, conv_b, w_down):
    u = causal_dwconv_2(h @ w_up, conv_w, conv_b)
    g, val = jnp.split(u, 2, axis=-1)
    return (jax.nn.silu(g) * val) @ w_down

def second_inputs(seed: int = 0) -> dict:
    key = jax.random.key(seed)
    ks = jax.random.split(key, 24)
    f32 = jnp.float32
    nrm = lambda k, shape, sc: jax.random.normal(k, shape, f32) * sc
    dt0 = jnp.exp(jax.random.uniform(ks[10], (DEPTH, N_SSM_HEADS), f32)
                  * (math.log(0.1) - math.log(0.001)) + math.log(0.001))
    return {
        'x': nrm(ks[0], (BATCH, SEQ, D_MODEL), 1.0),
        'c': nrm(ks[1], (BATCH, D_MODEL), 1.0),
        'w_ada': nrm(ks[2], (DEPTH, D_MODEL, 6 * D_MODEL), 0.5 * D_MODEL ** -0.5),
        'b_ada': nrm(ks[3], (DEPTH, 6 * D_MODEL), 0.01),
        'norm_mix_g': 1.0 + nrm(ks[4], (DEPTH, D_MODEL), 0.05),
        'w_in': nrm(ks[5], (DEPTH, D_MODEL, IN_COLS_2), D_MODEL ** -0.5),
        'rel_bias': nrm(ks[6], (REL_BUCKETS, N_ATTN_HEADS), 0.2),
        'attn_norm_g': 1.0 + nrm(ks[7], (DEPTH, ATTN_WIDTH_2), 0.05),
        'conv_ssm_w': nrm(ks[8], (DEPTH, SSM_CONV, SSM_CONV_CH), SSM_CONV ** -0.5),
        'conv_ssm_b': nrm(ks[9], (DEPTH, SSM_CONV_CH), 0.01),
        'dt_bias': dt0 + jnp.log(-jnp.expm1(-dt0)),
        'a_log': jnp.log(jax.random.uniform(ks[11], (DEPTH, N_SSM_HEADS), f32, 1.0, 16.0)),
        'd_skip': 1.0 + nrm(ks[12], (DEPTH, N_SSM_HEADS), 0.1),
        'ssm_norm_g': 1.0 + nrm(ks[13], (DEPTH, SSM_WIDTH), 0.05),
        'w_out': nrm(ks[14], (DEPTH, ATTN_WIDTH_2 + SSM_WIDTH, D_MODEL), (ATTN_WIDTH_2 + SSM_WIDTH) ** -0.5),
        'norm_ffn_g': 1.0 + nrm(ks[15], (DEPTH, D_MODEL), 0.05),
        'w_up': nrm(ks[16], (DEPTH, D_MODEL, 2 * FFN_DIM), D_MODEL ** -0.5),
        'conv_ffn_w': nrm(ks[17], (DEPTH, FFN_CONV, 2 * FFN_DIM), FFN_CONV ** -0.5),
        'conv_ffn_b': nrm(ks[18], (DEPTH, 2 * FFN_DIM), 0.01),
        'w_down': nrm(ks[19], (DEPTH, FFN_DIM, D_MODEL), FFN_DIM ** -0.5),
        'final_norm_g': 1.0 + nrm(ks[20], (D_MODEL,), 0.05),
    }

def second_block(x, c, w_ada, b_ada, norm_mix_g, w_in, rel_bias, attn_norm_g, conv_ssm_w, conv_ssm_b,
              dt_bias, a_log, d_skip, ssm_norm_g, w_out, norm_ffn_g, w_up, conv_ffn_w, conv_ffn_b,
              w_down, final_norm_g):
    bsz, s, _ = x.shape
    gn = N_SSM_GROUPS * D_STATE
    sizes = [ATTN_WIDTH_2, ATTN_WIDTH_2, ATTN_WIDTH_2, SSM_WIDTH, SSM_WIDTH, gn, gn, N_SSM_HEADS]
    split_at = [int(v) for v in np.cumsum(sizes)[:-1]]
    for l in range(DEPTH):
        mod = jax.nn.silu(c) @ w_ada[l] + b_ada[l]
        shift_m, scale_m, gate_m, shift_f, scale_f, gate_f = jnp.split(mod[:, None, :], 6, axis=-1)
        h = rms_norm(x, norm_mix_g[l]) * (1.0 + scale_m) + shift_m
        proj = h @ w_in[l]
        q, k, v, xs, z, bmat, cmat, dt_raw = jnp.split(proj, split_at, axis=-1)
        hd = (bsz, s, N_ATTN_HEADS, ATTN_HEAD_DIM)
        attn = moba_attention(q.reshape(hd), k.reshape(hd), v.reshape(hd), rel_bias)
        attn = rms_norm(attn, attn_norm_g[l])
        ssm = ssd_mixer(xs, z, bmat, cmat, dt_raw, conv_ssm_w[l], conv_ssm_b[l], dt_bias[l],
                        a_log[l], d_skip[l], ssm_norm_g[l])
        mix = jnp.concatenate([attn, ssm], axis=-1) @ w_out[l]
        x = x + gate_m * mix
        h = rms_norm(x, norm_ffn_g[l]) * (1.0 + scale_f) + shift_f
        x = x + gate_f * conv_ffn(h, w_up[l], conv_ffn_w[l], conv_ffn_b[l], w_down[l])
    return rms_norm(x, final_norm_g)


def setup_inputs(seed=0):
    out = dict(first_inputs(seed))
    for name, value in second_inputs(seed + 1).items():
        if name != "x":
            out[name + "_2"] = value
    return out


def reference(
    x, g_mix, w_in, b_f, b_gate, conv_w, w_conv_out, w_attn_out, w_mix_out, g_mlp, w_ff1, w_ff2,
    g_final, c_2, w_ada_2, b_ada_2, norm_mix_g_2, w_in_2, rel_bias_2, attn_norm_g_2,
    conv_ssm_w_2, conv_ssm_b_2, dt_bias_2, a_log_2, d_skip_2, ssm_norm_g_2, w_out_2,
    norm_ffn_g_2, w_up_2, conv_ffn_w_2, conv_ffn_b_2, w_down_2, final_norm_g_2,
):
    x = first_block(
        x, g_mix, w_in, b_f, b_gate, conv_w, w_conv_out, w_attn_out, w_mix_out, g_mlp, w_ff1,
        w_ff2, g_final,
    )
    return second_block(
        x, c_2, w_ada_2, b_ada_2, norm_mix_g_2, w_in_2, rel_bias_2, attn_norm_g_2, conv_ssm_w_2,
        conv_ssm_b_2, dt_bias_2, a_log_2, d_skip_2, ssm_norm_g_2, w_out_2, norm_ffn_g_2, w_up_2,
        conv_ffn_w_2, conv_ffn_b_2, w_down_2, final_norm_g_2,
    )


_drawn_inputs = setup_inputs


def setup_inputs(seed=0):
    import zlib

    import numpy as np

    out = dict(_drawn_inputs(seed))
    spreads = {}
    factors = {'g_mix': 2.786,
     'b_gate': 8.0,
     'g_mlp': 3.231,
     'g_final': 2.797,
     'b_ada_2': 3.964,
     'norm_mix_g_2': 3.108,
     'rel_bias_2': 3.818,
     'attn_norm_g_2': 5.19,
     'conv_ssm_b_2': 32.357,
     'd_skip_2': 196.433,
     'ssm_norm_g_2': 5.956,
     'norm_ffn_g_2': 3.938,
     'conv_ffn_b_2': 21.662}
    for name, (base, spread) in spreads.items():
        noise = np.random.default_rng([zlib.crc32(name.encode()), seed]).standard_normal(out[name].shape)
        drawn = base * np.exp(spread * noise) if base else spread * noise
        out[name] = __import__('jax').numpy.asarray(drawn.astype(out[name].dtype))
    for name, factor in factors.items():
        out[name] = (out[name] * factor).astype(out[name].dtype)
    return out
```

```python
from contextlib import ExitStack

import numpy as np

import concourse.bass as bass
from concourse import mybir
from concourse.alu_op_type import AluOpType as ALU

F32 = mybir.dt.float32
F32R = mybir.dt.float32r
ACT = mybir.ActivationFunctionType
AX_X = mybir.AxisListType.X

P = 128
T = 256
D = 2048
NC = D // P
EPS = 1e-6
FAR = -1e30
N_HEADS = 8
HEAD_SCALE = float(P) ** -0.5
SSM_HEADS = 16
SSM_DIM = 64
FF = 8192
FF_GROUPS = 4
FF_BLOCKS = FF // P // FF_GROUPS
FFN = 5632
FFN_GROUPS = 4
FFN_BLOCKS = FFN // P // FFN_GROUPS
FIRST_CHUNKS = 8
PIECE = FIRST_CHUNKS * P
ADA_COLS = 1024
ADA_GROUPS = 6 * D // ADA_COLS
CONV_CH = 12
REL_BUCKETS, REL_MAX_DIST = 32, 128
REL_W = 384

VEC_SIZES = [("g_mix", 16), ("g_mlp", 16), ("b_gate", 32), ("conv_w", 24), ("b_f", 8), ("g_final", 16),
             ("c", 16), ("b_ada", 96), ("g_mix2", 16), ("g_attn", 8), ("ssm_w", 48), ("ssm_b", 12),
             ("dt_bias", 16), ("a_log", 16), ("d_skip", 8), ("g_ssm", 8), ("g_ffn", 16),
             ("ffn_w", 264), ("ffn_b", 88), ("g_out", 16)]
VEC_AT, _n = {}, 0
for _name, _size in VEC_SIZES:
    VEC_AT[_name] = _n
    _n += _size
VEC_N = _n

IDENT_AT, LEOL_AT, ONEGT_AT, MASK_AT, FLIP_AT, CONST_N = 0, 128, 512, 768, 1152, 1280

GROUP1 = 2 * FF_BLOCKS
GROUP2 = 2 * FFN_BLOCKS + NC
STREAM = [("gate", 32), ("conv_in", 16), ("conv_mul", 8), ("qk", 16), ("v", 8), ("branch", 16), ("mix", 16),
          ("ff", FF_GROUPS * GROUP1), ("in2", 32), ("in2_conv", CONV_CH), ("out2", 16),
          ("ffn", FFN_GROUPS * GROUP2)]
PAIR0, _n = {}, 0
for _name, _size in STREAM:
    PAIR0[_name] = _n
    _n += _size // 2
ADA0 = {"gate": 0, "conv_in": 32, "qk": 48, "ff": 64}
NORMS = ["n1", "n2", "n3", "n3b", "na", "ng0", "ng1", "n4", "n5"]
NTH = {_name: _i + 1 for _i, _name in enumerate(NORMS)}
CHUNKS = {"h%d" % (_i + 1): NC * _i for _i in range(5)}
TAPS = {"conv_mul": 0, "in2_conv": 24, "up": 24 + 3 * CONV_CH}
CREDIT = 4


def build(nc, t):
    with ExitStack() as ctx:
        base = (nc.sbuf_base + 31) // 32 * 32
        ctx.enter_context(nc.sbuf_tensor("arena", [P, (NC * 2 * T) + 8], F32))

        def sb(name, shape, dt=F32):
            return ctx.enter_context(nc.sbuf_tensor(name, shape, dt))

        sems = {}

        def sem(name):
            if name not in sems:
                sems[name] = ctx.enter_context(nc.semaphore(name.replace(".", "_")))
            return sems[name]

        U = nc.alloc_sbuf_tensor_at("U", [P, NC, 2 * T], F32R, offset=base)
        G = nc.alloc_sbuf_tensor_at("G", [P, NC, 2, T], F32, offset=base)
        X = sb("X", [P, NC, T])
        H = sb("H", [P, NC, 2 * T], F32R)
        Z = sb("Z", [P, 44, T])
        w_raw = sb("w_raw", [P, 4, PIECE])
        w_hi = sb("w_hi", [P, 4, PIECE], F32R)
        w_lo = sb("w_lo", [P, 4, PIECE], F32R)
        ada_w = sb("ada_w", [P, 2, ADA_COLS])
        ada_acc = Z[:, 40:44, :].rearrange("p a t -> p (a t)")
        vec = sb("vec", [P, VEC_N])
        con = sb("con", [P, CONST_N])
        ones = sb("ones", [P, P])
        epsb = sb("epsb", [P, 1])
        R = sb("R", [P, T])
        ss = sb("ss", [P, T])
        scratch = sb("scratch", [P, 3072])
        small = sb("small", [P, 496])
        mod = sb("mod", [P, 96])
        g1 = sb("g1", [P, NC])
        g2 = sb("g2", [P, NC])
        silu_c = sb("silu_c", [P, NC])
        wn = sb("wn", [P, NC * 32], F32R)
        wf = wn[:, 0:NC * 16].rearrange("p (k n) -> p k n", k=NC)
        wdt = wn[:, :].rearrange("p (k n) -> p k n", k=NC)
        wf_raw = scratch[:, 2816:2944].rearrange("p (k n) -> p k n", k=NC)
        wdt_raw = scratch[:, 2560:2816].rearrange("p (k n) -> p k n", k=NC)
        rel = sb("rel", [REL_BUCKETS + 1, 8])
        relhot = Z[0:REL_BUCKETS + 1, 36:38, :].rearrange("p a t -> p (a t)")[:, 0:REL_W]
        relrow = Z[0:8, 38:40, :].rearrange("p a t -> p (a t)")[:, 0:REL_W]

        bank = [ctx.enter_context(nc.psum_tensor(f"bank{i}", [P, 512], F32)) for i in range(8)]

        std = bank[4][:, T:2 * T]
        ident = con[:, IDENT_AT:IDENT_AT + P]
        LEOL = con[:, LEOL_AT:LEOL_AT + 384]
        LEO, LE = LEOL[:, 0:256], LEOL[:, 0:128]
        ONEGT = con[:, ONEGT_AT:ONEGT_AT + 256]
        GT = ONEGT[:, 128:256]
        MASK = con[:, MASK_AT:MASK_AT + 384]
        flip = con[:, FLIP_AT:FLIP_AT + P]

        def V(name, i=0, n=1):
            return vec[:, bass.ds(VEC_AT[name] + i, n)]

        def work(i):
            return scratch[:, i * T:(i + 1) * T]

        half = [work(0), work(1)]
        total = [work(2), work(3)]
        wide = [work(4), work(5)]
        conv = [work(6), work(7)]
        half2 = [work(8), work(9)]
        sig = [work(10), work(11)]

        adaf = ada_w[:, :, :].rearrange("p a b -> p (a b)")
        dec0 = [adaf[:, 0:256], adaf[:, 256:512]]
        dec1 = [adaf[:, 512:640], adaf[:, 640:768]]
        qs = [adaf[:, 768:1024], adaf[:, 1024:1280]]
        vtok = [adaf[:, 1280:1536], adaf[:, 1536:1792]]
        logit = [scratch[:, 0:384], scratch[:, 384:768]]
        probT = [scratch[:, 768:1152], scratch[:, 1152:1536]]
        relb = [scratch[:, 1536:1792], scratch[:, 1792:2048]]
        prob = [scratch[:, 2048:2432], scratch[:, 2432:2816]]

        def hi(buf, k, n=1):
            return buf[:, k:k + n, 0:T] if n > 1 else buf[:, k, 0:T]

        def flat(ap):
            return ap.rearrange("p a t -> p (a t)")

        def zb(i, n=1):
            return flat(Z[:, bass.ds(i, n), :])

        def xb(i, n=1):
            return flat(X[:, bass.ds(i, n), :])

        def ob(buf, i, part):
            return flat(buf[:, bass.ds(i, 1), part * T:(part + 1) * T])

        block = ctx.enter_context(nc.Block())

        def piece(sp, pair, s, tiles, tile_pair, first=False):
            if not first:
                sp.wait_ge(sem("w_split"), 4 * pair + s + 1)
            cols = tiles.shape[2]
            lo, up = (0, PIECE) if s % 2 == 0 else (PIECE, cols)
            if cols < 2 * PIECE:
                cut = (cols // P + 1) // 2 * P
                lo, up = (0, cut) if s % 2 == 0 else (cut, cols)
            src = tiles[bass.ds(2 * tile_pair + s // 2, 1), :, lo:up].rearrange("a p c -> (a p) c")
            sp.dma_start(w_raw[:, s, 0:up - lo], src).then_inc(sem("w_landed%d" % s), 16)

        def stream(sp, pair0, pairs, tiles, tile_pair0):
            with sp.Fori(0, pairs) as i:
                for s in range(4):
                    piece(sp, pair0 + i, s, tiles, tile_pair0 + i)

        def cast_high0(act, A, slot):
            act.wait_ge(sem("w_landed%d" % slot), 16)
            A(w_hi[:, slot, :], w_raw[:, slot, :], ACT.Copy).then_inc(sem("w_high"), 1)

        def ssm_y(dve, STT, j):
            dve.wait_ge(sem("ssm.out"), 2 * j + 2)
            STT(zb(32 + j), zb(32 + j), V("d_skip", j), bank[6 + j % 2][:, 0:256], ALU.mult, ALU.add)\
                .then_inc(sem("ssm.y"), 1)

        @block.sync
        def _(sp):
            for i in range(4):
                sp.dma_start(X[:, 4 * i:4 * i + 4, :], t["x"][:, 4 * i:4 * i + 4, :]).then_inc(sem("x_landed%d" % i), 16)
                if i == 0:
                    sp.dma_start(vec[:, :], t["vectors"]).then_inc(sem("vec_landed"), 16)
            for s in range(4):
                piece(sp, 0, s, t["w_gate"], 0, first=True)
            sp.dma_start(wf_raw[:, :, :], t["w_f"]).then_inc(sem("wf_landed"), 16)
            sp.dma_start(con[:, :], t["consts"]).then_inc(sem("con_landed"), 16)
            sp.dma_start(wdt_raw[:, :, :], t["w_dt"]).then_inc(sem("wdt_landed"), 16)
            sp.dma_start(rel[0:REL_BUCKETS, :], t["rel_bias"]).then_inc(sem("con_landed"), 16)
            stream(sp, PAIR0["gate"] + 1, 15, t["w_gate"], 1)
            stream(sp, PAIR0["conv_in"], PAIR0["branch"] - PAIR0["conv_in"], t["w_z"], 0)
            stream(sp, PAIR0["branch"], 8, t["w_branch"], 0)
            stream(sp, PAIR0["mix"], 8, t["w_mix"], 0)
            sp.wait_ge(sem("at1.out"), N_HEADS)
            sp.dma_start(relhot, t["rel_onehot"]).then_inc(sem("hot_landed"), 16)
            with sp.Fori(0, FF_GROUPS) as g:
                stream(sp, PAIR0["ff"] + 16 * g, 8, t["w_ff1"], 8 * g)
                stream(sp, PAIR0["ff"] + 16 * g + 8, 8, t["w_ff2"], 8 * g)
            stream(sp, PAIR0["in2"], 22, t["w_in2"], 0)
            stream(sp, PAIR0["out2"], 8, t["w_out2"], 0)
            with sp.Fori(0, FFN_GROUPS) as g:
                stream(sp, PAIR0["ffn"] + 19 * g, 11, t["w_up"], 11 * g)
                stream(sp, PAIR0["ffn"] + 19 * g + 11, 8, t["w_down"], 8 * g)
            for m in range(NC):
                sp.wait_ge(sem("final.out"), m + 1)
                sp.dma_start(t["out"][:, m, :], zb(m)).then_inc(sem("out_stored"), 16)
            sp.wait_ge(sem("out_stored"), 16 * NC)

        @block.tensor
        def _(pe):
            def mm(out, lhsT, rhs, start, stop):
                return nc.tensor.matmul(out, lhsT, rhs, start=start, stop=stop, skip_group_check=True)

            def pair_of_units(pair, buf, chunks, operand, operand_base=0, two_banks=False):
                cut = FIRST_CHUNKS if chunks == NC else (chunks + 1) // 2
                for par in range(2):
                    pe.wait_ge(sem("bank_read"), 2 * pair + par + 1)
                    for h, (k0, n) in enumerate(((0, cut), (cut, chunks - cut))):
                        pe.wait_ge(sem("w_split"), CREDIT + 4 * pair + 2 * par + h + 1)
                        dst = bank[2 * h + par] if two_banks else bank[par]
                        for c in range(n):
                            if par == 0 and operand and c % 4 == 0:
                                pe.wait_ge(sem(operand), operand_base + k0 + min(c + 4, n))
                            lhs = slice(c * P, (c + 1) * P)
                            start = c == 0 and (h == 0 or two_banks)
                            stop = c == n - 1 and (h == 1 or two_banks)
                            mm(dst[:, :], w_hi[:, 2 * par + h, lhs], buf[:, k0 + c, :], start, False)
                            end = mm(dst[:, T:2 * T], w_lo[:, 2 * par + h, lhs], buf[:, k0 + c, 0:T], False, stop)
                        end.then_inc(sem("piece_used"), 1)

            def ada_reduce(group):
                pe.wait_ge(sem("ada_acc"), 1 + 16 * group + 16)
                pe.wait_ge(sem("mod_ready"), group)
                for b in range(ADA_COLS // P):
                    last = mm(bank[5][:, b:b + 1], ada_acc[:, b * P:(b + 1) * P], ones[:, 0:1], b == 0, True)
                last.then_inc(sem("ada_reduced"), 1)

            def sum_squares(name):
                pe.wait_ge(sem("norm.squares"), NTH[name])
                if NTH[name] > 1:
                    pe.wait_ge(sem("norm.root"), NTH[name] - 1)
                mm(bank[4][:, 0:T], ones[:, :], ss[:, :], True, True).then_inc(sem("norm.summed"), 1)

            pe.wait_ge(sem("ones_ready"), 1)
            sum_squares("n1")
            for b in range(2):
                last = mm(bank[6][:, b:b + 1], ss[:, b * P:(b + 1) * P], ones[:, 0:1], b == 0, True)
            last.then_inc(sem("n1.tok"), 1)
            for g in range(2):
                with pe.Fori(0, 8) as i:
                    pair_of_units(PAIR0["gate"] + 8 * g + i, H, NC, "h_ready", CHUNKS["h1"])
                ada_reduce(g)
            pe.wait_ge(sem("wn_split"), 1)
            for b in range(2):
                for k in range(NC):
                    toks = slice(b * P, (b + 1) * P)
                    mm(bank[4][:, 32 * b:32 * b + 16], H[:, k, toks], wf[:, k, :], b == 0 and k == 0, False)
                    last = mm(bank[4][:, 32 * b:32 * b + 8], H[:, k, T + b * P:T + (b + 1) * P], wf[:, k, 0:8],
                              False, k == NC - 1)
            last.then_inc(sem("soft.logits"), 1)
            with pe.Fori(0, 8) as i:
                pair_of_units(PAIR0["conv_in"] + i, H, NC, None)
            ada_reduce(2)
            with pe.Fori(0, 4) as i:
                pair_of_units(PAIR0["conv_mul"] + i, H, NC, None)
            with pe.Fori(0, 8) as i:
                pair_of_units(PAIR0["qk"] + i, H, NC, None)
            ada_reduce(3)
            with pe.Fori(0, 4) as i:
                pair_of_units(PAIR0["v"] + i, H, NC, None)

            def attention(name, q0, k0, v0, decay):
                def scores(h):
                    s = bank[h % 2]
                    pe.wait_ge(sem(name + ".q_scaled"), h + 1)
                    if h >= 2:
                        pe.wait_ge(sem(name + ".exps"), 2 * h - 2)
                    q, k = qs[h % 2], zb(k0 + h)
                    mm(s[:, 0:128], q[:, 0:128], k[:, 0:128], True, False)
                    mm(s[:, 128:384], q[:, 128:256], k, False, False)
                    if decay:
                        pe.wait_ge(sem(name + ".decay_ready"), 2 * h + 2)
                        mm(s[:, 0:128], dec0[h % 2][:, 0:128], GT, False, False)
                        mm(s[:, 128:256], dec0[h % 2][:, 128:256], GT, False, False)
                        mm(s[:, 128:384], dec1[h % 2], ONEGT, False, False)
                        last = mm(s[:, 0:384], ident, MASK, False, True)
                    else:
                        pe.wait_ge(sem("relb_landed%d" % (h % 2)), 16 * (h // 2 + 1))
                        mm(s[:, 0:128], flip, relb[h % 2][:, 128:256], False, False)
                        last = mm(s[:, 128:384], flip, relb[h % 2], False, True)
                    last.then_inc(sem(name + ".scores"), 1)
                    v = zb(v0 + h)
                    if h >= 2:
                        pe.wait_ge(sem(name + ".v_copied"), h - 1)
                    for b in range(2):
                        last = nc.tensor.transpose(bank[4 + h % 2][:, b * P:(b + 1) * P], v[:, b * P:(b + 1) * P], ident)
                    last.then_inc(sem(name + ".v_turned"), 1)

                def mix(h):
                    pe.wait_ge(sem(name + ".probs"), 2 * h + 2)
                    if h >= 2:
                        pe.wait_ge(sem(name + ".p_copied"), h - 1)
                    for b in range(3):
                        last = nc.tensor.transpose(bank[2 + h % 2][:, b * P:(b + 1) * P],
                                                   prob[h % 2][:, b * P:(b + 1) * P], ident)
                    last.then_inc(sem(name + ".p_turned"), 1)
                    pe.wait_ge(sem(name + ".v_copied"), h + 1)
                    pe.wait_ge(sem(name + ".p_copied"), h + 1)
                    if h >= 2:
                        pe.wait_ge(sem(name + ".out"), h - 1)
                    o = bank[6 + h % 2]
                    mm(o[:, 0:256], vtok[h % 2][:, 0:128], probT[h % 2][:, 0:256], True, False)
                    mm(o[:, 128:256], vtok[h % 2][:, 128:256], probT[h % 2][:, 256:384], False, True)\
                        .then_inc(sem(name + ".mixed"), 1)

                scores(0)
                for h in range(N_HEADS):
                    if h + 1 < N_HEADS:
                        scores(h + 1)
                    mix(h)

            pe.wait_ge(sem("con_landed"), 32)
            attention("at1", 16, 24, 32, True)
            pe.wait_ge(sem("conv_operand"), 1)
            pe.wait_ge(sem("at1.out"), N_HEADS)
            with pe.Fori(0, 8) as i:
                pair_of_units(PAIR0["branch"] + i, H, NC, None, two_banks=True)
            with pe.Fori(0, 8) as i:
                pair_of_units(PAIR0["mix"] + i, U, NC, "merged")
            sum_squares("n2")

            def ff_group(g):
                pair = PAIR0["ff"] + 16 * g
                with pe.Fori(0, 8) as i:
                    pair_of_units(pair + i, H, NC, "h_ready", CHUNKS["h2"])
                ada_reduce(2 * g + 4)
                with pe.Fori(0, 8) as i:
                    pair_of_units(pair + 8 + i, U, NC, "ff.u_ready", 16 * g)
                ada_reduce(2 * g + 5)

            with pe.Fori(0, FF_GROUPS - 1) as g:
                ff_group(g)
            ff_group(FF_GROUPS - 1)
            pe.wait_ge(sem("hot_landed"), 16)
            pe.wait_ge(sem("con_landed"), 32)
            pe.wait_ge(sem("rel_ones"), 1)
            mm(bank[6][0:8, 0:REL_W], rel[:, :], relhot, True, True).then_inc(sem("rel_made"), 1)
            sum_squares("n3")
            for k in range(NC):
                pe.wait_ge(sem("n3.squared"), k + 1)
                last = mm(bank[7][:, 0:T], ones[:, :], zb(k), k == 0, k == NC - 1)
            last.then_inc(sem("norm.summed"), 1)
            with pe.Fori(0, 16) as i:
                pair_of_units(PAIR0["in2"] + i, H, NC, "h_ready", CHUNKS["h3"])
            pe.wait_ge(sem("wn_split"), 2)
            for b in range(2):
                for k in range(NC):
                    toks = slice(b * P, (b + 1) * P)
                    mm(bank[4][:, 64 * b:64 * b + 32], H[:, k, toks], wdt[:, k, :], b == 0 and k == 0, False)
                    last = mm(bank[4][:, 64 * b:64 * b + 16], H[:, k, T + b * P:T + (b + 1) * P], wdt[:, k, 0:16],
                              False, k == NC - 1)
            last.then_inc(sem("soft.logits"), 1)
            with pe.Fori(0, CONV_CH // 2) as i:
                pair_of_units(PAIR0["in2_conv"] + i, H, NC, None)
            attention("at2", 0, 8, 16, False)

            pe.wait_ge(sem("in2_conv.out"), CONV_CH)
            for grp in range(2):
                b_, c_ = zb(40 + grp), zb(42 + grp)
                mm(bank[grp][:, 0:256], b_[:, 0:128], c_, True, False)
                mm(bank[grp][:, 256:384], b_[:, 128:256], c_[:, 128:256], False, True).then_inc(sem("cb_ready"), 1)
            for n in range(4):
                b, q = n // 2, n % 2
                if n >= 2:
                    pe.wait_ge(sem("xdt_ready"), n - 1)
                for j in range(4):
                    last = nc.tensor.transpose(bank[2 + n % 2][:, j * P:(j + 1) * P],
                                               zb(32 + 4 * q + j)[:, b * P:(b + 1) * P], ident)
                last.then_inc(sem("xs_turned"), 1)

            def decays(h):
                pe.wait_ge(sem("ssm.decay_ready"), 2 * h + 2)
                if h >= 2:
                    pe.wait_ge(sem("ssm.exp"), h - 1)
                else:
                    pe.wait_ge(sem("cb_masked"), 2)
                s = bank[h % 2]
                mm(s[:, 0:256], GT, dec0[h % 2], True, False)
                mm(s[:, 128:256], ones[:, :], dec1[h % 2], False, False)
                mm(s[:, 256:384], GT, dec1[h % 2], False, True).then_inc(sem("ssm.decays"), 1)

            def outputs(h):
                j, rows = h // 2, 64 * (h % 2)
                pe.wait_ge(sem("ssm.weights"), h + 1)
                if h % 2 == 0 and j >= 2:
                    pe.wait_ge(sem("ssm.y"), j - 1)
                o = bank[6 + j % 2][rows:rows + 64, 0:256]
                o2 = bank[6 + j % 2][rows:rows + 64, 128:256]
                xd = flat(Z[:, 8:16, :])
                w = logit[h % 2]
                mm(o, xd[:, h * 64:(h + 1) * 64], w[:, 0:256], True, False)
                mm(o2, xd[:, 1024 + h * 64:1024 + (h + 1) * 64], w[:, 256:384], False, True).then_inc(sem("ssm.out"), 1)

            pe.wait_ge(sem("xdt_ready"), 4)
            decays(0)
            for h in range(SSM_HEADS):
                if h + 1 < SSM_HEADS:
                    decays(h + 1)
                outputs(h)
            for name in ("na", "ng0", "ng1"):
                sum_squares(name)
            with pe.Fori(0, 8) as i:
                pair_of_units(PAIR0["out2"] + i, H, NC, "h_ready", CHUNKS["h4"])
            sum_squares("n4")

            def ffn_group(g):
                pair = PAIR0["ffn"] + 19 * g
                with pe.Fori(0, FFN_BLOCKS) as i:
                    pair_of_units(pair + i, H, NC, "h_ready", CHUNKS["h5"])
                with pe.Fori(0, 8) as i:
                    pair_of_units(pair + FFN_BLOCKS + i, U, FFN_BLOCKS, "ffn.u_ready", FFN_BLOCKS * g)

            with pe.Fori(0, FFN_GROUPS - 1) as g:
                ffn_group(g)
            ffn_group(FFN_GROUPS - 1)
            sum_squares("n5")

        @block.scalar
        def _(act):
            A = nc.scalar.activation

            def cast_high(pair, par, h):
                slot = 2 * par + h
                act.wait_ge(sem("w_landed%d" % slot), 16 * pair + 16)
                act.wait_ge(sem("piece_used"), 4 * pair + slot + 1)
                A(w_hi[:, slot, :], w_raw[:, slot, :], ACT.Copy).then_inc(sem("w_high"), 1)

            def load_ada(chunk, slot):
                act.wait_ge(sem("ada_acc"), chunk)
                act.dma_start(ada_w[:, slot, :], t["w_ada"][bass.ds(chunk, 1)].rearrange("a p c -> (a p) c"))\
                    .then_inc(sem("ada_landed%d" % slot), 16)

            def take_half(pair, par, scale=1.0):
                act.wait_ge(sem("piece_used"), CREDIT + 4 * pair + 2 * par + 2)
                A(half[par], bank[par][:, T:2 * T], ACT.Copy, scale=scale).then_inc(sem("halves"), 1)

            def root(name, count=D, src=bank[4]):
                act.wait_ge(sem("norm.summed"), NTH[name])
                if NTH[name] > 1:
                    act.wait_ge(sem("norm.inverse"), NTH[name] - 1)
                A(std, src[:, 0:T], ACT.Sqrt, bias=epsb[:, :], scale=1.0 / count).then_inc(sem("norm.root"), 1)

            act.wait_ge(sem("vec_landed"), 16)
            for i in range(4):
                act.wait_ge(sem("x_landed%d" % i), 16)
                for k in range(4 * i, 4 * i + 4):
                    A(H[:, k, 0:T], X[:, k, :], ACT.Copy, scale=V("g_mix", k)).then_inc(sem("h_high"), 1)
                A(zb(4 * i, 4), xb(4 * i, 4), ACT.Square).then_inc(sem("x_squares"), 1)
                cast_high0(act, A, i)
            act.wait_ge(sem("ones_ready"), 1)
            root("n1")
            act.wait_ge(sem("n1.tok"), 1)
            A(small[:, 0:2], bank[6][:, 0:2], ACT.Sqrt, bias=epsb[:, :], scale=1.0 / D).then_inc(sem("n1.stdtok"), 1)
            A(small[:, 16:32], V("c", 0, 16), ACT.Sigmoid).then_inc(sem("c_sig"), 1)
            act.wait_ge(sem("wf_landed"), 16)
            A(wf[:, :, 0:8], wf_raw, ACT.Copy).then_inc(sem("wn_high"), 1)
            act.wait_ge(sem("ada_credit"), 1)
            load_ada(0, 0)
            load_ada(1, 1)

            def plain(pair, par, chunk=None, ahead=True):
                take_half(pair, par)
                cast_high(pair + 1, par, 0)
                cast_high(pair + 1, par, 1)
                if chunk is not None and ahead:
                    load_ada(chunk + 2, par)

            for g in range(2):
                with act.Fori(0, 8) as i:
                    for par in range(2):
                        plain(PAIR0["gate"] + 8 * g + i, par, ADA0["gate"] + 16 * g + 2 * i + par)
            act.wait_ge(sem("soft.logits"), 1)
            for b in range(2):
                A(small[:, 32 + 8 * b:40 + 8 * b], bank[4][:, 32 * b + 8:32 * b + 16], ACT.Copy).then_inc(sem("soft.half"), 1)
            act.wait_ge(sem("soft.nabs"), 1)
            A(small[:, 64:80], small[:, 80:96], ACT.Exp).then_inc(sem("soft.exp"), 1)
            act.wait_ge(sem("soft.exp"), 1)
            A(small[:, 96:112], small[:, 64:80], ACT.Ln, bias=1.0).then_inc(sem("soft.ln"), 1)
            act.wait_ge(sem("wdt_landed"), 16)
            A(wdt[:, :, 0:16], wdt_raw, ACT.Copy).then_inc(sem("wn_high"), 1)
            with act.Fori(0, 8) as i:
                for par in range(2):
                    plain(PAIR0["conv_in"] + i, par, ADA0["conv_in"] + 2 * i + par)
            with act.Fori(0, 4) as i:
                for par in range(2):
                    plain(PAIR0["conv_mul"] + i, par)
            with act.Fori(0, 7) as i:
                for par in range(2):
                    plain(PAIR0["qk"] + i, par, ADA0["qk"] + 2 * i + par)
            for par in range(2):
                plain(PAIR0["qk"] + 7, par, ADA0["qk"] + 14 + par, ahead=False)
            with act.Fori(0, 4) as i:
                for par in range(2):
                    plain(PAIR0["v"] + i, par)

            def attention(name, q0, out_high):
                def early(h):
                    if h >= 2:
                        act.wait_ge(sem(name + ".scores"), h - 1)
                    A(qs[h % 2], zb(q0 + h), ACT.Copy, scale=HEAD_SCALE).then_inc(sem(name + ".q_scaled"), 1)
                    act.wait_ge(sem(name + ".v_turned"), h + 1)
                    if h >= 2:
                        act.wait_ge(sem(name + ".mixed"), h - 1)
                    A(vtok[h % 2], bank[4 + h % 2][:, 0:256], ACT.Copy).then_inc(sem(name + ".v_copied"), 1)

                def exps(h):
                    act.wait_ge(sem(name + ".maxes"), 2 * h + 2)
                    if h >= 2:
                        act.wait_ge(sem(name + ".p_turned"), h - 1)
                    for b, (lo, up) in enumerate(((0, 128), (128, 384))):
                        c = 128 + 2 * h + b
                        A(prob[h % 2][:, lo:up], bank[h % 2][:, lo:up], ACT.Exp, bias=small[:, c:c + 1],
                          accum_out=small[:, c + 16:c + 17]).then_inc(sem(name + ".exps"), 1)

                def late(h):
                    act.wait_ge(sem(name + ".p_turned"), h + 1)
                    A(probT[h % 2], bank[2 + h % 2][:, 0:384], ACT.Copy).then_inc(sem(name + ".p_copied"), 1)
                    if out_high:
                        act.wait_ge(sem(name + ".mixed"), h + 1)
                        A(H[:, 8 + h, 0:T], bank[6 + h % 2][:, 0:256], ACT.Copy).then_inc(sem(name + ".high"), 1)

                early(0)
                for h in range(N_HEADS):
                    if h + 1 < N_HEADS:
                        early(h + 1)
                    exps(h)
                    late(h)

            act.wait_ge(sem("qk.out"), 16)
            act.wait_ge(sem("v.out"), 8)
            attention("at1", 16, True)
            act.wait_ge(sem("conv_mul.out"), 8)
            A(H[:, 0:8, 0:T], Z[:, 8:16, :], ACT.Copy).then_inc(sem("conv_high"), 1)

            with act.Fori(0, 8) as i:
                for par in range(2):
                    pair, m = PAIR0["branch"] + i, 2 * i + par
                    act.wait_ge(sem("branch.gated"), 2 * m)
                    A(sig[par], flat(G[:, bass.ds(m, 1), 0, :]), ACT.Sigmoid, bias=V("b_gate", m)).then_inc(sem("gates_open"), 1)
                    A(wide[par], flat(G[:, bass.ds(m, 1), 1, :]), ACT.Sigmoid, bias=V("b_gate", 16 + m)).then_inc(sem("gates_open"), 1)
                    act.wait_ge(sem("piece_used"), CREDIT + 4 * pair + 2 * par + 2)
                    A(half[par], bank[par][:, T:2 * T], ACT.Copy).then_inc(sem("halves_b"), 1)
                    A(half2[par], bank[2 + par][:, T:2 * T], ACT.Copy).then_inc(sem("halves_b"), 1)
                    cast_high(pair + 1, par, 0)
                    cast_high(pair + 1, par, 1)
                    act.wait_ge(sem("merge"), m + 1)
                    act.sem_inc(sem("merge_seen"), 1)
                    A(ob(U, m, 0), conv[par], ACT.Copy).then_inc(sem("merged_high"), 1)
            with act.Fori(0, 8) as i:
                for par in range(2):
                    pair, m = PAIR0["mix"] + i, 2 * i + par
                    take_half(pair, par)
                    cast_high(pair + 1, par, 0)
                    act.wait_ge(sem("mix.x"), m + 1)
                    A(ob(H, m, 0), xb(m), ACT.Copy, scale=V("g_mlp", m)).then_inc(sem("h_high"), 1)
                    A(wide[par], xb(m), ACT.Square).then_inc(sem("mix.squared"), 1)
                    cast_high(pair + 1, par, 1)
            root("n2")
            load_ada(ADA0["ff"], 0)
            load_ada(ADA0["ff"] + 1, 1)

            def ff1_unit(pair, par, m, u, chunk):
                take_half(pair, par)
                cast_high(pair + 1, par, 0)
                act.wait_ge(sem("ff.relu"), m + 1)
                A(ob(U, u, 0), wide[par], ACT.Square).then_inc(sem("u_high"), 1)
                A(conv[par], wide[par], ACT.Square).then_inc(sem("ff.u_full"), 1)
                cast_high(pair + 1, par, 1)
                load_ada(chunk + 2, par)

            def ff2_unit(pair, par, m, block, chunk, squares=False):
                take_half(pair, par)
                cast_high(pair + 1, par, 0)
                if squares:
                    act.wait_ge(sem("ff.x"), m + 1)
                    A(wide[par], xb(block), ACT.Square).then_inc(sem("ff.squared"), 1)
                cast_high(pair + 1, par, 1)
                if chunk is not None:
                    load_ada(chunk + 2, par)

            def ff_group(g, final):
                pair = PAIR0["ff"] + 16 * g
                with act.Fori(0, 8) as i:
                    for par in range(2):
                        ff1_unit(pair + i, par, 16 * g + 2 * i + par, 2 * i + par, ADA0["ff"] + 32 * g + 2 * i + par)
                with act.Fori(0, 7 if final else 8) as i:
                    for par in range(2):
                        ff2_unit(pair + 8 + i, par, 16 * g + 2 * i + par, 2 * i + par, ADA0["ff"] + 32 * g + 16 + 2 * i + par, final)
                if final:
                    for par in range(2):
                        ff2_unit(pair + 15, par, 16 * g + 14 + par, 14 + par, None, True)

            with act.Fori(0, FF_GROUPS - 1) as g:
                ff_group(g, False)
            ff_group(FF_GROUPS - 1, True)
            root("n3")
            for k in range(NC):
                act.wait_ge(sem("n3.x"), k + 1)
                A(zb(k), xb(k), ACT.Square).then_inc(sem("n3.squared"), 1)
            root("n3b", src=bank[7])
            for k in range(NC):
                act.wait_ge(sem("normed"), k + 1)
                A(H[:, k, 0:T], work(4 + k % 4), ACT.Identity, bias=mod[:, k:k + 1]).then_inc(sem("h_high"), 1)
            with act.Fori(0, 16) as i:
                for par in range(2):
                    plain(PAIR0["in2"] + i, par)
            act.wait_ge(sem("soft.logits"), 2)
            for b in range(2):
                A(small[:, 192 + 16 * b:208 + 16 * b], bank[4][:, 64 * b + 16:64 * b + 32], ACT.Copy).then_inc(sem("soft.half"), 1)
            A(small[:, 480:496], V("a_log", 0, 16), ACT.Exp).then_inc(sem("a_exp"), 1)
            act.wait_ge(sem("soft.nabs"), 2)
            A(small[:, 224:256], small[:, 256:288], ACT.Exp).then_inc(sem("soft.exp"), 1)
            act.wait_ge(sem("soft.exp"), 2)
            A(small[:, 288:320], small[:, 224:256], ACT.Ln, bias=1.0).then_inc(sem("soft.ln"), 1)
            with act.Fori(0, CONV_CH // 2) as i:
                for par in range(2):
                    pair, m = PAIR0["in2_conv"] + i, 2 * i + par
                    take_half(pair, par)
                    cast_high(pair + 1, par, 0)
                    cast_high(pair + 1, par, 1)
                    act.wait_ge(sem("in2_conv.conv"), m + 1)
                    A(sig[par], conv[par], ACT.Sigmoid).then_inc(sem("in2_conv.sig"), 1)
            act.wait_ge(sem("in2.out"), 32)
            attention("at2", 0, False)
            for h in range(SSM_HEADS):
                act.wait_ge(sem("ssm.decays"), h + 1)
                if h >= 2:
                    act.wait_ge(sem("ssm.weights"), h - 1)
                A(prob[h % 2], bank[h % 2][:, 0:384], ACT.Exp).then_inc(sem("ssm.exp"), 1)
            act.wait_ge(sem("ssm.out"), SSM_HEADS)
            A(adaf, zb(24, 8), ACT.Sigmoid).then_inc(sem("z_sig"), 1)
            act.wait_ge(sem("at2.out"), N_HEADS)
            A(zb(8, 8), zb(0, 8), ACT.Square).then_inc(sem("at2.squared"), 1)
            root("na", 1024)
            act.wait_ge(sem("ssm.gated"), 1)
            A(zb(16, 8), zb(32, 8), ACT.Square).then_inc(sem("ssm.squared"), 1)
            for k in range(8):
                act.wait_ge(sem("normed"), NC + k + 1)
                A(H[:, k, 0:T], work(4 + k % 4), ACT.Copy).then_inc(sem("h_high"), 1)
            for grp in range(2):
                root("ng%d" % grp, 512)
                for k in range(8 + 4 * grp, 12 + 4 * grp):
                    act.wait_ge(sem("normed"), NC + k + 1)
                    A(H[:, k, 0:T], work(4 + k % 4), ACT.Copy).then_inc(sem("h_high"), 1)

            def gated_unit(name, pair, par, m, block, gate, squares, ahead=True):
                take_half(pair, par, scale=mod[:, bass.ds(gate + block, 1)])
                if ahead:
                    cast_high(pair + 1, par, 0)
                if squares:
                    act.wait_ge(sem(name + ".x"), m + 1)
                    A(wide[par], xb(block), ACT.Square).then_inc(sem(name + ".squared"), 1)
                if ahead:
                    cast_high(pair + 1, par, 1)

            with act.Fori(0, 8) as i:
                for par in range(2):
                    gated_unit("out2", PAIR0["out2"] + i, par, 2 * i + par, 2 * i + par, 32, True)
            root("n4")
            for k in range(NC):
                act.wait_ge(sem("normed"), 2 * NC + k + 1)
                A(H[:, k, 0:T], work(4 + k % 4), ACT.Identity, bias=mod[:, 48 + k:49 + k]).then_inc(sem("h_high"), 1)

            def ffn_group(g, final):
                pair = PAIR0["ffn"] + 19 * g
                with act.Fori(0, FFN_BLOCKS) as i:
                    take_half(pair + i, 0)
                    cast_high(pair + i + 1, 0, 0)
                    cast_high(pair + i + 1, 0, 1)
                    act.wait_ge(sem("up.conv"), 2 * FFN_BLOCKS * g + 2 * i + 1)
                    A(sig[0], conv[0], ACT.Sigmoid).then_inc(sem("up.sig"), 1)
                    take_half(pair + i, 1)
                    cast_high(pair + i + 1, 1, 0)
                    act.wait_ge(sem("up.act"), FFN_BLOCKS * g + i + 1)
                    A(ob(U, i, 0), wide[0], ACT.Copy).then_inc(sem("u_high"), 1)
                    cast_high(pair + i + 1, 1, 1)
                pair = pair + FFN_BLOCKS
                with act.Fori(0, 7 if final else 8) as i:
                    for par in range(2):
                        gated_unit("down", pair + i, par, 16 * g + 2 * i + par, 2 * i + par, 80, final)
                if final:
                    for par in range(2):
                        gated_unit("down", pair + 7, par, 16 * g + 14 + par, 14 + par, 80, True, ahead=False)

            with act.Fori(0, FFN_GROUPS - 1) as g:
                ffn_group(g, False)
            ffn_group(FFN_GROUPS - 1, True)
            root("n5")

        @block.vector
        def _(dve):
            v = nc.vector
            TT, STT, TS = v.tensor_tensor, v.scalar_tensor_tensor, v.tensor_scalar

            links = [0]

            def link(ins):
                links[0] += 1
                ins.then_inc(sem("dve_link"), 1)
                dve.wait_ge(sem("dve_link"), links[0])

            def split_low(pair, par, h):
                slot = 2 * par + h
                dve.wait_ge(sem("w_high"), 4 * pair + slot + 1)
                TT(w_lo[:, slot, :], w_raw[:, slot, :], w_hi[:, slot, :].bitcast(F32), ALU.subtract)\
                    .then_inc(sem("w_split"), 1)

            def add_halves(pair, par, out):
                dve.wait_ge(sem("halves"), units_with_half(pair, par))
                TT(out, bank[par][:, 0:T], half[par], ALU.add).then_inc(sem("bank_read"), 1)
                return 2 + 2 * pair + par + 1

            def units_with_half(pair, par):
                skipped = 16 if after_branch[0] else 0
                return 2 * pair + par + 1 - skipped

            after_branch = [False]

            def add_ada(chunk, k, par):
                dve.wait_ge(sem("ada_landed%d" % par), turn_value(chunk, par))
                dve.wait_ge(sem("ada_acc"), chunk + 1)
                STT(ada_acc[:, :], ada_w[:, par, :], silu_c[:, bass.ds(k, 1)], ada_acc[:, :], ALU.mult, ALU.add)\
                    .then_inc(sem("ada_acc"), 1)

            def turn_value(chunk, par):
                return chunk * 8 + (16 - 8 * par)

            def take_mod(group):
                dve.wait_ge(sem("ada_reduced"), group + 1)
                v.memset(ada_acc[:, :], 0.0).then_inc(sem("ada_zeroed"), 1)
                dve.wait_ge(sem("ada_zeroed"), group + 2)
                n = ADA_COLS // P
                TT(mod[:, bass.ds(group * n, n)], bank[5][:, 0:n], V("b_ada", group * n, n), ALU.add)\
                    .then_inc(sem("mod_ready"), 1)

            def inverse(name):
                dve.wait_ge(sem("norm.root"), NTH[name])
                v.reciprocal(R[:, :], std).then_inc(sem("norm.inverse"), 1)
                dve.wait_ge(sem("norm.inverse"), NTH[name])

            v.memset(epsb[:, :], EPS)
            v.memset(ada_acc[:, :], 0.0).then_inc(sem("ada_zeroed"), 1)
            v.memset(rel[REL_BUCKETS:REL_BUCKETS + 1, :], 1.0).then_inc(sem("rel_ones"), 1)
            v.memset(ones[:, :], 1.0).then_inc(sem("ones_ready"), 1)
            dve.sem_inc(sem("w_split"), CREDIT)
            dve.sem_inc(sem("piece_used"), CREDIT)
            dve.sem_inc(sem("bank_read"), 2)
            dve.sem_inc(sem("ada_acc"), 1)
            dve.sem_inc(sem("ada_credit"), 1)
            dve.wait_ge(sem("vec_landed"), 16)
            for i in range(4):
                for k in range(4 * i, 4 * i + 4):
                    dve.wait_ge(sem("h_high"), k + 1)
                    STT(H[:, k, T:2 * T], X[:, k, :], V("g_mix", k), H[:, k, 0:T].bitcast(F32), ALU.mult, ALU.subtract)\
                        .then_inc(sem("h_ready"), 1)
                dve.wait_ge(sem("w_high"), i + 1)
                TT(w_lo[:, i, :], w_raw[:, i, :], w_hi[:, i, :].bitcast(F32), ALU.subtract).then_inc(sem("w_split"), 1)
            dve.wait_ge(sem("x_squares"), 4)
            v.tensor_reduce(ss[:, :], Z[:, 0:NC, :].rearrange("p c t -> p t c"), AX_X, ALU.add)\
                .then_inc(sem("norm.squares"), 1)
            inverse("n1")
            dve.wait_ge(sem("n1.stdtok"), 1)
            link(v.reciprocal(small[:, 2:4], small[:, 0:2]))
            dve.wait_ge(sem("c_sig"), 1)
            link(TT(silu_c[:, :], V("c", 0, 16), small[:, 16:32], ALU.mult))
            dve.wait_ge(sem("wn_high"), 1)
            TT(wf[:, :, 8:16], wf_raw, wf[:, :, 0:8].bitcast(F32), ALU.subtract).then_inc(sem("wn_split"), 1)

            def plain_normed(name, pair, par, out, count, chunk=None, k=None):
                if chunk is not None:
                    add_ada(chunk, k, par)
                n = add_halves(pair, par, total[par])
                split_low(pair + 1, par, 0)
                dve.wait_ge(sem("bank_read"), n)
                TT(out, total[par], R[:, :], ALU.mult).then_inc(sem(name + ".out"), 1)
                split_low(pair + 1, par, 1)

            dve.wait_ge(sem("ada_zeroed"), 1)
            for g in range(2):
                with dve.Fori(0, 8) as i:
                    for par in range(2):
                        m = 16 * g + 2 * i + par
                        plain_normed("gate", PAIR0["gate"] + 8 * g + i, par,
                                     flat(G[:, bass.ds(8 * g + i, 1), par, :]), m, m, 2 * i + par)
                take_mod(g)
            dve.wait_ge(sem("soft.half"), 2)
            y, nabs, l = small[:, 48:64], small[:, 80:96], small[:, 96:112]
            logf = small[:, 112:128]
            for b in range(2):
                s = slice(8 * b, 8 * b + 8)
                link(TT(y[:, s], bank[4][:, 32 * b:32 * b + 8], small[:, 32 + 8 * b:40 + 8 * b], ALU.add))
                link(STT(y[:, s], y[:, s], small[:, 2 + b:3 + b], V("b_f", 0, 8), ALU.mult, ALU.add))
            STT(nabs, y, -1.0, y, ALU.mult, ALU.min).then_inc(sem("soft.nabs"), 1)
            dve.wait_ge(sem("soft.ln"), 1)
            link(STT(logf, y, 0.0, l, ALU.min, ALU.subtract))
            dve.wait_ge(sem("wn_high"), 2)
            TT(wdt[:, :, 16:32], wdt_raw, wdt[:, :, 0:16].bitcast(F32), ALU.subtract).then_inc(sem("wn_split"), 1)
            with dve.Fori(0, 8) as i:
                for par in range(2):
                    m = 2 * i + par
                    plain_normed("conv_in", PAIR0["conv_in"] + i, par, zb(m), m, ADA0["conv_in"] + m, m)
            take_mod(2)
            with dve.Fori(0, 4) as i:
                for par in range(2):
                    pair, m = PAIR0["conv_mul"] + i, 2 * i + par
                    n = add_halves(pair, par, total[par])
                    split_low(pair + 1, par, 0)
                    dve.wait_ge(sem("bank_read"), n)
                    TT(wide[par], total[par], R[:, :], ALU.mult).then_inc(sem("conv_mul.u"), 1)
                    dve.wait_ge(sem("conv_mul.u"), 2 * m + 1)
                    TT(total[par], wide[par], zb(8 + m), ALU.mult).then_inc(sem("conv_mul.u"), 1)
                    dve.wait_ge(sem("conv_mul.u"), 2 * m + 2)
                    u = total[par]
                    TS(conv[par], u, V("conv_w", 16 + m), None, ALU.mult).then_inc(sem("tap"), 1)
                    dve.wait_ge(sem("tap"), 3 * m + 1)
                    STT(conv[par][:, 1:T], u[:, 0:T - 1], V("conv_w", 8 + m), conv[par][:, 1:T], ALU.mult, ALU.add)\
                        .then_inc(sem("tap"), 1)
                    dve.wait_ge(sem("tap"), 3 * m + 2)
                    STT(conv[par][:, 2:T], u[:, 0:T - 2], V("conv_w", m), conv[par][:, 2:T], ALU.mult, ALU.add)\
                        .then_inc(sem("tap"), 1)
                    dve.wait_ge(sem("tap"), 3 * m + 3)
                    TT(zb(8 + m), conv[par], zb(m), ALU.mult).then_inc(sem("conv_mul.out"), 1)
                    split_low(pair + 1, par, 1)
            with dve.Fori(0, 8) as i:
                for par in range(2):
                    m = 2 * i + par
                    plain_normed("qk", PAIR0["qk"] + i, par, zb(16 + m), m, ADA0["qk"] + m, m)
            take_mod(3)
            with dve.Fori(0, 4) as i:
                for par in range(2):
                    m = 2 * i + par
                    plain_normed("v", PAIR0["v"] + i, par, zb(32 + m), m)

            def decay_operands(name, h, a0, a1):
                TS(dec0[h % 2], LEO, a0, None, ALU.mult).then_inc(sem(name + ".decay_ready"), 1)
                TS(dec1[h % 2], LE, a1, None, ALU.mult).then_inc(sem(name + ".decay_ready"), 1)

            def attention(name, decay):
                def softmax_in(h):
                    dve.wait_ge(sem(name + ".scores"), h + 1)
                    for b, (lo, up) in enumerate(((0, 128), (128, 384))):
                        c = 128 + 2 * h + b
                        v.tensor_reduce(small[:, c:c + 1], bank[h % 2][:, lo:up], AX_X, ALU.max, negate=True)\
                            .then_inc(sem(name + ".maxes"), 1)
                    if decay and h + 2 < N_HEADS:
                        decay_operands(name, h + 2, logf[:, h + 2:h + 3], logf[:, 8 + h + 2:9 + h + 2])

                def normalise(h):
                    dve.wait_ge(sem(name + ".exps"), 2 * h + 2)
                    c = 144 + 2 * h
                    link(v.reciprocal(small[:, c + 16:c + 18], small[:, c:c + 2]))
                    for b, (lo, up) in enumerate(((0, 128), (128, 384))):
                        TS(prob[h % 2][:, lo:up], prob[h % 2][:, lo:up], small[:, c + 16 + b:c + 17 + b], None, ALU.mult)\
                            .then_inc(sem(name + ".probs"), 1)

                def finish(h):
                    if decay:
                        dve.wait_ge(sem(name + ".high"), h + 1)
                        TT(H[:, 8 + h, T:2 * T], bank[6 + h % 2][:, 0:256], H[:, 8 + h, 0:T].bitcast(F32), ALU.subtract)\
                            .then_inc(sem(name + ".out"), 1)
                    else:
                        dve.wait_ge(sem(name + ".mixed"), h + 1)
                        v.tensor_copy(zb(h), bank[6 + h % 2][:, 0:256]).then_inc(sem(name + ".out"), 1)

                if decay:
                    for h in range(2):
                        decay_operands(name, h, logf[:, h:h + 1], logf[:, 8 + h:9 + h])
                softmax_in(0)
                for h in range(N_HEADS):
                    if h + 1 < N_HEADS:
                        softmax_in(h + 1)
                    normalise(h)
                    if h:
                        finish(h - 1)
                finish(N_HEADS - 1)

            dve.wait_ge(sem("con_landed"), 32)
            attention("at1", True)
            dve.wait_ge(sem("conv_high"), 1)
            TT(H[:, 0:8, T:2 * T], Z[:, 8:16, :], H[:, 0:8, 0:T].bitcast(F32), ALU.subtract).then_inc(sem("conv_operand"), 1)
            dve.sem_inc(sem("branch.gated"), 2)
            with dve.Fori(0, 8) as i:
                for par in range(2):
                    pair, m = PAIR0["branch"] + i, 2 * i + par
                    dve.wait_ge(sem("halves_b"), 2 * m + 2)
                    TT(total[par], bank[par][:, 0:T], half[par], ALU.add).then_inc(sem("branch.sum"), 1)
                    TT(conv[par], bank[2 + par][:, 0:T], half2[par], ALU.add).then_inc(sem("bank_read"), 1)
                    split_low(pair + 1, par, 0)
                    dve.wait_ge(sem("gates_open"), 2 * m + 2)
                    dve.wait_ge(sem("branch.sum"), m + 1)
                    dve.wait_ge(sem("bank_read"), 2 + 2 * pair + par + 1)
                    TT(total[par], total[par], sig[par], ALU.mult).then_inc(sem("branch.gated"), 1)
                    TT(conv[par], conv[par], wide[par], ALU.mult).then_inc(sem("branch.gated"), 1)
                    dve.wait_ge(sem("branch.gated"), 2 + 2 * m + 2)
                    TT(conv[par], total[par], conv[par], ALU.add).then_inc(sem("merge"), 1)
                    split_low(pair + 1, par, 1)
                    dve.wait_ge(sem("merged_high"), m + 1)
                    TT(ob(U, m, 1), conv[par], ob(U, m, 0).bitcast(F32), ALU.subtract).then_inc(sem("merged"), 1)
            after_branch[0] = True

            def clear_ss(name):
                v.memset(ss[:, :], 0.0).then_inc(sem(name + ".cleared"), 1)
                dve.wait_ge(sem(name + ".cleared"), 1)

            def add_square(name, m, local):
                dve.wait_ge(sem(name + ".squared"), local + 1)
                dve.wait_ge(sem(name + ".ss"), local)
                TT(ss[:, :], ss[:, :], wide_of(m), ALU.add).then_inc(sem(name + ".ss"), 1)

            def wide_of(par):
                return wide[par]

            def signal_squares(name, source):
                dve.wait_ge(sem(source + ".ss"), NC)
                dve.sem_inc(sem("norm.squares"), 1)

            clear_ss("mix")
            with dve.Fori(0, 8) as i:
                for par in range(2):
                    pair, m = PAIR0["mix"] + i, 2 * i + par
                    n = add_halves(pair, par, total[par])
                    split_low(pair + 1, par, 0)
                    dve.wait_ge(sem("bank_read"), n)
                    TT(xb(m), xb(m), total[par], ALU.add).then_inc(sem("mix.x"), 1)
                    split_low(pair + 1, par, 1)
                    dve.wait_ge(sem("h_high"), CHUNKS["h2"] + m + 1)
                    dve.wait_ge(sem("mix.x"), m + 1)
                    STT(ob(H, m, 1), xb(m), V("g_mlp", m), ob(H, m, 0).bitcast(F32), ALU.mult, ALU.subtract)\
                        .then_inc(sem("h_ready"), 1)
                    add_square("mix", par, m)
            signal_squares("n2", "mix")
            inverse("n2")

            def ff_group(g, final):
                pair = PAIR0["ff"] + 16 * g
                with dve.Fori(0, 8) as i:
                    for par in range(2):
                        u = 2 * i + par
                        m = 16 * g + u
                        add_ada(ADA0["ff"] + 32 * g + u, u, par)
                        n = add_halves(pair + i, par, total[par])
                        dve.wait_ge(sem("bank_read"), n)
                        STT(wide[par], total[par], 0.0, R[:, :], ALU.max, ALU.mult).then_inc(sem("ff.relu"), 1)
                        split_low(pair + i + 1, par, 0)
                        dve.wait_ge(sem("ff.u_full"), m + 1)
                        TT(ob(U, u, 1), conv[par], ob(U, u, 0).bitcast(F32), ALU.subtract).then_inc(sem("ff.u_ready"), 1)
                        split_low(pair + i + 1, par, 1)
                take_mod(2 * g + 4)
                if final:
                    clear_ss("ff")
                with dve.Fori(0, 8) as i:
                    for par in range(2):
                        u = 2 * i + par
                        m = 16 * g + u
                        add_ada(ADA0["ff"] + 32 * g + 16 + u, u, par)
                        n = add_halves(pair + 8 + i, par, total[par])
                        split_low(pair + 8 + i + 1, par, 0)
                        dve.wait_ge(sem("bank_read"), n)
                        TT(xb(u), xb(u), total[par], ALU.add).then_inc(sem("ff.x"), 1)
                        split_low(pair + 8 + i + 1, par, 1)
                        if final:
                            add_square("ff", par, u)
                take_mod(2 * g + 5)

            with dve.Fori(0, FF_GROUPS - 1) as g:
                ff_group(g, False)
            ff_group(FF_GROUPS - 1, True)
            signal_squares("n3", "ff")
            dve.wait_ge(sem("rel_made"), 1)
            v.tensor_copy(relrow[:, :], bank[6][0:8, 0:REL_W]).then_inc(sem("relrow_ready"), 1)
            dve.wait_ge(sem("mod_ready"), ADA_GROUPS)
            link(STT(g1[:, :], mod[:, 16:32], 1.0, V("g_mix2", 0, 16), ALU.add, ALU.mult))
            link(STT(g2[:, :], mod[:, 64:80], 1.0, V("g_ffn", 0, 16), ALU.add, ALU.mult))
            dve.wait_ge(sem("ff.x"), FF_GROUPS * NC)

            def modulated(name, gain, shift, chunks, normed):
                inverse(name)
                for k in range(NC + 1):
                    if k < NC:
                        if k >= 4:
                            dve.wait_ge(sem("h_ready"), chunks + k - 3)
                        STT(work(4 + k % 4), xb(k), gain[:, k:k + 1], R[:, :], ALU.mult, ALU.mult)\
                            .then_inc(sem("normed"), 1)
                    if k:
                        j = k - 1
                        dve.wait_ge(sem("h_high"), chunks + j + 1)
                        dve.wait_ge(sem("normed"), normed + j + 1)
                        STT(H[:, j, T:2 * T], work(4 + j % 4), mod[:, shift + j:shift + j + 1], H[:, j, 0:T].bitcast(F32),
                            ALU.add, ALU.subtract).then_inc(sem("h_ready"), 1)

            inverse("n3")
            for k in range(NC):
                STT(xb(k), xb(k), V("g_final", k), R[:, :], ALU.mult, ALU.mult).then_inc(sem("n3.x"), 1)
            dve.wait_ge(sem("n3.x"), NC)
            dve.sem_inc(sem("norm.squares"), 1)
            modulated("n3b", g1, 0, CHUNKS["h3"], 0)
            with dve.Fori(0, 16) as i:
                for par in range(2):
                    pair = PAIR0["in2"] + i
                    dve.wait_ge(sem("halves"), units_with_half(pair, par))
                    TT(zb(2 * i + par), bank[par][:, 0:T], half[par], ALU.add).then_inc(sem("bank_read"), 1)
                    split_low(pair + 1, par, 0)
                    split_low(pair + 1, par, 1)
            dve.wait_ge(sem("bank_read"), 2 + 2 * PAIR0["in2_conv"])
            dve.sem_inc(sem("in2.out"), 32)
            dve.wait_ge(sem("soft.half"), 4)
            y, nabs, l = small[:, 320:352], small[:, 256:288], small[:, 288:320]
            dt, dta = small[:, 352:384], small[:, 384:416]
            for b in range(2):
                s = slice(16 * b, 16 * b + 16)
                link(TT(y[:, s], bank[4][:, 64 * b:64 * b + 16], small[:, 192 + 16 * b:208 + 16 * b], ALU.add))
                link(TT(y[:, s], y[:, s], V("dt_bias", 0, 16), ALU.add))
            STT(nabs, y, -1.0, y, ALU.mult, ALU.min).then_inc(sem("soft.nabs"), 1)
            dve.wait_ge(sem("soft.ln"), 2)
            link(STT(dt, y, 0.0, l, ALU.max, ALU.add))
            dve.wait_ge(sem("a_exp"), 1)
            for b in range(2):
                s = slice(16 * b, 16 * b + 16)
                link(STT(dta[:, s], dt[:, s], -1.0, small[:, 480:496], ALU.mult, ALU.mult))
            dve.wait_ge(sem("relrow_stored"), 16)
            with dve.Fori(0, CONV_CH // 2) as i:
                for par in range(2):
                    pair, m = PAIR0["in2_conv"] + i, 2 * i + par
                    n = add_halves(pair, par, total[par])
                    split_low(pair + 1, par, 0)
                    dve.wait_ge(sem("bank_read"), n)
                    u = total[par]
                    TS(conv[par], u, V("ssm_w", 36 + m), V("ssm_b", m), ALU.mult, ALU.add).then_inc(sem("tap"), 1)
                    for d in range(1, 4):
                        dve.wait_ge(sem("tap"), TAPS["in2_conv"] + 3 * m + d)
                        step = STT(conv[par][:, d:T], u[:, 0:T - d], V("ssm_w", 36 - 12 * d + m), conv[par][:, d:T],
                                   ALU.mult, ALU.add)
                        step.then_inc(sem("tap" if d < 3 else "in2_conv.conv"), 1)
                    split_low(pair + 1, par, 1)
                    dve.wait_ge(sem("in2_conv.sig"), m + 1)
                    dve.wait_ge(sem("in2_conv.conv"), m + 1)
                    TT(zb(32 + m), conv[par], sig[par], ALU.mult).then_inc(sem("in2_conv.out"), 1)
            attention("at2", False)

            dve.wait_ge(sem("cb_ready"), 2)
            cbm = [Z[:, 16:20, :].rearrange("p a t -> p (a t)")[:, 384 * g_:384 * g_ + 384] for g_ in range(2)]
            for grp in range(2):
                TT(cbm[grp], bank[grp][:, 0:384], LEOL, ALU.mult).then_inc(sem("cb_masked"), 1)
            xd = flat(Z[:, 8:16, :])
            for n in range(4):
                b, q = n // 2, n % 2
                dve.wait_ge(sem("xs_turned"), n + 1)
                out = xd[:, 1024 * b + 512 * q:1024 * b + 512 * q + 512].rearrange("p (h d) -> p h d", d=64)
                src = bank[2 + n % 2][:, :].rearrange("p (h d) -> p h d", d=64)
                d_ = dt[:, 16 * b + 8 * q:16 * b + 8 * q + 8]
                TT(out, src, d_.unsqueeze(2).to_broadcast([P, 8, 64]), ALU.mult).then_inc(sem("xdt_ready"), 1)

            def ssm_decay(h):
                decay_operands("ssm", h, dta[:, h:h + 1], dta[:, 16 + h:17 + h])

            ssm_decay(0)
            ssm_decay(1)
            dve.wait_ge(sem("cb_masked"), 2)
            for h in range(SSM_HEADS):
                dve.wait_ge(sem("ssm.exp"), h + 1)
                if h >= 2:
                    dve.wait_ge(sem("ssm.out"), h - 1)
                TT(logit[h % 2], prob[h % 2], cbm[h // 8], ALU.mult).then_inc(sem("ssm.weights"), 1)
                if h + 2 < SSM_HEADS:
                    ssm_decay(h + 2)
                if h % 2 == 0 and h:
                    ssm_y(dve, STT, h // 2 - 1)
            ssm_y(dve, STT, SSM_HEADS // 2 - 1)
            dve.wait_ge(sem("z_sig"), 1)
            link(TT(zb(24, 8), zb(24, 8), adaf, ALU.mult))
            dve.wait_ge(sem("ssm.y"), 8)
            TT(zb(32, 8), zb(32, 8), zb(24, 8), ALU.mult).then_inc(sem("ssm.gated"), 1)

            def block_norm(name, first, n, src, gain, k0, squares):
                v.tensor_reduce(ss[:, :], Z[:, squares:squares + n, :].rearrange("p c t -> p t c"), AX_X, ALU.add)\
                    .then_inc(sem("norm.squares"), 1)
                inverse(name)
                for k in range(k0, k0 + n + 1):
                    if k < k0 + n:
                        if k >= 4:
                            dve.wait_ge(sem("h_ready"), CHUNKS["h4"] + k - 3)
                        STT(work(4 + k % 4), zb(src + k - k0), V(gain, first + k - k0), R[:, :], ALU.mult, ALU.mult)\
                            .then_inc(sem("normed"), 1)
                    if k > k0:
                        j = k - 1
                        dve.wait_ge(sem("h_high"), CHUNKS["h4"] + j + 1)
                        dve.wait_ge(sem("normed"), NC + j + 1)
                        TT(H[:, j, T:2 * T], work(4 + j % 4), H[:, j, 0:T].bitcast(F32), ALU.subtract)\
                            .then_inc(sem("h_ready"), 1)

            dve.wait_ge(sem("at2.squared"), 1)
            block_norm("na", 0, 8, 0, "g_attn", 0, 8)
            dve.wait_ge(sem("ssm.squared"), 1)
            block_norm("ng0", 0, 4, 32, "g_ssm", 8, 16)
            block_norm("ng1", 4, 4, 36, "g_ssm", 12, 20)

            def gated(name, pair, par, m, block, gate, squares, ahead=True):
                dve.wait_ge(sem("halves"), units_with_half(pair, par))
                STT(total[par], bank[par][:, 0:T], mod[:, bass.ds(gate + block, 1)], half[par], ALU.mult, ALU.add)\
                    .then_inc(sem("bank_read"), 1)
                if ahead:
                    split_low(pair + 1, par, 0)
                dve.wait_ge(sem("bank_read"), 2 + 2 * pair + par + 1)
                TT(xb(block), xb(block), total[par], ALU.add).then_inc(sem(name + ".x"), 1)
                if ahead:
                    split_low(pair + 1, par, 1)
                if squares:
                    add_square(name, par, block)

            clear_ss("out2")
            with dve.Fori(0, 8) as i:
                for par in range(2):
                    gated("out2", PAIR0["out2"] + i, par, 2 * i + par, 2 * i + par, 32, True)
            signal_squares("n4", "out2")
            dve.wait_ge(sem("out2.x"), NC)
            modulated("n4", g2, 48, CHUNKS["h5"], 2 * NC)

            def ffn_conv(pair, par, m, n):
                dve.wait_ge(sem("bank_read"), n)
                u = total[par]
                TS(conv[par], u, V("ffn_w", 176 + m), V("ffn_b", m), ALU.mult, ALU.add).then_inc(sem("tap"), 1)
                dve.wait_ge(sem("tap"), TAPS["up"] + 2 * m + 1)
                STT(conv[par][:, 1:T], u[:, 0:T - 1], V("ffn_w", 88 + m), conv[par][:, 1:T], ALU.mult, ALU.add)\
                    .then_inc(sem("tap"), 1)
                dve.wait_ge(sem("tap"), TAPS["up"] + 2 * m + 2)
                STT(conv[par][:, 2:T], u[:, 0:T - 2], V("ffn_w", m), conv[par][:, 2:T], ALU.mult, ALU.add)\
                    .then_inc(sem("up.conv"), 1)

            def ffn_group(g, final):
                pair = PAIR0["ffn"] + 19 * g
                with dve.Fori(0, FFN_BLOCKS) as i:
                    j = FFN_BLOCKS * g + i
                    m = 2 * FFN_BLOCKS * g + 2 * i
                    n = add_halves(pair + i, 0, total[0])
                    split_low(pair + i + 1, 0, 0)
                    ffn_conv(pair + i, 0, m, n)
                    split_low(pair + i + 1, 0, 1)
                    dve.wait_ge(sem("up.sig"), j + 1)
                    TT(wide[1], conv[0], sig[0], ALU.mult).then_inc(sem("up.silu"), 1)
                    n = add_halves(pair + i, 1, total[1])
                    ffn_conv(pair + i, 1, m + 1, n)
                    dve.wait_ge(sem("up.silu"), j + 1)
                    dve.wait_ge(sem("up.conv"), m + 2)
                    TT(wide[0], wide[1], conv[1], ALU.mult).then_inc(sem("up.act"), 1)
                    split_low(pair + i + 1, 1, 0)
                    dve.wait_ge(sem("u_high"), FF_GROUPS * FF_BLOCKS + j + 1)
                    TT(ob(U, i, 1), wide[0], ob(U, i, 0).bitcast(F32), ALU.subtract).then_inc(sem("ffn.u_ready"), 1)
                    split_low(pair + i + 1, 1, 1)
                pair = pair + FFN_BLOCKS
                if final:
                    clear_ss("down")
                with dve.Fori(0, 7 if final else 8) as i:
                    for par in range(2):
                        gated("down", pair + i, par, 16 * g + 2 * i + par, 2 * i + par, 80, final)
                if final:
                    for par in range(2):
                        gated("down", pair + 7, par, 16 * g + 14 + par, 14 + par, 80, True, ahead=False)

            with dve.Fori(0, FFN_GROUPS - 1) as g:
                ffn_group(g, False)
            ffn_group(FFN_GROUPS - 1, True)
            signal_squares("n5", "down")
            inverse("n5")
            for m in range(NC):
                STT(zb(m), xb(m), V("g_out", m), R[:, :], ALU.mult, ALU.mult).then_inc(sem("final.out"), 1)

        @block.gpsimd
        def _(pool):
            pool.wait_ge(sem("relrow_ready"), 1)
            pool.dma_start(t["rel_rows"], relrow[:, :]).then_inc(sem("relrow_stored"), 16)
            pool.wait_ge(sem("relrow_stored"), 16)
            pool.wait_ge(sem("in2_conv.out"), CONV_CH)
            for h in range(N_HEADS):
                if h >= 2:
                    pool.wait_ge(sem("at2.scores"), h - 1)
                rows = bass.AP(t["rel_rows"].tensor, h * REL_W, [[1, P], [1, 256]])
                pool.dma_start(relb[h % 2], rows).then_inc(sem("relb_landed%d" % (h % 2)), 16)


def make_constants():
    t_ = np.arange(P)
    ident = np.eye(P)
    le = (t_[:, None] <= t_[None, :]) * 1.0
    gt = (t_[:, None] > t_[None, :]) * 1.0
    one = np.ones((P, P))
    causal = np.where(t_[None, :] <= t_[:, None], 0.0, FAR)
    con = np.concatenate([ident, le, one, le, one, gt, causal, 0 * one, causal, ident[:, ::-1]], 1)
    return np.ascontiguousarray(con.astype(np.float32))


def make_onehot():
    dist = 255 - np.arange(REL_W)
    n = np.maximum(dist, 0)
    exact = REL_BUCKETS // 2
    nf = np.maximum(n, exact).astype(np.float32)
    large = exact + (np.log(nf / np.float32(exact)) / np.float32(np.log(REL_MAX_DIST / exact))
                     * np.float32(REL_BUCKETS - exact)).astype(np.int32)
    bucket = np.where(n < exact, n, np.minimum(large, REL_BUCKETS - 1))
    hot = np.zeros((REL_BUCKETS + 1, REL_W), np.float32)
    on = dist >= 0
    hot[bucket[on], np.arange(REL_W)[on]] = 1.0
    hot[REL_BUCKETS, ~on] = FAR
    return hot


def tiles(w):
    k, n = w.shape
    return np.ascontiguousarray(w.reshape(k // P, P, n // P, P).transpose(2, 1, 0, 3)).reshape(n // P, P, k)


def columns(v):
    return v.reshape(-1, P).T


def layout(a):
    a = {k: np.asarray(v) for k, v in a.items()}
    w_in, w2 = a["w_in"][0], a["w_in_2"][0]
    gates = tiles(w_in[:, 6152:10248]).reshape(2, NC, P, D).transpose(1, 0, 2, 3).reshape(32, P, D)
    cb, cc, cv = w_in[:, 0:1024], w_in[:, 1024:2048], w_in[:, 2048:3072]
    ff1, ff2 = tiles(a["w_ff1"][0]), a["w_ff2"][0].reshape(FF_GROUPS, -1, D)
    up = tiles(a["w_up_2"][0]).reshape(2, FFN // P, P, D).transpose(1, 0, 2, 3).reshape(-1, P, D)
    down = a["w_down_2"][0].reshape(FFN_GROUPS, -1, D)
    by_unit = lambda v: columns(v).reshape(P, 2, FFN // P).transpose(0, 2, 1).reshape(P, -1)
    row = lambda v: np.broadcast_to(v, (P, v.shape[-1]))
    conv2 = a["conv_ffn_w_2"][0]
    vectors = {
        "g_mix": columns(a["g_mix"]), "g_mlp": columns(a["g_mlp"]), "b_gate": columns(a["b_gate"]),
        "conv_w": np.concatenate([columns(a["conv_w"][0, j]) for j in range(3)], 1),
        "b_f": row(a["b_f"]), "g_final": columns(a["g_final"]), "c": columns(a["c_2"]),
        "b_ada": columns(a["b_ada_2"]), "g_mix2": columns(a["norm_mix_g_2"]), "g_attn": columns(a["attn_norm_g_2"]),
        "ssm_w": np.concatenate([columns(a["conv_ssm_w_2"][0, j]) for j in range(4)], 1),
        "ssm_b": columns(a["conv_ssm_b_2"]), "dt_bias": row(a["dt_bias_2"]), "a_log": row(a["a_log_2"]),
        "d_skip": columns(np.repeat(a["d_skip_2"][0], SSM_DIM)), "g_ssm": columns(a["ssm_norm_g_2"]),
        "g_ffn": columns(a["norm_ffn_g_2"]),
        "ffn_w": np.concatenate([by_unit(conv2[j]) for j in range(3)], 1), "ffn_b": by_unit(a["conv_ffn_b_2"]),
        "g_out": columns(a["final_norm_g_2"]),
    }
    by_chunk = lambda w: np.ascontiguousarray(w.reshape(NC, P, -1).transpose(1, 0, 2))
    arrays = {
        "x": by_chunk(a["x"][0].T),
        "vectors": np.concatenate([vectors[n] for n, _ in VEC_SIZES], 1),
        "consts": make_constants(),
        "rel_onehot": make_onehot(),
        "rel_bias": a["rel_bias_2"],
        "w_gate": gates,
        "w_z": np.concatenate([tiles(w) for w in (cb, cc, cv, w_in[:, 3072:6144])]),
        "w_f": by_chunk(w_in[:, 6144:6152]),
        "w_branch": np.concatenate([tiles(a["w_conv_out"][0]), tiles(a["w_attn_out"][0])], 2),
        "w_mix": tiles(a["w_mix_out"][0]),
        "w_ff1": ff1,
        "w_ff2": np.concatenate([tiles(g) for g in ff2]),
        "w_ada": a["w_ada_2"][0].reshape(NC, P, ADA_GROUPS, ADA_COLS).transpose(2, 0, 1, 3).reshape(-1, P, ADA_COLS),
        "w_in2": np.concatenate([tiles(w) for w in (w2[:, 0:3072], w2[:, 4096:5120], w2[:, 3072:4096], w2[:, 5120:5632])]),
        "w_dt": by_chunk(w2[:, 5632:5648]),
        "w_out2": tiles(a["w_out_2"][0]),
        "w_up": up,
        "w_down": np.concatenate([tiles(g) for g in down]),
    }
    return {name: np.ascontiguousarray(array) for name, array in arrays.items()}


def kernel(**a):
    import concourse.bacc as bacc
    from concourse.bass_utils import run_bass_kernel_spmd

    arrays = layout(a)
    nc = bacc.Bacc("TRN2", target_bir_lowering=False, num_devices=1)
    t, given = {}, {}
    for name, array in arrays.items():
        given["in_" + name] = array
        t[name] = nc.dram_tensor("in_" + name, array.shape, F32, kind="ExternalInput").ap()
    t["out"] = nc.dram_tensor("out_xT", (P, NC, T), F32, kind="ExternalOutput").ap()
    t["rel_rows"] = nc.dram_tensor("rel_rows", (N_HEADS, REL_W), F32, kind="Internal").ap()
    build(nc, t)
    r = run_bass_kernel_spmd(nc, [given], core_ids=[0])
    out = r.results[0]["out_xT"]
    return np.ascontiguousarray(out.transpose(2, 1, 0)).reshape(1, T, D)
```

```python
from contextlib import ExitStack

import numpy as np

import concourse.bass as bass
from concourse import mybir
from concourse.alu_op_type import AluOpType as ALU

F32 = mybir.dt.float32
F32R = mybir.dt.float32r
ACT = mybir.ActivationFunctionType
AX_X = mybir.AxisListType.X

P = 128
T = 256
D = 2048
NC = D // P
EPS = 1e-6
FAR = -1e30
N_HEADS = 8
HEAD_SCALE = float(P) ** -0.5
SSM_HEADS = 16
SSM_DIM = 64
FF = 8192
FF_GROUPS = 4
FF_BLOCKS = FF // P // FF_GROUPS
FFN = 5632
FFN_GROUPS = 4
FFN_BLOCKS = FFN // P // FFN_GROUPS
FIRST_CHUNKS = 8
PIECE = FIRST_CHUNKS * P
ADA_COLS = 1024
ADA_GROUPS = 6 * D // ADA_COLS
CONV_CH = 12
REL_BUCKETS, REL_MAX_DIST = 32, 128
REL_W = 384

VEC_SIZES = [("g_mix", 16), ("g_mlp", 16), ("b_gate", 32), ("conv_w", 24), ("b_f", 8), ("g_final", 16),
             ("c", 16), ("b_ada", 96), ("g_mix2", 16), ("g_attn", 8), ("ssm_w", 48), ("ssm_b", 12),
             ("dt_bias", 16), ("a_log", 16), ("d_skip", 8), ("g_ssm", 8), ("g_ffn", 16),
             ("ffn_w", 264), ("ffn_b", 88), ("g_out", 16)]
VEC_AT, _n = {}, 0
for _name, _size in VEC_SIZES:
    VEC_AT[_name] = _n
    _n += _size
VEC_N = _n

IDENT_AT, LEOL_AT, ONEGT_AT, MASK_AT, FLIP_AT, CONST_N = 0, 128, 512, 768, 1152, 1280

GROUP1 = 2 * FF_BLOCKS
GROUP2 = 2 * FFN_BLOCKS + NC
STREAM = [("gate", 16), ("conv_in", 16), ("conv_mul", 8), ("v", 8), ("qk", 16), ("gate2", 16), ("branch", 16), ("mix", 16),
          ("ff", FF_GROUPS * GROUP1), ("in2", 32), ("in2_conv", CONV_CH), ("out2", 16),
          ("ffn", FFN_GROUPS * GROUP2)]
PAIR0, _n = {}, 0
for _name, _size in STREAM:
    PAIR0[_name] = _n
    _n += _size // 2
ADA0 = {"gate": 0, "conv_in": 16, "qk": 32, "mix": 48, "ff": 64}
NORMS = ["n1", "n2", "n3", "n3b", "na", "ng0", "ng1", "n4", "n5"]
NTH = {_name: _i + 1 for _i, _name in enumerate(NORMS)}
CHUNKS = {"h%d" % (_i + 1): NC * _i for _i in range(5)}
TAPS = {"conv_mul": 0, "in2_conv": 24, "up": 24 + 3 * CONV_CH}
Z_BLOCKS = 44
CREDIT = 4


def build(nc, t):
    with ExitStack() as ctx:
        base = (nc.sbuf_base + 31) // 32 * 32
        ctx.enter_context(nc.sbuf_tensor("arena", [P, NC * 2 * T + Z_BLOCKS * T + 8], F32))

        def sb(name, shape, dt=F32):
            return ctx.enter_context(nc.sbuf_tensor(name, shape, dt))

        sems = {}

        def sem(name):
            if name not in sems:
                sems[name] = ctx.enter_context(nc.semaphore(name.replace(".", "_")))
            return sems[name]

        U = nc.alloc_sbuf_tensor_at("U", [P, NC, 2 * T], F32R, offset=base)
        G = nc.alloc_sbuf_tensor_at("G", [P, NC, 2, T], F32, offset=base)
        Z = nc.alloc_sbuf_tensor_at("Z", [P, Z_BLOCKS, T], F32, offset=base + NC * 2 * T * 4)
        B = nc.alloc_sbuf_tensor_at("B", [P, NC, 2 * T], F32R, offset=base + NC * 2 * T * 4)
        X = sb("X", [P, NC, T])
        H = sb("H", [P, NC, 2 * T], F32R)
        w_raw = sb("w_raw", [P, 4, PIECE])
        w_hi = sb("w_hi", [P, 4, PIECE], F32R)
        w_lo = sb("w_lo", [P, 4, PIECE], F32R)
        ada_w = sb("ada_w", [P, 2, ADA_COLS])
        ada_acc = Z[:, 40:44, :].rearrange("p a t -> p (a t)")
        vec = sb("vec", [P, VEC_N])
        con = sb("con", [P, CONST_N])
        ones = sb("ones", [P, P])
        epsb = sb("epsb", [P, 1])
        R = sb("R", [P, T])
        ss = sb("ss", [P, T])
        scratch = sb("scratch", [P, 3072])
        small = sb("small", [P, 496])
        mod = sb("mod", [P, 96])
        g1 = sb("g1", [P, NC])
        g2 = sb("g2", [P, NC])
        silu_c = sb("silu_c", [P, NC])
        wn = sb("wn", [P, NC * 32], F32R)
        wf = wn[:, 0:NC * 16].rearrange("p (k n) -> p k n", k=NC)
        wdt = wn[:, :].rearrange("p (k n) -> p k n", k=NC)
        wf_raw = scratch[:, 2816:2944].rearrange("p (k n) -> p k n", k=NC)
        wdt_raw = scratch[:, 2560:2816].rearrange("p (k n) -> p k n", k=NC)
        rel = sb("rel", [REL_BUCKETS + 1, 8])
        relhot = Z[0:REL_BUCKETS + 1, 36:38, :].rearrange("p a t -> p (a t)")[:, 0:REL_W]
        relrow = Z[0:8, 38:40, :].rearrange("p a t -> p (a t)")[:, 0:REL_W]

        bank = [ctx.enter_context(nc.psum_tensor(f"bank{i}", [P, 512], F32)) for i in range(8)]

        std = bank[4][:, T:2 * T]
        ident = con[:, IDENT_AT:IDENT_AT + P]
        LEOL = con[:, LEOL_AT:LEOL_AT + 384]
        LEO, LE = LEOL[:, 0:256], LEOL[:, 0:128]
        ONEGT = con[:, ONEGT_AT:ONEGT_AT + 256]
        GT = ONEGT[:, 128:256]
        MASK = con[:, MASK_AT:MASK_AT + 384]
        flip = con[:, FLIP_AT:FLIP_AT + P]

        def V(name, i=0, n=1):
            return vec[:, bass.ds(VEC_AT[name] + i, n)]

        def work(i):
            return scratch[:, i * T:(i + 1) * T]

        half = [work(0), work(1)]
        total = [work(2), work(3)]
        gate_total = [work(2), work(6)]
        wide = [work(4), work(5)]
        conv = [work(6), work(7)]
        half2 = [work(8), work(9)]
        sig = [work(10), work(11)]

        adaf = ada_w[:, :, :].rearrange("p a b -> p (a b)")
        dec0 = [adaf[:, 0:256], adaf[:, 256:512]]
        dec1 = [adaf[:, 512:640], adaf[:, 640:768]]
        qs = [adaf[:, 768:1024], adaf[:, 1024:1280]]
        vtok = [adaf[:, 1280:1536], adaf[:, 1536:1792]]
        logit = [scratch[:, 0:384], scratch[:, 384:768]]
        probT = [scratch[:, 768:1152], scratch[:, 1152:1536]]
        relb = [scratch[:, 1536:1792], scratch[:, 1792:2048]]
        prob = [scratch[:, 2048:2432], scratch[:, 2432:2816]]

        def hi(buf, k, n=1):
            return buf[:, k:k + n, 0:T] if n > 1 else buf[:, k, 0:T]

        def flat(ap):
            return ap.rearrange("p a t -> p (a t)")

        def zb(i, n=1):
            return flat(Z[:, bass.ds(i, n), :])

        def xb(i, n=1):
            return flat(X[:, bass.ds(i, n), :])

        def ob(buf, i, part):
            return flat(buf[:, bass.ds(i, 1), part * T:(part + 1) * T])

        block = ctx.enter_context(nc.Block())

        def piece(sp, pair, s, tiles, tile_pair, first=False):
            if not first:
                sp.wait_ge(sem("w_split"), 4 * pair + s + 1)
            cols = tiles.shape[2]
            lo, up = (0, PIECE) if s % 2 == 0 else (PIECE, cols)
            if cols < 2 * PIECE:
                cut = (cols // P + 1) // 2 * P
                lo, up = (0, cut) if s % 2 == 0 else (cut, cols)
            src = tiles[bass.ds(2 * tile_pair + s // 2, 1), :, lo:up].rearrange("a p c -> (a p) c")
            sp.dma_start(w_raw[:, s, 0:up - lo], src).then_inc(sem("w_landed%d" % s), 16)

        def stream(sp, pair0, pairs, tiles, tile_pair0):
            with sp.Fori(0, pairs) as i:
                for s in range(4):
                    piece(sp, pair0 + i, s, tiles, tile_pair0 + i)

        def cast_high0(act, A, slot):
            act.wait_ge(sem("w_landed%d" % slot), 16)
            A(w_hi[:, slot, :], w_raw[:, slot, :], ACT.Copy).then_inc(sem("w_high"), 1)

        def ssm_y(dve, STT, j):
            dve.wait_ge(sem("ssm.out"), 2 * j + 2)
            STT(zb(32 + j), zb(32 + j), V("d_skip", j), bank[6 + j % 2][:, 0:256], ALU.mult, ALU.add)\
                .then_inc(sem("ssm.y"), 1)

        @block.sync
        def _(sp):
            for i in range(4):
                sp.dma_start(X[:, 4 * i:4 * i + 4, :], t["x"][:, 4 * i:4 * i + 4, :]).then_inc(sem("x_landed%d" % i), 16)
                if i == 0:
                    sp.dma_start(vec[:, :], t["vectors"]).then_inc(sem("vec_landed"), 16)
                if i < 2:
                    piece(sp, 0, i, t["w_gate"], 0, first=True)
            for s in (2, 3):
                piece(sp, 0, s, t["w_gate"], 0, first=True)
            sp.dma_start(wf_raw[:, :, :], t["w_f"]).then_inc(sem("wf_landed"), 16)
            sp.dma_start(con[:, :], t["consts"]).then_inc(sem("con_landed"), 16)
            sp.dma_start(wdt_raw[:, :, :], t["w_dt"]).then_inc(sem("wdt_landed"), 16)
            sp.dma_start(rel[0:REL_BUCKETS, :], t["rel_bias"]).then_inc(sem("con_landed"), 16)
            stream(sp, PAIR0["gate"] + 1, 7, t["w_gate"], 1)
            stream(sp, PAIR0["conv_in"], PAIR0["gate2"] - PAIR0["conv_in"], t["w_z"], 0)
            stream(sp, PAIR0["gate2"], 8, t["w_gate"], 8)
            stream(sp, PAIR0["branch"], 8, t["w_branch"], 0)
            stream(sp, PAIR0["mix"], 8, t["w_mix"], 0)
            sp.wait_ge(sem("branch.operand"), 8 + N_HEADS)
            sp.dma_start(relhot, t["rel_onehot"]).then_inc(sem("hot_landed"), 16)
            with sp.Fori(0, FF_GROUPS) as g:
                stream(sp, PAIR0["ff"] + 16 * g, 8, t["w_ff1"], 8 * g)
                stream(sp, PAIR0["ff"] + 16 * g + 8, 8, t["w_ff2"], 8 * g)
            stream(sp, PAIR0["in2"], 22, t["w_in2"], 0)
            stream(sp, PAIR0["out2"], 8, t["w_out2"], 0)
            with sp.Fori(0, FFN_GROUPS) as g:
                stream(sp, PAIR0["ffn"] + 19 * g, 11, t["w_up"], 11 * g)
                stream(sp, PAIR0["ffn"] + 19 * g + 11, 8, t["w_down"], 8 * g)
            for m in range(NC):
                sp.wait_ge(sem("final.out"), m + 1)
                sp.dma_start(t["out"][:, m, :], zb(m)).then_inc(sem("out_stored"), 16)
            sp.wait_ge(sem("out_stored"), 16 * NC)

        @block.tensor
        def _(pe):
            def mm(out, lhsT, rhs, start, stop):
                return nc.tensor.matmul(out, lhsT, rhs, start=start, stop=stop, skip_group_check=True)

            def unit(pair, par, buf, chunks, operand=None, operand_base=0, two_banks=False):
                cut = FIRST_CHUNKS if chunks == NC else (chunks + 1) // 2
                pe.wait_ge(sem("bank_read"), 2 * pair + par + 1)
                for h, (k0, n) in enumerate(((0, cut), (cut, chunks - cut))):
                    pe.wait_ge(sem("w_split"), CREDIT + 4 * pair + 2 * par + h + 1)
                    dst = bank[2 * h + par] if two_banks else bank[par]
                    for c in range(n):
                        if par == 0 and operand and c % 4 == 0:
                            pe.wait_ge(sem(operand), operand_base + k0 + min(c + 4, n))
                        lhs = slice(c * P, (c + 1) * P)
                        start = c == 0 and (h == 0 or two_banks)
                        stop = c == n - 1 and (h == 1 or two_banks)
                        mm(dst[:, :], w_hi[:, 2 * par + h, lhs], buf[:, k0 + c, :], start, False)
                        end = mm(dst[:, T:2 * T], w_lo[:, 2 * par + h, lhs], buf[:, k0 + c, 0:T], False, stop)
                    end.then_inc(sem("piece_used"), 1)

            def pair_of_units(pair, *args, **kwargs):
                for par in range(2):
                    unit(pair, par, *args, **kwargs)

            def ada_reduce(group):
                pe.wait_ge(sem("ada_acc"), 1 + 16 * group + 16)
                pe.wait_ge(sem("mod_ready"), group)
                for b in range(ADA_COLS // P):
                    last = mm(bank[5][:, b:b + 1], ada_acc[:, b * P:(b + 1) * P], ones[:, 0:1], b == 0, True)
                last.then_inc(sem("ada_reduced"), 1)

            def sum_squares(name):
                pe.wait_ge(sem("norm.squares"), NTH[name])
                if NTH[name] > 1:
                    pe.wait_ge(sem("norm.root"), NTH[name] - 1)
                mm(bank[4][:, 0:T], ones[:, :], ss[:, :], True, True).then_inc(sem("norm.summed"), 1)

            pair_of_units(PAIR0["gate"], H, NC, "h_ready", CHUNKS["h1"])
            pe.wait_ge(sem("ones_ready"), 1)
            sum_squares("n1")
            for b in range(2):
                last = mm(bank[6][:, b:b + 1], ss[:, b * P:(b + 1) * P], ones[:, 0:1], b == 0, True)
            last.then_inc(sem("n1.tok"), 1)
            with pe.Fori(1, 8) as i:
                pair_of_units(PAIR0["gate"] + i, H, NC)
            ada_reduce(0)
            pe.wait_ge(sem("wn_split"), 1)
            for b in range(2):
                for k in range(NC):
                    toks = slice(b * P, (b + 1) * P)
                    mm(bank[4][:, 32 * b:32 * b + 16], H[:, k, toks], wf[:, k, :], b == 0 and k == 0, False)
                    last = mm(bank[4][:, 32 * b:32 * b + 8], H[:, k, T + b * P:T + (b + 1) * P], wf[:, k, 0:8],
                              False, k == NC - 1)
            last.then_inc(sem("soft.logits"), 1)
            with pe.Fori(0, 8) as i:
                pair_of_units(PAIR0["conv_in"] + i, H, NC)
            ada_reduce(1)
            with pe.Fori(0, 8) as i:
                pair_of_units(PAIR0["conv_mul"] + i, H, NC)
            with pe.Fori(0, 8) as i:
                pair_of_units(PAIR0["qk"] + i, H, NC)
            ada_reduce(2)

            def attention(name, k_step, k0, v0, decay, fill, out_sem, out0):
                def scores(h):
                    s = bank[2 + h % 2]
                    pe.wait_ge(sem(name + ".q_scaled"), h + 1)
                    if h >= 2:
                        pe.wait_ge(sem(name + ".exps"), 2 * h - 2)
                    q, k = qs[h % 2], zb(k0 + k_step * h)
                    mm(s[:, 0:128], q[:, 0:128], k[:, 0:128], True, False)
                    mm(s[:, 128:384], q[:, 128:256], k, False, False)
                    if decay:
                        pe.wait_ge(sem(name + ".decay_ready"), 2 * h + 2)
                        mm(s[:, 0:128], dec0[h % 2][:, 0:128], GT, False, False)
                        mm(s[:, 128:256], dec0[h % 2][:, 128:256], GT, False, False)
                        mm(s[:, 128:384], dec1[h % 2], ONEGT, False, False)
                        last = mm(s[:, 0:384], ident, MASK, False, True)
                    else:
                        pe.wait_ge(sem("relb_landed%d" % (h % 2)), 16 * (h // 2 + 1))
                        mm(s[:, 0:128], flip, relb[h % 2][:, 128:256], False, False)
                        last = mm(s[:, 128:384], flip, relb[h % 2], False, True)
                    last.then_inc(sem(name + ".scores"), 1)
                    v = zb(v0 + h)
                    if h >= 2:
                        pe.wait_ge(sem(name + ".v_copied"), h - 1)
                    for b in range(2):
                        last = nc.tensor.transpose(bank[4 + h % 2][:, b * P:(b + 1) * P], v[:, b * P:(b + 1) * P], ident)
                    last.then_inc(sem(name + ".v_turned"), 1)

                def turn_probs(h):
                    pe.wait_ge(sem(name + ".probs"), 2 * h + 2)
                    if h:
                        pe.wait_ge(sem(name + ".p_copied"), h)
                    for b in range(3):
                        last = nc.tensor.transpose(bank[6][:, b * P:(b + 1) * P], prob[h % 2][:, b * P:(b + 1) * P], ident)
                    last.then_inc(sem(name + ".p_turned"), 1)

                def mix(h):
                    pe.wait_ge(sem(name + ".v_copied"), h + 1)
                    pe.wait_ge(sem(name + ".p_copied"), h + 1)
                    if h:
                        pe.wait_ge(sem(out_sem), out0 + h)
                    mm(bank[7][:, 0:256], vtok[h % 2][:, 0:128], probT[h % 2][:, 0:256], True, False)
                    mm(bank[7][:, 128:256], vtok[h % 2][:, 128:256], probT[h % 2][:, 256:384], False, True)\
                        .then_inc(sem(name + ".mixed"), 1)

                scores(0)
                for h in range(N_HEADS):
                    fill(h, 0)
                    if h + 1 < N_HEADS:
                        scores(h + 1)
                    turn_probs(h)
                    fill(h, 1)
                    mix(h)

            pe.wait_ge(sem("con_landed"), 32)
            attention("at1", 2, 17, 32, True, lambda h, par: unit(PAIR0["gate2"] + h, par, H, NC), "branch.operand", 8)
            pair_of_units(PAIR0["branch"], B, NC, "branch.operand", two_banks=True)
            with pe.Fori(1, 8) as i:
                pair_of_units(PAIR0["branch"] + i, B, NC, two_banks=True)
            with pe.Fori(0, 8) as i:
                pair_of_units(PAIR0["mix"] + i, U, NC, "merged")
            ada_reduce(3)
            unit(PAIR0["ff"], 0, H, NC, "h_ready", CHUNKS["h2"])
            sum_squares("n2")
            unit(PAIR0["ff"], 1, H, NC)

            def ff1(g, first=0):
                with pe.Fori(first, 8) as i:
                    pair_of_units(PAIR0["ff"] + 16 * g + i, H, NC)

            def ff2(g):
                ada_reduce(2 * g + 4)
                with pe.Fori(0, 8) as i:
                    pair_of_units(PAIR0["ff"] + 16 * g + 8 + i, U, NC, "ff.u_ready", 16 * g)
                ada_reduce(2 * g + 5)

            ff1(0, 1)
            with pe.Fori(0, FF_GROUPS - 1) as g:
                ff2(g)
                ff1(g + 1)
            ff2(FF_GROUPS - 1)
            pe.wait_ge(sem("hot_landed"), 16)
            pe.wait_ge(sem("con_landed"), 32)
            pe.wait_ge(sem("rel_ones"), 1)
            mm(bank[6][0:8, 0:REL_W], rel[:, :], relhot, True, True).then_inc(sem("rel_made"), 1)
            sum_squares("n3")
            for k in range(NC):
                pe.wait_ge(sem("n3.squared"), k + 1)
                last = mm(bank[7][:, 0:T], ones[:, :], zb(k), k == 0, k == NC - 1)
            last.then_inc(sem("norm.summed"), 1)
            with pe.Fori(0, 16) as i:
                pair_of_units(PAIR0["in2"] + i, H, NC, "h_ready", CHUNKS["h3"])
            pe.wait_ge(sem("wn_split"), 2)
            for b in range(2):
                for k in range(NC):
                    toks = slice(b * P, (b + 1) * P)
                    mm(bank[4][:, 64 * b:64 * b + 32], H[:, k, toks], wdt[:, k, :], b == 0 and k == 0, False)
                    last = mm(bank[4][:, 64 * b:64 * b + 16], H[:, k, T + b * P:T + (b + 1) * P], wdt[:, k, 0:16],
                              False, k == NC - 1)
            last.then_inc(sem("soft.logits"), 1)
            with pe.Fori(0, CONV_CH // 2) as i:
                pair_of_units(PAIR0["in2_conv"] + i, H, NC, None)
            attention("at2", 1, 8, 16, False, lambda h, par: None, "at2.out", 0)

            pe.wait_ge(sem("in2_conv.out"), CONV_CH)
            for grp in range(2):
                b_, c_ = zb(40 + grp), zb(42 + grp)
                mm(bank[grp][:, 0:256], b_[:, 0:128], c_, True, False)
                mm(bank[grp][:, 256:384], b_[:, 128:256], c_[:, 128:256], False, True).then_inc(sem("cb_ready"), 1)
            for n in range(4):
                b, q = n // 2, n % 2
                if n >= 2:
                    pe.wait_ge(sem("xdt_ready"), n - 1)
                for j in range(4):
                    last = nc.tensor.transpose(bank[2 + n % 2][:, j * P:(j + 1) * P],
                                               zb(32 + 4 * q + j)[:, b * P:(b + 1) * P], ident)
                last.then_inc(sem("xs_turned"), 1)

            def decays(h):
                pe.wait_ge(sem("ssm.decay_ready"), 2 * h + 2)
                if h >= 2:
                    pe.wait_ge(sem("ssm.exp"), h - 1)
                else:
                    pe.wait_ge(sem("cb_masked"), 2)
                s = bank[h % 2]
                mm(s[:, 0:256], GT, dec0[h % 2], True, False)
                mm(s[:, 128:256], ones[:, :], dec1[h % 2], False, False)
                mm(s[:, 256:384], GT, dec1[h % 2], False, True).then_inc(sem("ssm.decays"), 1)

            def outputs(h):
                j, rows = h // 2, 64 * (h % 2)
                pe.wait_ge(sem("ssm.weights"), h + 1)
                if h % 2 == 0 and j >= 2:
                    pe.wait_ge(sem("ssm.y"), j - 1)
                o = bank[6 + j % 2][rows:rows + 64, 0:256]
                o2 = bank[6 + j % 2][rows:rows + 64, 128:256]
                xd = flat(Z[:, 8:16, :])
                w = logit[h % 2]
                mm(o, xd[:, h * 64:(h + 1) * 64], w[:, 0:256], True, False)
                mm(o2, xd[:, 1024 + h * 64:1024 + (h + 1) * 64], w[:, 256:384], False, True).then_inc(sem("ssm.out"), 1)

            pe.wait_ge(sem("xdt_ready"), 4)
            decays(0)
            for h in range(SSM_HEADS):
                if h + 1 < SSM_HEADS:
                    decays(h + 1)
                outputs(h)
            for name in ("na", "ng0", "ng1"):
                sum_squares(name)
            with pe.Fori(0, 8) as i:
                pair_of_units(PAIR0["out2"] + i, H, NC, "h_ready", CHUNKS["h4"])
            sum_squares("n4")

            def ffn_group(g):
                pair = PAIR0["ffn"] + 19 * g
                with pe.Fori(0, FFN_BLOCKS) as i:
                    pair_of_units(pair + i, H, NC, "h_ready", CHUNKS["h5"])
                with pe.Fori(0, 8) as i:
                    pair_of_units(pair + FFN_BLOCKS + i, U, FFN_BLOCKS, "ffn.u_ready", FFN_BLOCKS * g)

            with pe.Fori(0, FFN_GROUPS - 1) as g:
                ffn_group(g)
            ffn_group(FFN_GROUPS - 1)
            sum_squares("n5")

        @block.scalar
        def _(act):
            A = nc.scalar.activation

            def cast_high(pair, par, h):
                slot = 2 * par + h
                act.wait_ge(sem("w_landed%d" % slot), 16 * pair + 16)
                act.wait_ge(sem("piece_used"), 4 * pair + slot + 1)
                A(w_hi[:, slot, :], w_raw[:, slot, :], ACT.Copy).then_inc(sem("w_high"), 1)

            def load_sigmoid():
                A(small[:, 16:17], V("c"), ACT.Sigmoid)

            def load_ada(chunk, slot):
                act.wait_ge(sem("ada_acc"), chunk)
                act.dma_start(ada_w[:, slot, :], t["w_ada"][bass.ds(chunk, 1)].rearrange("a p c -> (a p) c"))\
                    .then_inc(sem("ada_landed%d" % slot), 16)

            def take_half(pair, par, scale=1.0):
                act.wait_ge(sem("piece_used"), CREDIT + 4 * pair + 2 * par + 2)
                A(half[par], bank[par][:, T:2 * T], ACT.Copy, scale=scale).then_inc(sem("halves"), 1)

            def root(name, count=D, src=bank[4]):
                act.wait_ge(sem("norm.summed"), NTH[name])
                if NTH[name] > 1:
                    act.wait_ge(sem("norm.inverse"), NTH[name] - 1)
                A(std, src[:, 0:T], ACT.Sqrt, bias=epsb[:, :], scale=1.0 / count).then_inc(sem("norm.root"), 1)

            act.wait_ge(sem("vec_landed"), 16)
            def first_chunks(i):
                act.wait_ge(sem("x_landed%d" % i), 16)
                for k in range(4 * i, 4 * i + 4):
                    A(H[:, k, 0:T], X[:, k, :], ACT.Copy, scale=V("g_mix", k)).then_inc(sem("h_high"), 1)

            for i in range(4):
                first_chunks(i)
                if i < 2:
                    cast_high0(act, A, i)
            cast_high0(act, A, 2)
            cast_high0(act, A, 3)
            for i in range(4):
                A(zb(4 * i, 4), xb(4 * i, 4), ACT.Square).then_inc(sem("x_squares"), 1)
            A(small[:, 16:32], V("c", 0, 16), ACT.Sigmoid).then_inc(sem("c_sig"), 1)
            act.wait_ge(sem("ada_credit"), 1)
            load_ada(0, 0)
            load_ada(1, 1)

            def plain(pair, par, chunk=None, ahead=True):
                take_half(pair, par)
                cast_high(pair + 1, par, 0)
                cast_high(pair + 1, par, 1)
                if chunk is not None and ahead:
                    load_ada(chunk + 2, par)

            for par in range(2):
                plain(PAIR0["gate"], par)
            for par in range(2):
                load_ada(ADA0["gate"] + 2 + par, par)
            root("n1")
            act.wait_ge(sem("n1.tok"), 1)
            A(small[:, 0:2], bank[6][:, 0:2], ACT.Sqrt, bias=epsb[:, :], scale=1.0 / D).then_inc(sem("n1.stdtok"), 1)
            act.wait_ge(sem("wf_landed"), 16)
            A(wf[:, :, 0:8], wf_raw, ACT.Copy).then_inc(sem("wn_high"), 1)
            with act.Fori(1, 8) as i:
                for par in range(2):
                    plain(PAIR0["gate"] + i, par, ADA0["gate"] + 2 * i + par)
            act.wait_ge(sem("soft.logits"), 1)
            for b in range(2):
                A(small[:, 32 + 8 * b:40 + 8 * b], bank[4][:, 32 * b + 8:32 * b + 16], ACT.Copy).then_inc(sem("soft.half"), 1)
            act.wait_ge(sem("soft.nabs"), 1)
            A(small[:, 64:80], small[:, 80:96], ACT.Exp).then_inc(sem("soft.exp"), 1)
            act.wait_ge(sem("soft.exp"), 1)
            A(small[:, 96:112], small[:, 64:80], ACT.Ln, bias=1.0).then_inc(sem("soft.ln"), 1)
            act.wait_ge(sem("wdt_landed"), 16)
            A(wdt[:, :, 0:16], wdt_raw, ACT.Copy).then_inc(sem("wn_high"), 1)
            with act.Fori(0, 8) as i:
                for par in range(2):
                    plain(PAIR0["conv_in"] + i, par, ADA0["conv_in"] + 2 * i + par)
            with act.Fori(0, 4) as i:
                for par in range(2):
                    plain(PAIR0["conv_mul"] + i, par)
                    act.wait_ge(sem("conv_mul.y"), 2 * i + par + 1)
                    act.sem_inc(sem("wait_over"), 1)
                    A(ob(B, 2 * i + par, 0), wide[par], ACT.Copy).then_inc(sem("conv_mul.high"), 1)
            with act.Fori(0, 4) as i:
                for par in range(2):
                    plain(PAIR0["v"] + i, par)
            with act.Fori(0, 7) as i:
                for par in range(2):
                    plain(PAIR0["qk"] + i, par, ADA0["qk"] + 2 * i + par)
            for par in range(2):
                plain(PAIR0["qk"] + 7, par, ADA0["qk"] + 14 + par, ahead=False)

            def attention(name, q0, q_step, out_high, fill):
                def scale_q(h):
                    if h >= 2:
                        act.wait_ge(sem(name + ".scores"), h - 1)
                    A(qs[h % 2], zb(q0 + q_step * h), ACT.Copy, scale=HEAD_SCALE).then_inc(sem(name + ".q_scaled"), 1)

                def copy_values(h):
                    act.wait_ge(sem(name + ".v_turned"), h + 1)
                    if h >= 2:
                        act.wait_ge(sem(name + ".mixed"), h - 1)
                    A(vtok[h % 2], bank[4 + h % 2][:, 0:256], ACT.Copy).then_inc(sem(name + ".v_copied"), 1)

                def exps(h):
                    act.wait_ge(sem(name + ".maxes"), 2 * h + 2)
                    if h >= 2:
                        act.wait_ge(sem(name + ".p_turned"), h - 1)
                    for b, (lo, up) in enumerate(((0, 128), (128, 384))):
                        c = 128 + 2 * h + b
                        A(prob[h % 2][:, lo:up], bank[2 + h % 2][:, lo:up], ACT.Exp, bias=small[:, c:c + 1],
                          accum_out=small[:, c + 16:c + 17]).then_inc(sem(name + ".exps"), 1)

                def copy_probs(h):
                    act.wait_ge(sem(name + ".p_turned"), h + 1)
                    if h >= 2:
                        act.wait_ge(sem(name + ".mixed"), h - 1)
                    A(probT[h % 2], bank[6][:, 0:384], ACT.Copy).then_inc(sem(name + ".p_copied"), 1)

                def high(h):
                    act.wait_ge(sem(name + ".mixed"), h + 1)
                    A(ob(B, 8 + h, 0), bank[7][:, 0:256], ACT.Copy).then_inc(sem(name + ".high"), 1)

                scale_q(0)
                copy_values(0)
                exps(0)
                for h in range(N_HEADS):
                    if h + 1 < N_HEADS:
                        scale_q(h + 1)
                    if out_high and h:
                        high(h - 1)
                    fill(h, 0)
                    if h + 1 < N_HEADS:
                        copy_values(h + 1)
                    copy_probs(h)
                    if h + 1 < N_HEADS:
                        exps(h + 1)
                    fill(h, 1)
                if out_high:
                    high(N_HEADS - 1)

            act.wait_ge(sem("qk.out"), 16)
            act.wait_ge(sem("v.out"), 8)
            attention("at1", 16, 2, True, lambda h, par: plain(PAIR0["gate2"] + h, par))
            load_ada(ADA0["mix"], 0)
            load_ada(ADA0["mix"] + 1, 1)
            load_sigmoid()

            with act.Fori(0, 8) as i:
                for par in range(2):
                    pair, m = PAIR0["branch"] + i, 2 * i + par
                    act.wait_ge(sem("branch.gated"), 2 * m)
                    A(sig[par], flat(G[:, bass.ds(m, 1), 0, :]), ACT.Sigmoid, bias=V("b_gate", m)).then_inc(sem("gates_open"), 1)
                    A(wide[par], flat(G[:, bass.ds(m, 1), 1, :]), ACT.Sigmoid, bias=V("b_gate", 16 + m)).then_inc(sem("gates_open"), 1)
                    act.wait_ge(sem("piece_used"), CREDIT + 4 * pair + 2 * par + 2)
                    A(half[par], bank[par][:, T:2 * T], ACT.Copy).then_inc(sem("halves_b"), 1)
                    A(half2[par], bank[2 + par][:, T:2 * T], ACT.Copy).then_inc(sem("halves_b"), 1)
                    cast_high(pair + 1, par, 0)
                    cast_high(pair + 1, par, 1)
                    act.wait_ge(sem("merge"), m + 1)
                    act.sem_inc(sem("wait_over"), 1)
                    A(ob(U, m, 0), conv[par], ACT.Copy).then_inc(sem("merged_high"), 1)
            with act.Fori(0, 8) as i:
                for par in range(2):
                    pair, m = PAIR0["mix"] + i, 2 * i + par
                    take_half(pair, par)
                    cast_high(pair + 1, par, 0)
                    cast_high(pair + 1, par, 1)
                    act.wait_ge(sem("mix.x"), m + 1)
                    A(ob(H, m, 0), xb(m), ACT.Copy, scale=V("g_mlp", m)).then_inc(sem("h_high"), 1)
                    A(wide[par], xb(m), ACT.Square).then_inc(sem("mix.squared"), 1)
                    load_ada(ADA0["mix"] + m + 2, par)
            root("n2")

            def ff1_unit(pair, par, m, u, chunk):
                take_half(pair, par)
                cast_high(pair + 1, par, 0)
                act.wait_ge(sem("ff.relu"), m + 1)
                A(ob(U, u, 0), wide[par], ACT.Square).then_inc(sem("u_high"), 1)
                A(conv[par], wide[par], ACT.Square).then_inc(sem("ff.u_full"), 1)
                cast_high(pair + 1, par, 1)
                load_ada(chunk + 2, par)

            def ff2_unit(pair, par, m, block, chunk, squares=False):
                take_half(pair, par)
                cast_high(pair + 1, par, 0)
                cast_high(pair + 1, par, 1)
                if squares:
                    act.wait_ge(sem("ff.x"), m + 1)
                    A(wide[par], xb(block), ACT.Square).then_inc(sem("ff.squared"), 1)
                if chunk is not None:
                    load_ada(chunk + 2, par)

            def ff_group(g, final):
                pair = PAIR0["ff"] + 16 * g
                with act.Fori(0, 8) as i:
                    for par in range(2):
                        ff1_unit(pair + i, par, 16 * g + 2 * i + par, 2 * i + par, ADA0["ff"] + 32 * g + 2 * i + par)
                with act.Fori(0, 7 if final else 8) as i:
                    for par in range(2):
                        ff2_unit(pair + 8 + i, par, 16 * g + 2 * i + par, 2 * i + par, ADA0["ff"] + 32 * g + 16 + 2 * i + par, final)
                if final:
                    for par in range(2):
                        ff2_unit(pair + 15, par, 16 * g + 14 + par, 14 + par, None, True)

            with act.Fori(0, FF_GROUPS - 1) as g:
                ff_group(g, False)
            ff_group(FF_GROUPS - 1, True)
            root("n3")
            for k in range(NC):
                act.wait_ge(sem("n3.x"), k + 1)
                A(zb(k), xb(k), ACT.Square).then_inc(sem("n3.squared"), 1)
            root("n3b", src=bank[7])
            for k in range(NC):
                act.wait_ge(sem("normed"), k + 1)
                A(H[:, k, 0:T], work(4 + k % 4), ACT.Identity, bias=mod[:, k:k + 1]).then_inc(sem("h_high"), 1)
            with act.Fori(0, 16) as i:
                for par in range(2):
                    plain(PAIR0["in2"] + i, par)
            act.wait_ge(sem("soft.logits"), 2)
            for b in range(2):
                A(small[:, 192 + 16 * b:208 + 16 * b], bank[4][:, 64 * b + 16:64 * b + 32], ACT.Copy).then_inc(sem("soft.half"), 1)
            A(small[:, 480:496], V("a_log", 0, 16), ACT.Exp).then_inc(sem("a_exp"), 1)
            act.wait_ge(sem("soft.nabs"), 2)
            A(small[:, 224:256], small[:, 256:288], ACT.Exp).then_inc(sem("soft.exp"), 1)
            act.wait_ge(sem("soft.exp"), 2)
            A(small[:, 288:320], small[:, 224:256], ACT.Ln, bias=1.0).then_inc(sem("soft.ln"), 1)
            load_sigmoid()
            with act.Fori(0, CONV_CH // 2) as i:
                for par in range(2):
                    pair, m = PAIR0["in2_conv"] + i, 2 * i + par
                    take_half(pair, par)
                    cast_high(pair + 1, par, 0)
                    cast_high(pair + 1, par, 1)
                    act.wait_ge(sem("in2_conv.conv"), m + 1)
                    A(sig[par], conv[par], ACT.Sigmoid).then_inc(sem("in2_conv.sig"), 1)
            act.wait_ge(sem("in2.out"), 32)
            attention("at2", 0, 1, False, lambda h, par: None)
            for h in range(SSM_HEADS):
                act.wait_ge(sem("ssm.decays"), h + 1)
                if h >= 2:
                    act.wait_ge(sem("ssm.weights"), h - 1)
                A(prob[h % 2], bank[h % 2][:, 0:384], ACT.Exp).then_inc(sem("ssm.exp"), 1)
            act.wait_ge(sem("ssm.out"), SSM_HEADS)
            A(adaf, zb(24, 8), ACT.Sigmoid).then_inc(sem("z_sig"), 1)
            act.wait_ge(sem("at2.out"), N_HEADS)
            A(zb(8, 8), zb(0, 8), ACT.Square).then_inc(sem("at2.squared"), 1)
            root("na", 1024)
            act.wait_ge(sem("ssm.gated"), 1)
            A(zb(16, 8), zb(32, 8), ACT.Square).then_inc(sem("ssm.squared"), 1)
            for k in range(8):
                act.wait_ge(sem("normed"), NC + k + 1)
                A(H[:, k, 0:T], work(4 + k % 4), ACT.Copy).then_inc(sem("h_high"), 1)
            for grp in range(2):
                root("ng%d" % grp, 512)
                for k in range(8 + 4 * grp, 12 + 4 * grp):
                    act.wait_ge(sem("normed"), NC + k + 1)
                    A(H[:, k, 0:T], work(4 + k % 4), ACT.Copy).then_inc(sem("h_high"), 1)

            def gated_unit(name, pair, par, m, block, gate, squares, ahead=True):
                take_half(pair, par, scale=mod[:, bass.ds(gate + block, 1)])
                if ahead:
                    cast_high(pair + 1, par, 0)
                    cast_high(pair + 1, par, 1)
                if squares:
                    act.wait_ge(sem(name + ".x"), m + 1)
                    A(wide[par], xb(block), ACT.Square).then_inc(sem(name + ".squared"), 1)

            with act.Fori(0, 8) as i:
                for par in range(2):
                    gated_unit("out2", PAIR0["out2"] + i, par, 2 * i + par, 2 * i + par, 32, True)
            root("n4")
            for k in range(NC):
                act.wait_ge(sem("normed"), 2 * NC + k + 1)
                A(H[:, k, 0:T], work(4 + k % 4), ACT.Identity, bias=mod[:, 48 + k:49 + k]).then_inc(sem("h_high"), 1)

            def ffn_group(g, final):
                pair = PAIR0["ffn"] + 19 * g
                load_sigmoid()
                with act.Fori(0, FFN_BLOCKS) as i:
                    take_half(pair + i, 0)
                    cast_high(pair + i + 1, 0, 0)
                    cast_high(pair + i + 1, 0, 1)
                    act.wait_ge(sem("up.conv"), 2 * FFN_BLOCKS * g + 2 * i + 1)
                    A(sig[0], conv[0], ACT.Sigmoid).then_inc(sem("up.sig"), 1)
                    take_half(pair + i, 1)
                    cast_high(pair + i + 1, 1, 0)
                    act.wait_ge(sem("up.act"), FFN_BLOCKS * g + i + 1)
                    A(ob(U, i, 0), wide[0], ACT.Copy).then_inc(sem("u_high"), 1)
                    cast_high(pair + i + 1, 1, 1)
                pair = pair + FFN_BLOCKS
                with act.Fori(0, 7 if final else 8) as i:
                    for par in range(2):
                        gated_unit("down", pair + i, par, 16 * g + 2 * i + par, 2 * i + par, 80, final)
                if final:
                    for par in range(2):
                        gated_unit("down", pair + 7, par, 16 * g + 14 + par, 14 + par, 80, True, ahead=False)

            with act.Fori(0, FFN_GROUPS - 1) as g:
                ffn_group(g, False)
            ffn_group(FFN_GROUPS - 1, True)
            root("n5")

        @block.vector
        def _(dve):
            v = nc.vector
            TT, STT, TS = v.tensor_tensor, v.scalar_tensor_tensor, v.tensor_scalar

            links = [0]

            def link(ins):
                links[0] += 1
                ins.then_inc(sem("dve_link"), 1)
                dve.wait_ge(sem("dve_link"), links[0])

            def split_low(pair, par, h):
                slot = 2 * par + h
                dve.wait_ge(sem("w_high"), 4 * pair + slot + 1)
                TT(w_lo[:, slot, :], w_raw[:, slot, :], w_hi[:, slot, :].bitcast(F32), ALU.subtract)\
                    .then_inc(sem("w_split"), 1)

            def add_halves(pair, par, out):
                dve.wait_ge(sem("halves"), units_with_half(pair, par))
                TT(out, bank[par][:, 0:T], half[par], ALU.add).then_inc(sem("bank_read"), 1)
                return 2 + 2 * pair + par + 1

            def units_with_half(pair, par):
                skipped = 16 if after_branch[0] else 0
                return 2 * pair + par + 1 - skipped

            after_branch = [False]

            def add_ada(chunk, k, par):
                dve.wait_ge(sem("ada_landed%d" % par), turn_value(chunk, par))
                dve.wait_ge(sem("ada_acc"), chunk + 1)
                STT(ada_acc[:, :], ada_w[:, par, :], silu_c[:, bass.ds(k, 1)], ada_acc[:, :], ALU.mult, ALU.add)\
                    .then_inc(sem("ada_acc"), 1)

            def turn_value(chunk, par):
                return chunk * 8 + (16 - 8 * par)

            def take_mod(group):
                dve.wait_ge(sem("ada_reduced"), group + 1)
                v.memset(ada_acc[:, :], 0.0).then_inc(sem("ada_zeroed"), 1)
                dve.wait_ge(sem("ada_zeroed"), group + 2)
                n = ADA_COLS // P
                TT(mod[:, bass.ds(group * n, n)], bank[5][:, 0:n], V("b_ada", group * n, n), ALU.add)\
                    .then_inc(sem("mod_ready"), 1)

            def inverse(name):
                dve.wait_ge(sem("norm.root"), NTH[name])
                v.reciprocal(R[:, :], std).then_inc(sem("norm.inverse"), 1)
                dve.wait_ge(sem("norm.inverse"), NTH[name])

            v.memset(epsb[:, :], EPS)
            v.memset(ada_acc[:, :], 0.0).then_inc(sem("ada_zeroed"), 1)
            v.memset(rel[REL_BUCKETS:REL_BUCKETS + 1, :], 1.0).then_inc(sem("rel_ones"), 1)
            v.memset(ones[:, :], 1.0).then_inc(sem("ones_ready"), 1)
            dve.sem_inc(sem("w_split"), CREDIT)
            dve.sem_inc(sem("piece_used"), CREDIT)
            dve.sem_inc(sem("bank_read"), 2)
            dve.sem_inc(sem("ada_acc"), 1)
            dve.sem_inc(sem("ada_credit"), 1)
            dve.wait_ge(sem("vec_landed"), 16)

            def first_low(i):
                dve.wait_ge(sem("w_high"), i + 1)
                TT(w_lo[:, i, :], w_raw[:, i, :], w_hi[:, i, :].bitcast(F32), ALU.subtract).then_inc(sem("w_split"), 1)

            for i in range(4):
                for k in range(4 * i, 4 * i + 4):
                    dve.wait_ge(sem("h_high"), k + 1)
                    STT(H[:, k, T:2 * T], X[:, k, :], V("g_mix", k), H[:, k, 0:T].bitcast(F32), ALU.mult, ALU.subtract)\
                        .then_inc(sem("h_ready"), 1)
                if i < 2:
                    first_low(i)
            first_low(2)
            first_low(3)
            dve.wait_ge(sem("x_squares"), 4)
            v.tensor_reduce(ss[:, :], Z[:, 0:NC, :].rearrange("p c t -> p t c"), AX_X, ALU.add)\
                .then_inc(sem("norm.squares"), 1)

            def plain_normed(name, pair, par, out, chunk=None, k=None, total=total):
                if chunk is not None:
                    add_ada(chunk, k, par)
                n = add_halves(pair, par, total[par])
                split_low(pair + 1, par, 0)
                dve.wait_ge(sem("bank_read"), n)
                TT(out, total[par], R[:, :], ALU.mult).then_inc(sem(name + ".out"), 1)
                split_low(pair + 1, par, 1)

            for par in range(2):
                n = add_halves(PAIR0["gate"], par, total[par])
                split_low(PAIR0["gate"] + 1, par, 0)
                split_low(PAIR0["gate"] + 1, par, 1)
            dve.wait_ge(sem("ada_zeroed"), 1)
            dve.wait_ge(sem("c_sig"), 1)
            link(TT(silu_c[:, :], V("c", 0, 16), small[:, 16:32], ALU.mult))
            for par in range(2):
                add_ada(ADA0["gate"] + par, par, par)
            inverse("n1")
            dve.wait_ge(sem("bank_read"), n)
            for par in range(2):
                TT(flat(G[:, 0:1, par, :]), total[par], R[:, :], ALU.mult).then_inc(sem("gate.out"), 1)
            dve.wait_ge(sem("gate.out"), 2)
            dve.wait_ge(sem("n1.stdtok"), 1)
            link(v.reciprocal(small[:, 2:4], small[:, 0:2]))
            dve.wait_ge(sem("wn_high"), 1)
            TT(wf[:, :, 8:16], wf_raw, wf[:, :, 0:8].bitcast(F32), ALU.subtract).then_inc(sem("wn_split"), 1)
            with dve.Fori(1, 8) as i:
                for par in range(2):
                    plain_normed("gate", PAIR0["gate"] + i, par, flat(G[:, bass.ds(i, 1), par, :]),
                                 ADA0["gate"] + 2 * i + par, 2 * i + par)
            take_mod(0)
            dve.wait_ge(sem("soft.half"), 2)
            y, nabs, l = small[:, 48:64], small[:, 80:96], small[:, 96:112]
            logf = small[:, 112:128]
            for b in range(2):
                s = slice(8 * b, 8 * b + 8)
                link(TT(y[:, s], bank[4][:, 32 * b:32 * b + 8], small[:, 32 + 8 * b:40 + 8 * b], ALU.add))
                link(STT(y[:, s], y[:, s], small[:, 2 + b:3 + b], V("b_f", 0, 8), ALU.mult, ALU.add))
            STT(nabs, y, -1.0, y, ALU.mult, ALU.min).then_inc(sem("soft.nabs"), 1)
            dve.wait_ge(sem("soft.ln"), 1)
            link(STT(logf, y, 0.0, l, ALU.min, ALU.subtract))
            dve.wait_ge(sem("wn_high"), 2)
            TT(wdt[:, :, 16:32], wdt_raw, wdt[:, :, 0:16].bitcast(F32), ALU.subtract).then_inc(sem("wn_split"), 1)
            with dve.Fori(0, 8) as i:
                for par in range(2):
                    m = 2 * i + par
                    plain_normed("conv_in", PAIR0["conv_in"] + i, par, zb(m), ADA0["conv_in"] + m, m)
            take_mod(1)
            with dve.Fori(0, 4) as i:
                for par in range(2):
                    pair, m = PAIR0["conv_mul"] + i, 2 * i + par
                    n = add_halves(pair, par, total[par])
                    split_low(pair + 1, par, 0)
                    dve.wait_ge(sem("bank_read"), n)
                    TT(wide[par], total[par], R[:, :], ALU.mult).then_inc(sem("conv_mul.u"), 1)
                    dve.wait_ge(sem("conv_mul.u"), 2 * m + 1)
                    TT(total[par], wide[par], zb(2 * m + 1), ALU.mult).then_inc(sem("conv_mul.u"), 1)
                    dve.wait_ge(sem("conv_mul.u"), 2 * m + 2)
                    u = total[par]
                    TS(conv[par], u, V("conv_w", 16 + m), None, ALU.mult).then_inc(sem("tap"), 1)
                    dve.wait_ge(sem("tap"), 3 * m + 1)
                    STT(conv[par][:, 1:T], u[:, 0:T - 1], V("conv_w", 8 + m), conv[par][:, 1:T], ALU.mult, ALU.add)\
                        .then_inc(sem("tap"), 1)
                    dve.wait_ge(sem("tap"), 3 * m + 2)
                    STT(conv[par][:, 2:T], u[:, 0:T - 2], V("conv_w", m), conv[par][:, 2:T], ALU.mult, ALU.add)\
                        .then_inc(sem("tap"), 1)
                    dve.wait_ge(sem("tap"), 3 * m + 3)
                    TT(wide[par], conv[par], zb(2 * m), ALU.mult).then_inc(sem("conv_mul.y"), 1)
                    split_low(pair + 1, par, 1)
                    dve.wait_ge(sem("conv_mul.high"), m + 1)
                    TT(ob(B, m, 1), wide[par], ob(B, m, 0).bitcast(F32), ALU.subtract).then_inc(sem("branch.operand"), 1)
            with dve.Fori(0, 4) as i:
                for par in range(2):
                    m = 2 * i + par
                    plain_normed("v", PAIR0["v"] + i, par, zb(32 + m))
            with dve.Fori(0, 8) as i:
                for par in range(2):
                    m = 2 * i + par
                    plain_normed("qk", PAIR0["qk"] + i, par, zb(16 + m), ADA0["qk"] + m, m)
            take_mod(2)

            def decay_operands(name, h, a0, a1):
                TS(dec0[h % 2], LEO, a0, None, ALU.mult).then_inc(sem(name + ".decay_ready"), 1)
                TS(dec1[h % 2], LE, a1, None, ALU.mult).then_inc(sem(name + ".decay_ready"), 1)

            def attention(name, decay, fill, out_sem):
                def maxes(h):
                    dve.wait_ge(sem(name + ".scores"), h + 1)
                    for b, (lo, up) in enumerate(((0, 128), (128, 384))):
                        c = 128 + 2 * h + b
                        v.tensor_reduce(small[:, c:c + 1], bank[2 + h % 2][:, lo:up], AX_X, ALU.max, negate=True)\
                            .then_inc(sem(name + ".maxes"), 1)
                    if decay and h + 2 < N_HEADS:
                        decay_operands(name, h + 2, logf[:, h + 2:h + 3], logf[:, 8 + h + 2:9 + h + 2])

                def normalise(h):
                    dve.wait_ge(sem(name + ".exps"), 2 * h + 2)
                    c = 144 + 2 * h
                    link(v.reciprocal(small[:, c + 16:c + 18], small[:, c:c + 2]))
                    for b, (lo, up) in enumerate(((0, 128), (128, 384))):
                        TS(prob[h % 2][:, lo:up], prob[h % 2][:, lo:up], small[:, c + 16 + b:c + 17 + b], None, ALU.mult)\
                            .then_inc(sem(name + ".probs"), 1)

                def finish(h):
                    if decay:
                        dve.wait_ge(sem(name + ".high"), h + 1)
                        TT(ob(B, 8 + h, 1), bank[7][:, 0:256], ob(B, 8 + h, 0).bitcast(F32), ALU.subtract)\
                            .then_inc(sem(out_sem), 1)
                    else:
                        dve.wait_ge(sem(name + ".mixed"), h + 1)
                        v.tensor_copy(zb(h), bank[7][:, 0:256]).then_inc(sem(out_sem), 1)

                if decay:
                    for h in range(2):
                        decay_operands(name, h, logf[:, h:h + 1], logf[:, 8 + h:9 + h])
                maxes(0)
                normalise(0)
                for h in range(N_HEADS):
                    if h:
                        finish(h - 1)
                    fill(h, 0)
                    if h + 1 < N_HEADS:
                        maxes(h + 1)
                        normalise(h + 1)
                    fill(h, 1)
                finish(N_HEADS - 1)

            dve.wait_ge(sem("con_landed"), 32)
            attention("at1", True, lambda h, par: plain_normed(
                "gate", PAIR0["gate2"] + h, par, flat(G[:, 8 + h:9 + h, par, :]), total=gate_total), "branch.operand")
            dve.sem_inc(sem("branch.gated"), 2)
            with dve.Fori(0, 8) as i:
                for par in range(2):
                    pair, m = PAIR0["branch"] + i, 2 * i + par
                    dve.wait_ge(sem("halves_b"), 2 * m + 2)
                    TT(total[par], bank[par][:, 0:T], half[par], ALU.add).then_inc(sem("branch.sum"), 1)
                    TT(conv[par], bank[2 + par][:, 0:T], half2[par], ALU.add).then_inc(sem("bank_read"), 1)
                    split_low(pair + 1, par, 0)
                    dve.wait_ge(sem("gates_open"), 2 * m + 2)
                    dve.wait_ge(sem("branch.sum"), m + 1)
                    dve.wait_ge(sem("bank_read"), 2 + 2 * pair + par + 1)
                    TT(total[par], total[par], sig[par], ALU.mult).then_inc(sem("branch.gated"), 1)
                    TT(conv[par], conv[par], wide[par], ALU.mult).then_inc(sem("branch.gated"), 1)
                    dve.wait_ge(sem("branch.gated"), 2 + 2 * m + 2)
                    TT(conv[par], total[par], conv[par], ALU.add).then_inc(sem("merge"), 1)
                    split_low(pair + 1, par, 1)
                    dve.wait_ge(sem("merged_high"), m + 1)
                    TT(ob(U, m, 1), conv[par], ob(U, m, 0).bitcast(F32), ALU.subtract).then_inc(sem("merged"), 1)
            after_branch[0] = True

            def clear_ss(name):
                v.memset(ss[:, :], 0.0).then_inc(sem(name + ".cleared"), 1)
                dve.wait_ge(sem(name + ".cleared"), 1)

            def add_square(name, m, local):
                dve.wait_ge(sem(name + ".squared"), local + 1)
                dve.wait_ge(sem(name + ".ss"), local)
                TT(ss[:, :], ss[:, :], wide_of(m), ALU.add).then_inc(sem(name + ".ss"), 1)

            def wide_of(par):
                return wide[par]

            def signal_squares(name, source):
                dve.wait_ge(sem(source + ".ss"), NC)
                dve.sem_inc(sem("norm.squares"), 1)

            clear_ss("mix")
            with dve.Fori(0, 8) as i:
                for par in range(2):
                    pair, m = PAIR0["mix"] + i, 2 * i + par
                    add_ada(ADA0["mix"] + m, m, par)
                    n = add_halves(pair, par, total[par])
                    dve.wait_ge(sem("bank_read"), n)
                    TT(xb(m), xb(m), total[par], ALU.add).then_inc(sem("mix.x"), 1)
                    split_low(pair + 1, par, 0)
                    split_low(pair + 1, par, 1)
                    dve.wait_ge(sem("h_high"), CHUNKS["h2"] + m + 1)
                    dve.wait_ge(sem("mix.x"), m + 1)
                    STT(ob(H, m, 1), xb(m), V("g_mlp", m), ob(H, m, 0).bitcast(F32), ALU.mult, ALU.subtract)\
                        .then_inc(sem("h_ready"), 1)
                    add_square("mix", par, m)
            signal_squares("n2", "mix")
            take_mod(3)
            inverse("n2")

            def ff_group(g, final):
                pair = PAIR0["ff"] + 16 * g
                with dve.Fori(0, 8) as i:
                    for par in range(2):
                        u = 2 * i + par
                        m = 16 * g + u
                        add_ada(ADA0["ff"] + 32 * g + u, u, par)
                        n = add_halves(pair + i, par, total[par])
                        dve.wait_ge(sem("bank_read"), n)
                        STT(wide[par], total[par], 0.0, R[:, :], ALU.max, ALU.mult).then_inc(sem("ff.relu"), 1)
                        split_low(pair + i + 1, par, 0)
                        dve.wait_ge(sem("ff.u_full"), m + 1)
                        TT(ob(U, u, 1), conv[par], ob(U, u, 0).bitcast(F32), ALU.subtract).then_inc(sem("ff.u_ready"), 1)
                        split_low(pair + i + 1, par, 1)
                take_mod(2 * g + 4)
                if final:
                    clear_ss("ff")
                with dve.Fori(0, 8) as i:
                    for par in range(2):
                        u = 2 * i + par
                        m = 16 * g + u
                        add_ada(ADA0["ff"] + 32 * g + 16 + u, u, par)
                        n = add_halves(pair + 8 + i, par, total[par])
                        if not final:
                            split_low(pair + 8 + i + 1, par, 0)
                        dve.wait_ge(sem("bank_read"), n)
                        TT(xb(u), xb(u), total[par], ALU.add).then_inc(sem("ff.x"), 1)
                        if final:
                            split_low(pair + 8 + i + 1, par, 0)
                        split_low(pair + 8 + i + 1, par, 1)
                        if final:
                            add_square("ff", par, u)
                take_mod(2 * g + 5)

            with dve.Fori(0, FF_GROUPS - 1) as g:
                ff_group(g, False)
            ff_group(FF_GROUPS - 1, True)
            signal_squares("n3", "ff")
            dve.wait_ge(sem("rel_made"), 1)
            v.tensor_copy(relrow[:, :], bank[6][0:8, 0:REL_W]).then_inc(sem("relrow_ready"), 1)
            dve.wait_ge(sem("mod_ready"), ADA_GROUPS)
            link(STT(g1[:, :], mod[:, 16:32], 1.0, V("g_mix2", 0, 16), ALU.add, ALU.mult))
            link(STT(g2[:, :], mod[:, 64:80], 1.0, V("g_ffn", 0, 16), ALU.add, ALU.mult))
            dve.wait_ge(sem("ff.x"), FF_GROUPS * NC)

            def modulated(name, gain, shift, chunks, normed):
                inverse(name)
                for k in range(NC + 1):
                    if k < NC:
                        if k >= 4:
                            dve.wait_ge(sem("h_ready"), chunks + k - 3)
                        STT(work(4 + k % 4), xb(k), gain[:, k:k + 1], R[:, :], ALU.mult, ALU.mult)\
                            .then_inc(sem("normed"), 1)
                    if k:
                        j = k - 1
                        dve.wait_ge(sem("h_high"), chunks + j + 1)
                        dve.wait_ge(sem("normed"), normed + j + 1)
                        STT(H[:, j, T:2 * T], work(4 + j % 4), mod[:, shift + j:shift + j + 1], H[:, j, 0:T].bitcast(F32),
                            ALU.add, ALU.subtract).then_inc(sem("h_ready"), 1)

            inverse("n3")
            for k in range(NC):
                STT(xb(k), xb(k), V("g_final", k), R[:, :], ALU.mult, ALU.mult).then_inc(sem("n3.x"), 1)
            dve.wait_ge(sem("n3.x"), NC)
            dve.sem_inc(sem("norm.squares"), 1)
            modulated("n3b", g1, 0, CHUNKS["h3"], 0)
            with dve.Fori(0, 16) as i:
                for par in range(2):
                    pair = PAIR0["in2"] + i
                    dve.wait_ge(sem("halves"), units_with_half(pair, par))
                    TT(zb(2 * i + par), bank[par][:, 0:T], half[par], ALU.add).then_inc(sem("bank_read"), 1)
                    split_low(pair + 1, par, 0)
                    split_low(pair + 1, par, 1)
            dve.wait_ge(sem("bank_read"), 2 + 2 * PAIR0["in2_conv"])
            dve.sem_inc(sem("in2.out"), 32)
            dve.wait_ge(sem("soft.half"), 4)
            y, nabs, l = small[:, 320:352], small[:, 256:288], small[:, 288:320]
            dt, dta = small[:, 352:384], small[:, 384:416]
            for b in range(2):
                s = slice(16 * b, 16 * b + 16)
                link(TT(y[:, s], bank[4][:, 64 * b:64 * b + 16], small[:, 192 + 16 * b:208 + 16 * b], ALU.add))
                link(TT(y[:, s], y[:, s], V("dt_bias", 0, 16), ALU.add))
            STT(nabs, y, -1.0, y, ALU.mult, ALU.min).then_inc(sem("soft.nabs"), 1)
            dve.wait_ge(sem("soft.ln"), 2)
            link(STT(dt, y, 0.0, l, ALU.max, ALU.add))
            dve.wait_ge(sem("a_exp"), 1)
            for b in range(2):
                s = slice(16 * b, 16 * b + 16)
                link(STT(dta[:, s], dt[:, s], -1.0, small[:, 480:496], ALU.mult, ALU.mult))
            dve.wait_ge(sem("relrow_stored"), 16)
            with dve.Fori(0, CONV_CH // 2) as i:
                for par in range(2):
                    pair, m = PAIR0["in2_conv"] + i, 2 * i + par
                    n = add_halves(pair, par, total[par])
                    split_low(pair + 1, par, 0)
                    dve.wait_ge(sem("bank_read"), n)
                    u = total[par]
                    TS(conv[par], u, V("ssm_w", 36 + m), V("ssm_b", m), ALU.mult, ALU.add).then_inc(sem("tap"), 1)
                    for d in range(1, 4):
                        dve.wait_ge(sem("tap"), TAPS["in2_conv"] + 3 * m + d)
                        step = STT(conv[par][:, d:T], u[:, 0:T - d], V("ssm_w", 36 - 12 * d + m), conv[par][:, d:T],
                                   ALU.mult, ALU.add)
                        step.then_inc(sem("tap" if d < 3 else "in2_conv.conv"), 1)
                    split_low(pair + 1, par, 1)
                    dve.wait_ge(sem("in2_conv.sig"), m + 1)
                    dve.wait_ge(sem("in2_conv.conv"), m + 1)
                    TT(zb(32 + m), conv[par], sig[par], ALU.mult).then_inc(sem("in2_conv.out"), 1)
            attention("at2", False, lambda h, par: None, "at2.out")

            dve.wait_ge(sem("cb_ready"), 2)
            cbm = [Z[:, 16:20, :].rearrange("p a t -> p (a t)")[:, 384 * g_:384 * g_ + 384] for g_ in range(2)]
            for grp in range(2):
                TT(cbm[grp], bank[grp][:, 0:384], LEOL, ALU.mult).then_inc(sem("cb_masked"), 1)
            xd = flat(Z[:, 8:16, :])
            for n in range(4):
                b, q = n // 2, n % 2
                dve.wait_ge(sem("xs_turned"), n + 1)
                out = xd[:, 1024 * b + 512 * q:1024 * b + 512 * q + 512].rearrange("p (h d) -> p h d", d=64)
                src = bank[2 + n % 2][:, :].rearrange("p (h d) -> p h d", d=64)
                d_ = dt[:, 16 * b + 8 * q:16 * b + 8 * q + 8]
                TT(out, src, d_.unsqueeze(2).to_broadcast([P, 8, 64]), ALU.mult).then_inc(sem("xdt_ready"), 1)

            def ssm_decay(h):
                decay_operands("ssm", h, dta[:, h:h + 1], dta[:, 16 + h:17 + h])

            ssm_decay(0)
            ssm_decay(1)
            dve.wait_ge(sem("cb_masked"), 2)
            for h in range(SSM_HEADS):
                dve.wait_ge(sem("ssm.exp"), h + 1)
                if h >= 2:
                    dve.wait_ge(sem("ssm.out"), h - 1)
                TT(logit[h % 2], prob[h % 2], cbm[h // 8], ALU.mult).then_inc(sem("ssm.weights"), 1)
                if h + 2 < SSM_HEADS:
                    ssm_decay(h + 2)
                if h % 2 == 0 and h:
                    ssm_y(dve, STT, h // 2 - 1)
            ssm_y(dve, STT, SSM_HEADS // 2 - 1)
            dve.wait_ge(sem("z_sig"), 1)
            link(TT(zb(24, 8), zb(24, 8), adaf, ALU.mult))
            dve.wait_ge(sem("ssm.y"), 8)
            TT(zb(32, 8), zb(32, 8), zb(24, 8), ALU.mult).then_inc(sem("ssm.gated"), 1)

            def block_norm(name, first, n, src, gain, k0, squares):
                v.tensor_reduce(ss[:, :], Z[:, squares:squares + n, :].rearrange("p c t -> p t c"), AX_X, ALU.add)\
                    .then_inc(sem("norm.squares"), 1)
                inverse(name)
                for k in range(k0, k0 + n + 1):
                    if k < k0 + n:
                        if k >= 4:
                            dve.wait_ge(sem("h_ready"), CHUNKS["h4"] + k - 3)
                        STT(work(4 + k % 4), zb(src + k - k0), V(gain, first + k - k0), R[:, :], ALU.mult, ALU.mult)\
                            .then_inc(sem("normed"), 1)
                    if k > k0:
                        j = k - 1
                        dve.wait_ge(sem("h_high"), CHUNKS["h4"] + j + 1)
                        dve.wait_ge(sem("normed"), NC + j + 1)
                        TT(H[:, j, T:2 * T], work(4 + j % 4), H[:, j, 0:T].bitcast(F32), ALU.subtract)\
                            .then_inc(sem("h_ready"), 1)

            dve.wait_ge(sem("at2.squared"), 1)
            block_norm("na", 0, 8, 0, "g_attn", 0, 8)
            dve.wait_ge(sem("ssm.squared"), 1)
            block_norm("ng0", 0, 4, 32, "g_ssm", 8, 16)
            block_norm("ng1", 4, 4, 36, "g_ssm", 12, 20)

            def gated(name, pair, par, m, block, gate, squares, ahead=True):
                dve.wait_ge(sem("halves"), units_with_half(pair, par))
                STT(total[par], bank[par][:, 0:T], mod[:, bass.ds(gate + block, 1)], half[par], ALU.mult, ALU.add)\
                    .then_inc(sem("bank_read"), 1)
                if ahead and not squares:
                    split_low(pair + 1, par, 0)
                dve.wait_ge(sem("bank_read"), 2 + 2 * pair + par + 1)
                TT(xb(block), xb(block), total[par], ALU.add).then_inc(sem(name + ".x"), 1)
                if ahead and squares:
                    split_low(pair + 1, par, 0)
                if ahead:
                    split_low(pair + 1, par, 1)
                if squares:
                    add_square(name, par, block)

            clear_ss("out2")
            with dve.Fori(0, 8) as i:
                for par in range(2):
                    gated("out2", PAIR0["out2"] + i, par, 2 * i + par, 2 * i + par, 32, True)
            signal_squares("n4", "out2")
            dve.wait_ge(sem("out2.x"), NC)
            modulated("n4", g2, 48, CHUNKS["h5"], 2 * NC)

            def ffn_conv(pair, par, m, n):
                dve.wait_ge(sem("bank_read"), n)
                u = total[par]
                TS(conv[par], u, V("ffn_w", 176 + m), V("ffn_b", m), ALU.mult, ALU.add).then_inc(sem("tap"), 1)
                dve.wait_ge(sem("tap"), TAPS["up"] + 2 * m + 1)
                STT(conv[par][:, 1:T], u[:, 0:T - 1], V("ffn_w", 88 + m), conv[par][:, 1:T], ALU.mult, ALU.add)\
                    .then_inc(sem("tap"), 1)
                dve.wait_ge(sem("tap"), TAPS["up"] + 2 * m + 2)
                STT(conv[par][:, 2:T], u[:, 0:T - 2], V("ffn_w", m), conv[par][:, 2:T], ALU.mult, ALU.add)\
                    .then_inc(sem("up.conv"), 1)

            def ffn_group(g, final):
                pair = PAIR0["ffn"] + 19 * g
                with dve.Fori(0, FFN_BLOCKS) as i:
                    j = FFN_BLOCKS * g + i
                    m = 2 * FFN_BLOCKS * g + 2 * i
                    n = add_halves(pair + i, 0, total[0])
                    split_low(pair + i + 1, 0, 0)
                    ffn_conv(pair + i, 0, m, n)
                    split_low(pair + i + 1, 0, 1)
                    dve.wait_ge(sem("up.sig"), j + 1)
                    TT(wide[1], conv[0], sig[0], ALU.mult).then_inc(sem("up.silu"), 1)
                    n = add_halves(pair + i, 1, total[1])
                    ffn_conv(pair + i, 1, m + 1, n)
                    dve.wait_ge(sem("up.silu"), j + 1)
                    dve.wait_ge(sem("up.conv"), m + 2)
                    TT(wide[0], wide[1], conv[1], ALU.mult).then_inc(sem("up.act"), 1)
                    split_low(pair + i + 1, 1, 0)
                    dve.wait_ge(sem("u_high"), FF_GROUPS * FF_BLOCKS + j + 1)
                    TT(ob(U, i, 1), wide[0], ob(U, i, 0).bitcast(F32), ALU.subtract).then_inc(sem("ffn.u_ready"), 1)
                    split_low(pair + i + 1, 1, 1)
                pair = pair + FFN_BLOCKS
                if final:
                    clear_ss("down")
                with dve.Fori(0, 7 if final else 8) as i:
                    for par in range(2):
                        gated("down", pair + i, par, 16 * g + 2 * i + par, 2 * i + par, 80, final)
                if final:
                    for par in range(2):
                        gated("down", pair + 7, par, 16 * g + 14 + par, 14 + par, 80, True, ahead=False)

            with dve.Fori(0, FFN_GROUPS - 1) as g:
                ffn_group(g, False)
            ffn_group(FFN_GROUPS - 1, True)
            signal_squares("n5", "down")
            inverse("n5")
            for m in range(NC):
                STT(zb(m), xb(m), V("g_out", m), R[:, :], ALU.mult, ALU.mult).then_inc(sem("final.out"), 1)

        @block.gpsimd
        def _(pool):
            pool.wait_ge(sem("relrow_ready"), 1)
            pool.dma_start(t["rel_rows"], relrow[:, :]).then_inc(sem("relrow_stored"), 16)
            pool.wait_ge(sem("relrow_stored"), 16)
            pool.wait_ge(sem("in2_conv.out"), CONV_CH)
            for h in range(N_HEADS):
                if h >= 2:
                    pool.wait_ge(sem("at2.scores"), h - 1)
                rows = bass.AP(t["rel_rows"].tensor, h * REL_W, [[1, P], [1, 256]])
                pool.dma_start(relb[h % 2], rows).then_inc(sem("relb_landed%d" % (h % 2)), 16)


def make_constants():
    t_ = np.arange(P)
    ident = np.eye(P)
    le = (t_[:, None] <= t_[None, :]) * 1.0
    gt = (t_[:, None] > t_[None, :]) * 1.0
    one = np.ones((P, P))
    causal = np.where(t_[None, :] <= t_[:, None], 0.0, FAR)
    con = np.concatenate([ident, le, one, le, one, gt, causal, 0 * one, causal, ident[:, ::-1]], 1)
    return np.ascontiguousarray(con.astype(np.float32))


def make_onehot():
    dist = 255 - np.arange(REL_W)
    n = np.maximum(dist, 0)
    exact = REL_BUCKETS // 2
    nf = np.maximum(n, exact).astype(np.float32)
    large = exact + (np.log(nf / np.float32(exact)) / np.float32(np.log(REL_MAX_DIST / exact))
                     * np.float32(REL_BUCKETS - exact)).astype(np.int32)
    bucket = np.where(n < exact, n, np.minimum(large, REL_BUCKETS - 1))
    hot = np.zeros((REL_BUCKETS + 1, REL_W), np.float32)
    on = dist >= 0
    hot[bucket[on], np.arange(REL_W)[on]] = 1.0
    hot[REL_BUCKETS, ~on] = FAR
    return hot


def tiles(w):
    k, n = w.shape
    return np.ascontiguousarray(w.reshape(k // P, P, n // P, P).transpose(2, 1, 0, 3)).reshape(n // P, P, k)


def in_turn(a, b):
    return np.stack([tiles(a), tiles(b)], 1).reshape(-1, P, a.shape[0])


def columns(v):
    return v.reshape(-1, P).T


def layout(a):
    a = {k: np.asarray(v) for k, v in a.items()}
    w_in, w2 = a["w_in"][0], a["w_in_2"][0]
    gates = tiles(w_in[:, 6152:10248]).reshape(2, NC, P, D).transpose(1, 0, 2, 3).reshape(32, P, D)
    cb, cc, cv = w_in[:, 0:1024], w_in[:, 1024:2048], w_in[:, 2048:3072]
    ff1, ff2 = tiles(a["w_ff1"][0]), a["w_ff2"][0].reshape(FF_GROUPS, -1, D)
    up = tiles(a["w_up_2"][0]).reshape(2, FFN // P, P, D).transpose(1, 0, 2, 3).reshape(-1, P, D)
    down = a["w_down_2"][0].reshape(FFN_GROUPS, -1, D)
    by_unit = lambda v: columns(v).reshape(P, 2, FFN // P).transpose(0, 2, 1).reshape(P, -1)
    row = lambda v: np.broadcast_to(v, (P, v.shape[-1]))
    conv2 = a["conv_ffn_w_2"][0]
    vectors = {
        "g_mix": columns(a["g_mix"]), "g_mlp": columns(a["g_mlp"]), "b_gate": columns(a["b_gate"]),
        "conv_w": np.concatenate([columns(a["conv_w"][0, j]) for j in range(3)], 1),
        "b_f": row(a["b_f"]), "g_final": columns(a["g_final"]), "c": columns(a["c_2"]),
        "b_ada": columns(a["b_ada_2"]), "g_mix2": columns(a["norm_mix_g_2"]), "g_attn": columns(a["attn_norm_g_2"]),
        "ssm_w": np.concatenate([columns(a["conv_ssm_w_2"][0, j]) for j in range(4)], 1),
        "ssm_b": columns(a["conv_ssm_b_2"]), "dt_bias": row(a["dt_bias_2"]), "a_log": row(a["a_log_2"]),
        "d_skip": columns(np.repeat(a["d_skip_2"][0], SSM_DIM)), "g_ssm": columns(a["ssm_norm_g_2"]),
        "g_ffn": columns(a["norm_ffn_g_2"]),
        "ffn_w": np.concatenate([by_unit(conv2[j]) for j in range(3)], 1), "ffn_b": by_unit(a["conv_ffn_b_2"]),
        "g_out": columns(a["final_norm_g_2"]),
    }
    by_chunk = lambda w: np.ascontiguousarray(w.reshape(NC, P, -1).transpose(1, 0, 2))
    arrays = {
        "x": by_chunk(a["x"][0].T),
        "vectors": np.concatenate([vectors[n] for n, _ in VEC_SIZES], 1),
        "consts": make_constants(),
        "rel_onehot": make_onehot(),
        "rel_bias": a["rel_bias_2"],
        "w_gate": gates,
        "w_z": np.concatenate([in_turn(cb, cc), tiles(cv), tiles(w_in[:, 5120:6144]),
                               in_turn(w_in[:, 3072:4096], w_in[:, 4096:5120])]),
        "w_f": by_chunk(w_in[:, 6144:6152]),
        "w_branch": np.concatenate([tiles(a["w_conv_out"][0]), tiles(a["w_attn_out"][0])], 2),
        "w_mix": tiles(a["w_mix_out"][0]),
        "w_ff1": ff1,
        "w_ff2": np.concatenate([tiles(g) for g in ff2]),
        "w_ada": a["w_ada_2"][0].reshape(NC, P, ADA_GROUPS, ADA_COLS).transpose(2, 0, 1, 3).reshape(-1, P, ADA_COLS),
        "w_in2": np.concatenate([tiles(w) for w in (w2[:, 0:3072], w2[:, 4096:5120], w2[:, 3072:4096], w2[:, 5120:5632])]),
        "w_dt": by_chunk(w2[:, 5632:5648]),
        "w_out2": tiles(a["w_out_2"][0]),
        "w_up": up,
        "w_down": np.concatenate([tiles(g) for g in down]),
    }
    return {name: np.ascontiguousarray(array) for name, array in arrays.items()}


def kernel(**a):
    import concourse.bacc as bacc
    from concourse.bass_utils import run_bass_kernel_spmd

    arrays = layout(a)
    nc = bacc.Bacc("TRN2", target_bir_lowering=False, num_devices=1)
    t, given = {}, {}
    for name, array in arrays.items():
        given["in_" + name] = array
        t[name] = nc.dram_tensor("in_" + name, array.shape, F32, kind="ExternalInput").ap()
    t["out"] = nc.dram_tensor("out_xT", (P, NC, T), F32, kind="ExternalOutput").ap()
    t["rel_rows"] = nc.dram_tensor("rel_rows", (N_HEADS, REL_W), F32, kind="Internal").ap()
    build(nc, t)
    r = run_bass_kernel_spmd(nc, [given], core_ids=[0])
    out = r.results[0]["out_xT"]
    return np.ascontiguousarray(out.transpose(2, 1, 0)).reshape(1, T, D)
```

```python
from collections import namedtuple
from contextlib import ExitStack

import numpy as np

import concourse.bass as bass
from concourse import mybir
from concourse.alu_op_type import AluOpType as ALU

F32 = mybir.dt.float32
F32R = mybir.dt.float32r
ACT = mybir.ActivationFunctionType
AX_X = mybir.AxisListType.X

P = 128
T = 256
D = 2048
NC = D // P
EPS = 1e-6
FAR = -1e30
N_HEADS = 8
HEAD_SCALE = float(P) ** -0.5
SSM_HEADS = 16
SSM_DIM = 64
FF = 8192
FF_GROUPS = 4
FF_BLOCKS = FF // P // FF_GROUPS
FFN = 5632
FFN_GROUPS = 4
FFN_BLOCKS = FFN // P // FFN_GROUPS
FIRST_CHUNKS = 8
PIECE = FIRST_CHUNKS * P
ADA_COLS = 1024
ADA_GROUPS = 6 * D // ADA_COLS
CONV_CH = 12
REL_BUCKETS, REL_MAX_DIST = 32, 128
REL_W = 384

VEC_SIZES = [("g_mix", 16), ("g_mlp", 16), ("b_gate", 32), ("conv_w", 24), ("b_f", 8), ("g_final", 16),
             ("c", 16), ("b_ada", 96), ("g_mix2", 16), ("g_attn", 8), ("ssm_w", 48), ("ssm_b", 12),
             ("dt_bias", 16), ("a_log", 16), ("d_skip", 8), ("g_ssm", 8), ("g_ffn", 16),
             ("ffn_w", 264), ("ffn_b", 88), ("g_out", 16)]
VEC_AT, _n = {}, 0
for _name, _size in VEC_SIZES:
    VEC_AT[_name] = _n
    _n += _size
VEC_N = _n

IDENT_AT, LEOL_AT, ONEGT_AT, MASK_AT, FLIP_AT, CONST_N = 0, 128, 512, 768, 1152, 1280

GROUP1 = 2 * FF_BLOCKS
GROUP2 = 2 * FFN_BLOCKS + NC
STREAM = [("gate", 16), ("conv_in", 16), ("conv_mul", 8), ("v", 8), ("qk", 16), ("gate2", 16), ("branch", 16), ("mix", 16),
          ("ff", FF_GROUPS * GROUP1), ("in2", 24), ("in2_conv", CONV_CH), ("in2_z", 8), ("out2", 16),
          ("ffn", FFN_GROUPS * GROUP2)]
PAIR0, _n = {}, 0
for _name, _size in STREAM:
    PAIR0[_name] = _n
    _n += _size // 2
ADA0 = {"gate": 0, "conv_in": 16, "qk": 32, "mix": 48, "ff": 64}
NORMS = ["n1", "n2", "n3", "n3b", "na", "ng0", "ng1", "n4", "n5"]
NTH = {_name: _i + 1 for _i, _name in enumerate(NORMS)}
CHUNKS = {"h%d" % (_i + 1): NC * _i for _i in range(5)}
TAPS = {"conv_mul": 0, "in2_conv": 24, "up": 24 + 3 * CONV_CH}
OUT_PARTS = [(0, 4), (4, 4), (8, 4), (12, 2), (14, 2)]
Z_BLOCKS = 44
CREDIT = 4


Tiles = namedtuple("Tiles", "qs vtok prob probT dec0 dec1")


def build(nc, t):
    with ExitStack() as ctx:
        base = (nc.sbuf_base + 31) // 32 * 32
        ctx.enter_context(nc.sbuf_tensor("arena", [P, NC * 2 * T + Z_BLOCKS * T + 8], F32))

        def sb(name, shape, dt=F32):
            return ctx.enter_context(nc.sbuf_tensor(name, shape, dt))

        sems = {}

        def sem(name):
            if name not in sems:
                sems[name] = ctx.enter_context(nc.semaphore(name.replace(".", "_")))
            return sems[name]

        U = nc.alloc_sbuf_tensor_at("U", [P, NC, 2 * T], F32R, offset=base)
        G = nc.alloc_sbuf_tensor_at("G", [P, NC, 2, T], F32, offset=base)
        Z = nc.alloc_sbuf_tensor_at("Z", [P, Z_BLOCKS, T], F32, offset=base + NC * 2 * T * 4)
        B = nc.alloc_sbuf_tensor_at("B", [P, NC, 2 * T], F32R, offset=base + NC * 2 * T * 4)
        X = sb("X", [P, NC, T])
        H = sb("H", [P, NC, 2 * T], F32R)
        w_raw = sb("w_raw", [P, 4, PIECE])
        w_hi = sb("w_hi", [P, 4, PIECE], F32R)
        w_lo = sb("w_lo", [P, 4, PIECE], F32R)
        ada_w = sb("ada_w", [P, 2, ADA_COLS])
        ada_acc = Z[:, 40:44, :].rearrange("p a t -> p (a t)")
        vec = sb("vec", [P, VEC_N])
        con = sb("con", [P, CONST_N])
        ones = sb("ones", [P, P])
        epsb = sb("epsb", [P, 1])
        R = sb("R", [P, T])
        ss = sb("ss", [P, T])
        scratch = sb("scratch", [P, 3072])
        small = sb("small", [P, 496])
        mod = sb("mod", [P, 96])
        g1 = sb("g1", [P, NC])
        g2 = sb("g2", [P, NC])
        silu_c = sb("silu_c", [P, NC])
        wn = sb("wn", [P, NC * 32], F32R)
        wf = wn[:, 0:NC * 16].rearrange("p (k n) -> p k n", k=NC)
        wdt = wn[:, :].rearrange("p (k n) -> p k n", k=NC)
        wf_raw = scratch[:, 2816:2944].rearrange("p (k n) -> p k n", k=NC)
        wdt_raw = scratch[:, 2560:2816].rearrange("p (k n) -> p k n", k=NC)
        rel = sb("rel", [REL_BUCKETS + 1, 8])
        relhot = Z[0:REL_BUCKETS + 1, 36:38, :].rearrange("p a t -> p (a t)")[:, 0:REL_W]
        relrow = Z[0:8, 38:40, :].rearrange("p a t -> p (a t)")[:, 0:REL_W]

        bank = [ctx.enter_context(nc.psum_tensor(f"bank{i}", [P, 512], F32)) for i in range(8)]

        std = bank[4][:, T:2 * T]
        ident = con[:, IDENT_AT:IDENT_AT + P]
        LEOL = con[:, LEOL_AT:LEOL_AT + 384]
        LEO, LE = LEOL[:, 0:256], LEOL[:, 0:128]
        ONEGT = con[:, ONEGT_AT:ONEGT_AT + 256]
        GT = ONEGT[:, 128:256]
        MASK = con[:, MASK_AT:MASK_AT + 384]
        flip = con[:, FLIP_AT:FLIP_AT + P]

        def V(name, i=0, n=1):
            return vec[:, bass.ds(VEC_AT[name] + i, n)]

        def work(i):
            return scratch[:, i * T:(i + 1) * T]

        half = [work(0), work(1)]
        total = [work(2), work(3)]
        gate_total = [work(2), work(6)]
        wide = [work(4), work(5)]
        conv = [work(6), work(7)]
        half2 = [work(8), work(9)]
        sig = [work(10), work(11)]

        adaf = ada_w[:, :, :].rearrange("p a b -> p (a b)")

        def pair_at(area, col, size):
            return [area[:, col:col + size], area[:, col + size:col + 2 * size]]

        at1 = Tiles(qs=pair_at(adaf, 768, T), vtok=pair_at(adaf, 1280, T), prob=pair_at(scratch, 2048, 384),
                    probT=pair_at(scratch, 768, 384), dec0=pair_at(adaf, 0, 256), dec1=pair_at(adaf, 512, 128))
        idle = G[:, :, :, :].rearrange("p a b t -> p (a b t)")
        at2 = Tiles(qs=pair_at(idle, 0, T), vtok=pair_at(idle, 512, T), prob=pair_at(idle, 1024, 384),
                    probT=pair_at(idle, 1792, 384), dec0=pair_at(idle, 2560, 256), dec1=pair_at(idle, 3072, 128))
        relb = pair_at(idle, 3328, T)
        ssm_w = pair_at(idle, 3840, 384)
        cbm = pair_at(idle, 4608, 384)
        xd = idle[:, 5376:7424]
        R2 = work(8)
        R_squared = work(9)
        ssg = work(9)

        def flat(ap):
            return ap.rearrange("p a t -> p (a t)")

        def zb(i, n=1):
            return flat(Z[:, bass.ds(i, n), :])

        def xb(i, n=1):
            return flat(X[:, bass.ds(i, n), :])

        def ob(buf, i, part):
            return flat(buf[:, bass.ds(i, 1), part * T:(part + 1) * T])

        block = ctx.enter_context(nc.Block())

        def piece(sp, pair, s, tiles, tile_pair, first=False):
            if not first:
                sp.wait_ge(sem("w_split"), 4 * pair + s + 1)
            cols = tiles.shape[2]
            lo, up = (0, PIECE) if s % 2 == 0 else (PIECE, cols)
            if cols < 2 * PIECE:
                cut = (cols // P + 1) // 2 * P
                lo, up = (0, cut) if s % 2 == 0 else (cut, cols)
            src = tiles[bass.ds(2 * tile_pair + s // 2, 1), :, lo:up].rearrange("a p c -> (a p) c")
            sp.dma_start(w_raw[:, s, 0:up - lo], src).then_inc(sem("w_landed%d" % s), 16)

        def stream(sp, pair0, pairs, tiles, tile_pair0):
            with sp.Fori(0, pairs) as i:
                for s in range(4):
                    piece(sp, pair0 + i, s, tiles, tile_pair0 + i)

        def cast_high0(act, A, slot):
            act.wait_ge(sem("w_landed%d" % slot), 16)
            A(w_hi[:, slot, :], w_raw[:, slot, :], ACT.Copy).then_inc(sem("w_high"), 1)

        def ssm_y(dve, STT, j):
            dve.wait_ge(sem("ssm.out"), 2 * j + 2)
            STT(zb(32 + j), zb(32 + j), V("d_skip", j), bank[6 + j % 2][:, 0:256], ALU.mult, ALU.add)\
                .then_inc(sem("ssm.y"), 1)

        @block.sync
        def _(sp):
            for i in range(4):
                sp.dma_start(X[:, 4 * i:4 * i + 4, :], t["x"][:, 4 * i:4 * i + 4, :]).then_inc(sem("x_landed%d" % i), 16)
                if i == 0:
                    sp.dma_start(vec[:, :], t["vectors"]).then_inc(sem("vec_landed"), 16)
                if i < 2:
                    piece(sp, 0, i, t["w_gate"], 0, first=True)
            for s in (2, 3):
                piece(sp, 0, s, t["w_gate"], 0, first=True)
            sp.dma_start(wf_raw[:, :, :], t["w_f"]).then_inc(sem("wf_landed"), 16)
            sp.dma_start(con[:, :], t["consts"]).then_inc(sem("con_landed"), 16)
            sp.dma_start(wdt_raw[:, :, :], t["w_dt"]).then_inc(sem("wdt_landed"), 16)
            sp.dma_start(rel[0:REL_BUCKETS, :], t["rel_bias"]).then_inc(sem("con_landed"), 16)
            stream(sp, PAIR0["gate"] + 1, 7, t["w_gate"], 1)
            stream(sp, PAIR0["conv_in"], PAIR0["gate2"] - PAIR0["conv_in"], t["w_z"], 0)
            stream(sp, PAIR0["gate2"], 8, t["w_gate"], 8)
            stream(sp, PAIR0["branch"], 8, t["w_branch"], 0)
            stream(sp, PAIR0["mix"], 8, t["w_mix"], 0)
            sp.wait_ge(sem("branch.operand"), 8 + N_HEADS)
            sp.dma_start(relhot, t["rel_onehot"]).then_inc(sem("hot_landed"), 16)
            with sp.Fori(0, FF_GROUPS) as g:
                stream(sp, PAIR0["ff"] + 16 * g, 8, t["w_ff1"], 8 * g)
                stream(sp, PAIR0["ff"] + 16 * g + 8, 8, t["w_ff2"], 8 * g)
            stream(sp, PAIR0["in2"], PAIR0["out2"] - PAIR0["in2"], t["w_in2"], 0)
            stream(sp, PAIR0["out2"], 8, t["w_out2"], 0)
            with sp.Fori(0, FFN_GROUPS) as g:
                stream(sp, PAIR0["ffn"] + 19 * g, 11, t["w_up"], 11 * g)
                stream(sp, PAIR0["ffn"] + 19 * g + 11, 8, t["w_down"], 8 * g)
            for n, (m, size) in enumerate(OUT_PARTS):
                sp.wait_ge(sem("final.out"), n + 1)
                sp.dma_start(t["out"][:, m:m + size, :], Z[:, m:m + size, :]).then_inc(sem("out_stored"), 16)
            sp.wait_ge(sem("out_stored"), 16 * len(OUT_PARTS))

        @block.tensor
        def _(pe):
            def mm(out, lhsT, rhs, start, stop):
                return nc.tensor.matmul(out, lhsT, rhs, start=start, stop=stop, skip_group_check=True)

            def unit(pair, par, buf, chunks, operand=None, operand_base=0, two_banks=False, between=None):
                cut = FIRST_CHUNKS if chunks == NC else (chunks + 1) // 2
                pe.wait_ge(sem("bank_read"), 2 * pair + par + 1)
                for h, (k0, n) in enumerate(((0, cut), (cut, chunks - cut))):
                    if h and between:
                        between()
                    pe.wait_ge(sem("w_split"), CREDIT + 4 * pair + 2 * par + h + 1)
                    dst = bank[2 * h + par] if two_banks else bank[par]
                    for c in range(n):
                        if par == 0 and operand and c % 2 == 0:
                            pe.wait_ge(sem(operand), operand_base + k0 + min(c + 2, n))
                        lhs = slice(c * P, (c + 1) * P)
                        start = c == 0 and (h == 0 or two_banks)
                        stop = c == n - 1 and (h == 1 or two_banks)
                        mm(dst[:, :], w_hi[:, 2 * par + h, lhs], buf[:, k0 + c, :], start, False)
                        end = mm(dst[:, T:2 * T], w_lo[:, 2 * par + h, lhs], buf[:, k0 + c, 0:T], False, stop)
                    end.then_inc(sem("piece_used"), 1)

            def pair_of_units(pair, *args, **kwargs):
                for par in range(2):
                    unit(pair, par, *args, **kwargs)

            def ada_reduce(group):
                pe.wait_ge(sem("ada_acc"), 1 + 16 * group + 16)
                pe.wait_ge(sem("mod_ready"), group)
                for b in range(ADA_COLS // P):
                    last = mm(bank[5][:, b:b + 1], ada_acc[:, b * P:(b + 1) * P], ones[:, 0:1], b == 0, True)
                last.then_inc(sem("ada_reduced"), 1)

            def sum_squares(name):
                pe.wait_ge(sem("norm.squares"), NTH[name])
                if NTH[name] > 1 and name != "n3b":
                    pe.wait_ge(sem("norm.root"), NTH[name] - 1)
                out, squares = (bank[7], ssg) if name == "n3b" else (bank[4], ss[:, :])
                mm(out[:, 0:T], ones[:, :], squares, True, True).then_inc(sem("norm.summed"), 1)

            pair_of_units(PAIR0["gate"], H, NC, "h_ready", CHUNKS["h1"])
            pe.wait_ge(sem("ones_ready"), 1)
            sum_squares("n1")
            for b in range(2):
                last = mm(bank[6][:, b:b + 1], ss[:, b * P:(b + 1) * P], ones[:, 0:1], b == 0, True)
            last.then_inc(sem("n1.tok"), 1)
            with pe.Fori(1, 8) as i:
                pair_of_units(PAIR0["gate"] + i, H, NC)
            ada_reduce(0)
            pe.wait_ge(sem("wn_split"), 1)
            for b in range(2):
                for k in range(NC):
                    toks = slice(b * P, (b + 1) * P)
                    mm(bank[4][:, 32 * b:32 * b + 16], H[:, k, toks], wf[:, k, :], b == 0 and k == 0, False)
                    last = mm(bank[4][:, 32 * b:32 * b + 8], H[:, k, T + b * P:T + (b + 1) * P], wf[:, k, 0:8],
                              False, k == NC - 1)
            last.then_inc(sem("soft.logits"), 1)
            with pe.Fori(0, 8) as i:
                pair_of_units(PAIR0["conv_in"] + i, H, NC)
            ada_reduce(1)
            with pe.Fori(0, 8) as i:
                pair_of_units(PAIR0["conv_mul"] + i, H, NC)
            with pe.Fori(0, 8) as i:
                pair_of_units(PAIR0["qk"] + i, H, NC)
            ada_reduce(2)

            def attention(name, tl, k_step, k0, v0, decay, fill, out_sem, out0):
                def scores(h):
                    s = bank[2 + h % 2]
                    pe.wait_ge(sem(name + ".q_scaled"), h + 1)
                    if h >= 2:
                        pe.wait_ge(sem(name + ".exps"), 2 * h - 2)
                    q, k = tl.qs[h % 2], zb(k0 + k_step * h)
                    mm(s[:, 0:128], q[:, 0:128], k[:, 0:128], True, False)
                    mm(s[:, 128:384], q[:, 128:256], k, False, False)
                    if decay:
                        pe.wait_ge(sem(name + ".decay_ready"), 2 * h + 2)
                        mm(s[:, 0:128], tl.dec0[h % 2][:, 0:128], GT, False, False)
                        mm(s[:, 128:256], tl.dec0[h % 2][:, 128:256], GT, False, False)
                        mm(s[:, 128:384], tl.dec1[h % 2], ONEGT, False, False)
                        last = mm(s[:, 0:384], ident, MASK, False, True)
                    else:
                        pe.wait_ge(sem("relb_landed%d" % (h % 2)), 16 * (h // 2 + 1))
                        mm(s[:, 0:128], flip, relb[h % 2][:, 128:256], False, False)
                        last = mm(s[:, 128:384], flip, relb[h % 2], False, True)
                    last.then_inc(sem(name + ".scores"), 1)
                    v = zb(v0 + h)
                    if h >= 2:
                        pe.wait_ge(sem(name + ".v_copied"), h - 1)
                    for b in range(2):
                        last = nc.tensor.transpose(bank[4 + h % 2][:, b * P:(b + 1) * P], v[:, b * P:(b + 1) * P], ident)
                    last.then_inc(sem(name + ".v_turned"), 1)

                def turn_probs(h):
                    pe.wait_ge(sem(name + ".probs"), 2 * h + 2)
                    if h:
                        pe.wait_ge(sem(name + ".p_copied"), h)
                    for b in range(3):
                        last = nc.tensor.transpose(bank[6][:, b * P:(b + 1) * P], tl.prob[h % 2][:, b * P:(b + 1) * P], ident)
                    last.then_inc(sem(name + ".p_turned"), 1)

                def mix(h):
                    pe.wait_ge(sem(name + ".v_copied"), h + 1)
                    pe.wait_ge(sem(name + ".p_copied"), h + 1)
                    if h:
                        pe.wait_ge(sem(out_sem), out0 + h)
                    mm(bank[7][:, 0:256], tl.vtok[h % 2][:, 0:128], tl.probT[h % 2][:, 0:256], True, False)
                    mm(bank[7][:, 128:256], tl.vtok[h % 2][:, 128:256], tl.probT[h % 2][:, 256:384], False, True)\
                        .then_inc(sem(name + ".mixed"), 1)

                scores(0)
                for h in range(N_HEADS):
                    fill(h, 0)
                    if h + 1 < N_HEADS:
                        scores(h + 1)
                    turn_probs(h)
                    fill(h, 1)
                    mix(h)

            pe.wait_ge(sem("con_landed"), 32)
            attention("at1", at1, 2, 17, 32, True, lambda h, par: unit(PAIR0["gate2"] + h, par, H, NC), "branch.operand", 8)
            pair_of_units(PAIR0["branch"], B, NC, "branch.operand", two_banks=True)
            with pe.Fori(1, 8) as i:
                pair_of_units(PAIR0["branch"] + i, B, NC, two_banks=True)
            with pe.Fori(0, 8) as i:
                pair_of_units(PAIR0["mix"] + i, U, NC, "merged")
            ada_reduce(3)
            unit(PAIR0["ff"], 0, H, NC, "h_ready", CHUNKS["h2"])
            sum_squares("n2")
            unit(PAIR0["ff"], 1, H, NC)

            def ff1(g, first=0):
                with pe.Fori(first, 8) as i:
                    pair_of_units(PAIR0["ff"] + 16 * g + i, H, NC)

            def ff2(g):
                ada_reduce(2 * g + 4)
                with pe.Fori(0, 8) as i:
                    pair_of_units(PAIR0["ff"] + 16 * g + 8 + i, U, NC, "ff.u_ready", 16 * g)
                ada_reduce(2 * g + 5)

            ff1(0, 1)
            with pe.Fori(0, FF_GROUPS - 1) as g:
                ff2(g)
                ff1(g + 1)
            ff2(FF_GROUPS - 1)
            pe.wait_ge(sem("hot_landed"), 16)
            pe.wait_ge(sem("con_landed"), 32)
            pe.wait_ge(sem("rel_ones"), 1)
            mm(bank[6][0:8, 0:REL_W], rel[:, :], relhot, True, True).then_inc(sem("rel_made"), 1)
            sum_squares("n3")
            sum_squares("n3b")
            with pe.Fori(0, 6) as i:
                pair_of_units(PAIR0["in2"] + i, H, NC, "h_ready", CHUNKS["h3"])
            pe.wait_ge(sem("wn_split"), 2)
            for b in range(2):
                for k in range(NC):
                    toks = slice(b * P, (b + 1) * P)
                    mm(bank[4][:, 64 * b:64 * b + 32], H[:, k, toks], wdt[:, k, :], b == 0 and k == 0, False)
                    last = mm(bank[4][:, 64 * b:64 * b + 16], H[:, k, T + b * P:T + (b + 1) * P], wdt[:, k, 0:16],
                              False, k == NC - 1)
            last.then_inc(sem("soft.logits"), 1)
            with pe.Fori(6, 12) as i:
                pair_of_units(PAIR0["in2"] + i, H, NC)
            attention("at2", at2, 1, 8, 16, False, lambda h, par: unit(PAIR0["in2_conv"] + h, par, H, NC), "at2.out", 0)

            def z_unit(u):
                unit(PAIR0["in2_z"] + u // 2, u % 2, H, NC)

            pe.wait_ge(sem("in2_conv.out"), CONV_CH)
            for grp in range(2):
                b_, c_ = zb(40 + grp), zb(42 + grp)
                mm(bank[2 + grp][:, 0:256], b_[:, 0:128], c_, True, False)
                mm(bank[2 + grp][:, 256:384], b_[:, 128:256], c_[:, 128:256], False, True).then_inc(sem("cb_ready"), 1)
            for n in range(4):
                b, q = n // 2, n % 2
                if n == 2:
                    z_unit(4)
                if n >= 2:
                    pe.wait_ge(sem("xdt_ready"), n - 1)
                for j in range(4):
                    last = nc.tensor.transpose(bank[4 + n % 2][:, j * P:(j + 1) * P],
                                               zb(32 + 4 * q + j)[:, b * P:(b + 1) * P], ident)
                last.then_inc(sem("xs_turned"), 1)

            def decays(h):
                pe.wait_ge(sem("ssm.decay_ready"), 2 * h + 2)
                if h >= 2:
                    pe.wait_ge(sem("ssm.exp"), h - 1)
                else:
                    pe.wait_ge(sem("cb_masked"), 2)
                s = bank[2 + h % 2]
                mm(s[:, 0:256], GT, at2.dec0[h % 2], True, False)
                mm(s[:, 128:256], ones[:, :], at2.dec1[h % 2], False, False)
                mm(s[:, 256:384], GT, at2.dec1[h % 2], False, True).then_inc(sem("ssm.decays"), 1)

            def outputs(h):
                j, rows = h // 2, 64 * (h % 2)
                pe.wait_ge(sem("ssm.weights"), h + 1)
                if h % 2 == 0 and j >= 2:
                    pe.wait_ge(sem("ssm.y"), j - 1)
                o = bank[6 + j % 2][rows:rows + 64, 0:256]
                o2 = bank[6 + j % 2][rows:rows + 64, 128:256]
                w = ssm_w[h % 2]
                mm(o, xd[:, h * 64:(h + 1) * 64], w[:, 0:256], True, False)
                mm(o2, xd[:, 1024 + h * 64:1024 + (h + 1) * 64], w[:, 256:384], False, True).then_inc(sem("ssm.out"), 1)

            decays(0)
            pe.wait_ge(sem("xdt_ready"), 4)
            sum_squares("na")
            for h in range(SSM_HEADS):
                if h + 1 < SSM_HEADS:
                    decays(h + 1)
                if h in (0, 2, 4):
                    z_unit(5 + h // 2)
                outputs(h)
                if h == 11:
                    sum_squares("ng0")
            unit(PAIR0["out2"], 0, H, NC, "h_ready", CHUNKS["h4"], between=lambda: sum_squares("ng1"))
            unit(PAIR0["out2"], 1, H, NC)
            with pe.Fori(1, 8) as i:
                pair_of_units(PAIR0["out2"] + i, H, NC)
            sum_squares("n4")

            def ffn_group(g):
                pair = PAIR0["ffn"] + 19 * g
                with pe.Fori(0, FFN_BLOCKS) as i:
                    pair_of_units(pair + i, H, NC, "h_ready", CHUNKS["h5"])
                with pe.Fori(0, 8) as i:
                    pair_of_units(pair + FFN_BLOCKS + i, U, FFN_BLOCKS, "ffn.u_ready", FFN_BLOCKS * g)

            with pe.Fori(0, FFN_GROUPS - 1) as g:
                ffn_group(g)
            ffn_group(FFN_GROUPS - 1)
            sum_squares("n5")

        @block.scalar
        def _(act):
            A = nc.scalar.activation

            def cast_high(pair, par, h):
                slot = 2 * par + h
                act.wait_ge(sem("w_landed%d" % slot), 16 * pair + 16)
                act.wait_ge(sem("piece_used"), 4 * pair + slot + 1)
                A(w_hi[:, slot, :], w_raw[:, slot, :], ACT.Copy).then_inc(sem("w_high"), 1)

            def load_sigmoid():
                A(small[:, 16:17], V("c"), ACT.Sigmoid)

            def load_ada(chunk, slot):
                act.wait_ge(sem("ada_acc"), chunk)
                act.dma_start(ada_w[:, slot, :], t["w_ada"][bass.ds(chunk, 1)].rearrange("a p c -> (a p) c"))\
                    .then_inc(sem("ada_landed%d" % slot), 16)

            def take_half(pair, par, scale=1.0):
                act.wait_ge(sem("piece_used"), CREDIT + 4 * pair + 2 * par + 2)
                A(half[par], bank[par][:, T:2 * T], ACT.Copy, scale=scale).then_inc(sem("halves"), 1)

            def root(name, count=D, src=bank[4]):
                act.wait_ge(sem("norm.summed"), NTH[name])
                if NTH[name] > 1:
                    act.wait_ge(sem("norm.inverse"), NTH[name] - 1)
                A(std, src[:, 0:T], ACT.Sqrt, bias=epsb[:, :], scale=1.0 / count).then_inc(sem("norm.root"), 1)

            act.wait_ge(sem("vec_landed"), 16)
            def first_chunks(i):
                act.wait_ge(sem("x_landed%d" % i), 16)
                for k in range(4 * i, 4 * i + 4):
                    A(H[:, k, 0:T], X[:, k, :], ACT.Copy, scale=V("g_mix", k)).then_inc(sem("h_high"), 1)

            for i in range(4):
                first_chunks(i)
                if i < 2:
                    cast_high0(act, A, i)
            cast_high0(act, A, 2)
            cast_high0(act, A, 3)
            for i in range(4):
                A(zb(4 * i, 4), xb(4 * i, 4), ACT.Square).then_inc(sem("x_squares"), 1)
            A(small[:, 16:32], V("c", 0, 16), ACT.Sigmoid).then_inc(sem("c_sig"), 1)
            act.wait_ge(sem("ada_credit"), 1)
            load_ada(0, 0)
            load_ada(1, 1)

            def plain(pair, par, chunk=None, ahead=True):
                take_half(pair, par)
                cast_high(pair + 1, par, 0)
                cast_high(pair + 1, par, 1)
                if chunk is not None and ahead:
                    load_ada(chunk + 2, par)

            for par in range(2):
                plain(PAIR0["gate"], par)
            root("n1")
            act.wait_ge(sem("n1.tok"), 1)
            A(small[:, 0:2], bank[6][:, 0:2], ACT.Sqrt, bias=epsb[:, :], scale=1.0 / D).then_inc(sem("n1.stdtok"), 1)
            act.wait_ge(sem("wf_landed"), 16)
            A(wf[:, :, 0:8], wf_raw, ACT.Copy).then_inc(sem("wn_high"), 1)
            for par in range(2):
                load_ada(ADA0["gate"] + 2 + par, par)
            with act.Fori(1, 8) as i:
                for par in range(2):
                    plain(PAIR0["gate"] + i, par, ADA0["gate"] + 2 * i + par)
            act.wait_ge(sem("soft.logits"), 1)
            for b in range(2):
                A(small[:, 32 + 8 * b:40 + 8 * b], bank[4][:, 32 * b + 8:32 * b + 16], ACT.Copy).then_inc(sem("soft.half"), 1)
            act.wait_ge(sem("soft.nabs"), 1)
            A(small[:, 64:80], small[:, 80:96], ACT.Exp).then_inc(sem("soft.exp"), 1)
            act.wait_ge(sem("soft.exp"), 1)
            A(small[:, 96:112], small[:, 64:80], ACT.Ln, bias=1.0).then_inc(sem("soft.ln"), 1)
            act.wait_ge(sem("wdt_landed"), 16)
            A(wdt[:, :, 0:16], wdt_raw, ACT.Copy).then_inc(sem("wn_high"), 1)
            with act.Fori(0, 8) as i:
                for par in range(2):
                    plain(PAIR0["conv_in"] + i, par, ADA0["conv_in"] + 2 * i + par)
            with act.Fori(0, 4) as i:
                for par in range(2):
                    plain(PAIR0["conv_mul"] + i, par)
                    act.wait_ge(sem("conv_mul.y"), 2 * i + par + 1)
                    act.sem_inc(sem("wait_over"), 1)
                    A(ob(B, 2 * i + par, 0), wide[par], ACT.Copy).then_inc(sem("conv_mul.high"), 1)
            with act.Fori(0, 4) as i:
                for par in range(2):
                    plain(PAIR0["v"] + i, par)
            with act.Fori(0, 7) as i:
                for par in range(2):
                    plain(PAIR0["qk"] + i, par, ADA0["qk"] + 2 * i + par)
            for par in range(2):
                plain(PAIR0["qk"] + 7, par, ADA0["qk"] + 14 + par, ahead=False)

            def attention(name, tl, q0, q_step, out_high, fill):
                def scale_q(h):
                    if h >= 2:
                        act.wait_ge(sem(name + ".scores"), h - 1)
                    A(tl.qs[h % 2], zb(q0 + q_step * h), ACT.Copy, scale=HEAD_SCALE).then_inc(sem(name + ".q_scaled"), 1)

                def copy_values(h):
                    act.wait_ge(sem(name + ".v_turned"), h + 1)
                    if h >= 2:
                        act.wait_ge(sem(name + ".mixed"), h - 1)
                    A(tl.vtok[h % 2], bank[4 + h % 2][:, 0:256], ACT.Copy).then_inc(sem(name + ".v_copied"), 1)

                def exps(h):
                    act.wait_ge(sem(name + ".maxes"), 2 * h + 2)
                    if h >= 2:
                        act.wait_ge(sem(name + ".p_turned"), h - 1)
                    for b, (lo, up) in enumerate(((0, 128), (128, 384))):
                        c = 128 + 2 * h + b
                        A(tl.prob[h % 2][:, lo:up], bank[2 + h % 2][:, lo:up], ACT.Exp, bias=small[:, c:c + 1],
                          accum_out=small[:, c + 16:c + 17]).then_inc(sem(name + ".exps"), 1)

                def copy_probs(h):
                    act.wait_ge(sem(name + ".p_turned"), h + 1)
                    if h >= 2:
                        act.wait_ge(sem(name + ".mixed"), h - 1)
                    A(tl.probT[h % 2], bank[6][:, 0:384], ACT.Copy).then_inc(sem(name + ".p_copied"), 1)

                def high(h):
                    act.wait_ge(sem(name + ".mixed"), h + 1)
                    if out_high:
                        A(ob(B, 8 + h, 0), bank[7][:, 0:256], ACT.Copy).then_inc(sem(name + ".high"), 1)
                    else:
                        A(zb(8 + h), bank[7][:, 0:256], ACT.Square).then_inc(sem(name + ".squared"), 1)

                scale_q(0)
                copy_values(0)
                exps(0)
                for h in range(N_HEADS):
                    if h + 1 < N_HEADS:
                        scale_q(h + 1)
                    if h:
                        high(h - 1)
                    fill(h, 0)
                    if h + 1 < N_HEADS:
                        copy_values(h + 1)
                    copy_probs(h)
                    if h + 1 < N_HEADS:
                        exps(h + 1)
                    fill(h, 1)
                high(N_HEADS - 1)

            act.wait_ge(sem("qk.out"), 16)
            act.wait_ge(sem("v.out"), 8)
            attention("at1", at1, 16, 2, True, lambda h, par: plain(PAIR0["gate2"] + h, par))
            load_ada(ADA0["mix"], 0)
            load_ada(ADA0["mix"] + 1, 1)
            load_sigmoid()

            with act.Fori(0, 8) as i:
                for par in range(2):
                    pair, m = PAIR0["branch"] + i, 2 * i + par
                    act.wait_ge(sem("branch.gated"), 2 * m + 2)
                    A(sig[par], flat(G[:, bass.ds(m, 1), 0, :]), ACT.Sigmoid, bias=V("b_gate", m)).then_inc(sem("gates_open"), 1)
                    A(wide[par], flat(G[:, bass.ds(m, 1), 1, :]), ACT.Sigmoid, bias=V("b_gate", 16 + m)).then_inc(sem("gates_open"), 1)
                    act.wait_ge(sem("piece_used"), CREDIT + 4 * pair + 2 * par + 2)
                    A(half[par], bank[par][:, T:2 * T], ACT.Copy).then_inc(sem("halves_b"), 1)
                    A(half2[par], bank[2 + par][:, T:2 * T], ACT.Copy).then_inc(sem("halves_b"), 1)
                    cast_high(pair + 1, par, 0)
                    cast_high(pair + 1, par, 1)
                    act.wait_ge(sem("merge"), m + 1)
                    act.sem_inc(sem("wait_over"), 1)
                    A(ob(U, m, 0), conv[par], ACT.Copy).then_inc(sem("merged_high"), 1)
            with act.Fori(0, 8) as i:
                for par in range(2):
                    pair, m = PAIR0["mix"] + i, 2 * i + par
                    take_half(pair, par)
                    cast_high(pair + 1, par, 0)
                    cast_high(pair + 1, par, 1)
                    act.wait_ge(sem("mix.x"), m + 1)
                    A(ob(H, m, 0), xb(m), ACT.Copy, scale=V("g_mlp", m)).then_inc(sem("h_high"), 1)
                    A(wide[par], xb(m), ACT.Square).then_inc(sem("mix.squared"), 1)
                    load_ada(ADA0["mix"] + m + 2, par)
            root("n2")

            def ff1_unit(pair, par, m, u, chunk):
                take_half(pair, par)
                cast_high(pair + 1, par, 0)
                act.wait_ge(sem("ff.relu"), m + 1)
                A(ob(U, u, 0), wide[par], ACT.Square).then_inc(sem("u_high"), 1)
                A(conv[par], wide[par], ACT.Square).then_inc(sem("ff.u_full"), 1)
                cast_high(pair + 1, par, 1)
                load_ada(chunk + 2, par)

            def ff2_unit(pair, par, m, block, chunk, squares=False):
                take_half(pair, par)
                cast_high(pair + 1, par, 0)
                cast_high(pair + 1, par, 1)
                if squares:
                    act.wait_ge(sem("ff.x"), m + 1)
                    A(wide[par], xb(block), ACT.Square).then_inc(sem("ff.squared"), 1)
                    A(conv[par], xb(block), ACT.Square, scale=V("g_final", block)).then_inc(sem("ff.squared_g"), 1)
                if chunk is not None:
                    load_ada(chunk + 2, par)

            def ff_group(g, final):
                pair = PAIR0["ff"] + 16 * g
                with act.Fori(0, 8) as i:
                    for par in range(2):
                        ff1_unit(pair + i, par, 16 * g + 2 * i + par, 2 * i + par, ADA0["ff"] + 32 * g + 2 * i + par)
                with act.Fori(0, 7 if final else 8) as i:
                    for par in range(2):
                        ff2_unit(pair + 8 + i, par, 16 * g + 2 * i + par, 2 * i + par, ADA0["ff"] + 32 * g + 16 + 2 * i + par, final)
                if final:
                    for par in range(2):
                        ff2_unit(pair + 15, par, 16 * g + 14 + par, 14 + par, None, True)

            with act.Fori(0, FF_GROUPS - 1) as g:
                ff_group(g, False)
            ff_group(FF_GROUPS - 1, True)
            root("n3")
            act.wait_ge(sem("n3.inverted"), 2)
            A(std, work(0), ACT.Sqrt, bias=epsb[:, :], scale=1.0 / D).then_inc(sem("norm.root"), 1)
            for k in range(NC):
                act.wait_ge(sem("normed"), k + 1)
                A(H[:, k, 0:T], work(4 + k % 4), ACT.Identity, bias=mod[:, k:k + 1]).then_inc(sem("h_high"), 1)
            with act.Fori(0, 6) as i:
                for par in range(2):
                    plain(PAIR0["in2"] + i, par)
            act.wait_ge(sem("soft.logits"), 2)
            for b in range(2):
                A(small[:, 192 + 16 * b:208 + 16 * b], bank[4][:, 64 * b + 16:64 * b + 32], ACT.Copy).then_inc(sem("soft.half"), 1)
            A(small[:, 480:496], V("a_log", 0, 16), ACT.Exp).then_inc(sem("a_exp"), 1)
            act.wait_ge(sem("soft.nabs"), 2)
            A(small[:, 224:256], small[:, 256:288], ACT.Exp).then_inc(sem("soft.exp"), 1)
            act.wait_ge(sem("soft.exp"), 2)
            A(small[:, 288:320], small[:, 224:256], ACT.Ln, bias=1.0).then_inc(sem("soft.ln"), 1)
            with act.Fori(6, 12) as i:
                for par in range(2):
                    plain(PAIR0["in2"] + i, par)

            def second_fill(h, par):
                plain(PAIR0["in2_conv"] + h, par)
                m = 2 * h + par
                if m < CONV_CH:
                    act.wait_ge(sem("in2_conv.conv"), m + 1)
                    A(sig[par], conv[par], ACT.Sigmoid).then_inc(sem("in2_conv.sig"), 1)

            def z_sigmoid(grp):
                act.wait_ge(sem("bank_read"), 2 + 2 * PAIR0["in2_z"] + 4 * grp + 4)
                A(adaf[:, 1024 * grp:1024 * grp + 1024], zb(24 + 4 * grp, 4), ACT.Sigmoid).then_inc(sem("z_sig"), 1)

            def norm_high(k):
                act.wait_ge(sem("normed"), NC + k + 1)
                A(H[:, k, 0:T], work(4 + k % 4), ACT.Copy).then_inc(sem("h_high"), 1)

            def ssm_squares(grp):
                act.wait_ge(sem("ssm.gated"), 4 * grp + 4)
                A(zb(16 + 4 * grp, 4), zb(32 + 4 * grp, 4), ACT.Square).then_inc(sem("ssm.squared"), 1)

            act.wait_ge(sem("in2.out"), 24)
            attention("at2", at2, 0, 1, False, second_fill)
            z_sigmoid(0)
            plain(PAIR0["in2_z"] + 2, 0)
            root("na", 1024)
            for h in range(SSM_HEADS):
                act.wait_ge(sem("ssm.decays"), h + 1)
                if h >= 2:
                    act.wait_ge(sem("ssm.weights"), h - 1)
                A(at2.prob[h % 2], bank[2 + h % 2][:, 0:384], ACT.Exp).then_inc(sem("ssm.exp"), 1)
                if h in (1, 3, 5):
                    plain(PAIR0["in2_z"] + (5 + h // 2) // 2, (5 + h // 2) % 2)
                if h == 6:
                    z_sigmoid(1)
                if h >= 7:
                    norm_high(h - 7)
                if h == 9:
                    ssm_squares(0)
                if h == 12:
                    root("ng0", 512)
            norm_high(9)
            ssm_squares(1)
            for k in range(10, 12):
                norm_high(k)
            root("ng1", 512)
            for k in range(12, 16):
                norm_high(k)

            def gated_unit(name, pair, par, m, block, gate, squares, ahead=True):
                take_half(pair, par, scale=mod[:, bass.ds(gate + block, 1)])
                if ahead:
                    cast_high(pair + 1, par, 0)
                    cast_high(pair + 1, par, 1)
                if squares:
                    act.wait_ge(sem(name + ".x"), m + 1)
                    A(wide[par], xb(block), ACT.Square).then_inc(sem(name + ".squared"), 1)
                    if name == "down":
                        A(zb(block), xb(block), ACT.Copy, scale=V("g_out", block)).then_inc(sem("down.gained"), 1)

            with act.Fori(0, 8) as i:
                for par in range(2):
                    gated_unit("out2", PAIR0["out2"] + i, par, 2 * i + par, 2 * i + par, 32, True)
            root("n4")
            for k in range(NC):
                act.wait_ge(sem("normed"), 2 * NC + k + 1)
                A(H[:, k, 0:T], work(4 + k % 4), ACT.Identity, bias=mod[:, 48 + k:49 + k]).then_inc(sem("h_high"), 1)

            def ffn_group(g, final):
                pair = PAIR0["ffn"] + 19 * g
                load_sigmoid()
                with act.Fori(0, FFN_BLOCKS) as i:
                    take_half(pair + i, 0)
                    cast_high(pair + i + 1, 0, 0)
                    cast_high(pair + i + 1, 0, 1)
                    act.wait_ge(sem("up.conv"), 2 * FFN_BLOCKS * g + 2 * i + 1)
                    A(sig[0], conv[0], ACT.Sigmoid).then_inc(sem("up.sig"), 1)
                    take_half(pair + i, 1)
                    cast_high(pair + i + 1, 1, 0)
                    act.wait_ge(sem("up.act"), FFN_BLOCKS * g + i + 1)
                    A(ob(U, i, 0), wide[0], ACT.Copy).then_inc(sem("u_high"), 1)
                    cast_high(pair + i + 1, 1, 1)
                pair = pair + FFN_BLOCKS
                with act.Fori(0, 7 if final else 8) as i:
                    for par in range(2):
                        gated_unit("down", pair + i, par, 16 * g + 2 * i + par, 2 * i + par, 80, final)
                if final:
                    for par in range(2):
                        gated_unit("down", pair + 7, par, 16 * g + 14 + par, 14 + par, 80, True, ahead=False)

            with act.Fori(0, FFN_GROUPS - 1) as g:
                ffn_group(g, False)
            ffn_group(FFN_GROUPS - 1, True)
            root("n5")

        @block.vector
        def _(dve):
            v = nc.vector
            TT, STT, TS = v.tensor_tensor, v.scalar_tensor_tensor, v.tensor_scalar

            links = [0]

            def link(ins):
                links[0] += 1
                ins.then_inc(sem("dve_link"), 1)
                dve.wait_ge(sem("dve_link"), links[0])

            def split_low(pair, par, h):
                slot = 2 * par + h
                dve.wait_ge(sem("w_high"), 4 * pair + slot + 1)
                TT(w_lo[:, slot, :], w_raw[:, slot, :], w_hi[:, slot, :].bitcast(F32), ALU.subtract)\
                    .then_inc(sem("w_split"), 1)

            def add_halves(pair, par, out):
                dve.wait_ge(sem("halves"), units_with_half(pair, par))
                TT(out, bank[par][:, 0:T], half[par], ALU.add).then_inc(sem("bank_read"), 1)
                return 2 + 2 * pair + par + 1

            def units_with_half(pair, par):
                skipped = 16 if after_branch[0] else 0
                return 2 * pair + par + 1 - skipped

            after_branch = [False]

            def add_ada(chunk, k, par):
                dve.wait_ge(sem("ada_landed%d" % par), turn_value(chunk, par))
                dve.wait_ge(sem("ada_acc"), chunk + 1)
                STT(ada_acc[:, :], ada_w[:, par, :], silu_c[:, bass.ds(k, 1)], ada_acc[:, :], ALU.mult, ALU.add)\
                    .then_inc(sem("ada_acc"), 1)

            def turn_value(chunk, par):
                return chunk * 8 + (16 - 8 * par)

            def take_mod(group):
                dve.wait_ge(sem("ada_reduced"), group + 1)
                v.memset(ada_acc[:, :], 0.0).then_inc(sem("ada_zeroed"), 1)
                dve.wait_ge(sem("ada_zeroed"), group + 2)
                n = ADA_COLS // P
                TT(mod[:, bass.ds(group * n, n)], bank[5][:, 0:n], V("b_ada", group * n, n), ALU.add)\
                    .then_inc(sem("mod_ready"), 1)

            def inverse(name, out=R[:, :]):
                dve.wait_ge(sem("norm.root"), NTH[name])
                v.reciprocal(out, std).then_inc(sem("norm.inverse"), 1)
                dve.wait_ge(sem("norm.inverse"), NTH[name])

            v.memset(epsb[:, :], EPS)
            v.memset(ada_acc[:, :], 0.0).then_inc(sem("ada_zeroed"), 1)
            v.memset(rel[REL_BUCKETS:REL_BUCKETS + 1, :], 1.0).then_inc(sem("rel_ones"), 1)
            v.memset(ones[:, :], 1.0).then_inc(sem("ones_ready"), 1)
            dve.sem_inc(sem("w_split"), CREDIT)
            dve.sem_inc(sem("piece_used"), CREDIT)
            dve.sem_inc(sem("bank_read"), 2)
            dve.sem_inc(sem("ada_acc"), 1)
            dve.sem_inc(sem("ada_credit"), 1)
            dve.wait_ge(sem("vec_landed"), 16)

            def first_low(i):
                dve.wait_ge(sem("w_high"), i + 1)
                TT(w_lo[:, i, :], w_raw[:, i, :], w_hi[:, i, :].bitcast(F32), ALU.subtract).then_inc(sem("w_split"), 1)

            for i in range(4):
                for k in range(4 * i, 4 * i + 4):
                    dve.wait_ge(sem("h_high"), k + 1)
                    STT(H[:, k, T:2 * T], X[:, k, :], V("g_mix", k), H[:, k, 0:T].bitcast(F32), ALU.mult, ALU.subtract)\
                        .then_inc(sem("h_ready"), 1)
                if i < 2:
                    first_low(i)
            first_low(2)
            first_low(3)
            dve.wait_ge(sem("x_squares"), 4)
            v.tensor_reduce(ss[:, :], Z[:, 0:NC, :].rearrange("p c t -> p t c"), AX_X, ALU.add)\
                .then_inc(sem("norm.squares"), 1)

            def plain_normed(name, pair, par, out, chunk=None, k=None, total=total, scale=R[:, :]):
                if chunk is not None:
                    add_ada(chunk, k, par)
                n = add_halves(pair, par, total[par])
                split_low(pair + 1, par, 0)
                dve.wait_ge(sem("bank_read"), n)
                TT(out, total[par], scale, ALU.mult).then_inc(sem(name + ".out"), 1)
                split_low(pair + 1, par, 1)

            for par in range(2):
                n = add_halves(PAIR0["gate"], par, total[par])
                split_low(PAIR0["gate"] + 1, par, 0)
                split_low(PAIR0["gate"] + 1, par, 1)
            dve.wait_ge(sem("ada_zeroed"), 1)
            dve.wait_ge(sem("c_sig"), 1)
            link(TT(silu_c[:, :], V("c", 0, 16), small[:, 16:32], ALU.mult))
            for par in range(2):
                add_ada(ADA0["gate"] + par, par, par)
            inverse("n1")
            dve.wait_ge(sem("bank_read"), n)
            for par in range(2):
                TT(flat(G[:, 0:1, par, :]), total[par], R[:, :], ALU.mult).then_inc(sem("gate.out"), 1)
            link(TT(R_squared, R[:, :], R[:, :], ALU.mult))
            dve.wait_ge(sem("gate.out"), 2)
            dve.wait_ge(sem("n1.stdtok"), 1)
            link(v.reciprocal(small[:, 2:4], small[:, 0:2]))
            dve.wait_ge(sem("wn_high"), 1)
            TT(wf[:, :, 8:16], wf_raw, wf[:, :, 0:8].bitcast(F32), ALU.subtract).then_inc(sem("wn_split"), 1)
            with dve.Fori(1, 8) as i:
                for par in range(2):
                    plain_normed("gate", PAIR0["gate"] + i, par, flat(G[:, bass.ds(i, 1), par, :]),
                                 ADA0["gate"] + 2 * i + par, 2 * i + par)
            take_mod(0)
            dve.wait_ge(sem("soft.half"), 2)
            y, nabs, l = small[:, 48:64], small[:, 80:96], small[:, 96:112]
            logf = small[:, 112:128]
            for b in range(2):
                s = slice(8 * b, 8 * b + 8)
                link(TT(y[:, s], bank[4][:, 32 * b:32 * b + 8], small[:, 32 + 8 * b:40 + 8 * b], ALU.add))
                link(STT(y[:, s], y[:, s], small[:, 2 + b:3 + b], V("b_f", 0, 8), ALU.mult, ALU.add))
            STT(nabs, y, -1.0, y, ALU.mult, ALU.min).then_inc(sem("soft.nabs"), 1)
            dve.wait_ge(sem("soft.ln"), 1)
            link(STT(logf, y, 0.0, l, ALU.min, ALU.subtract))
            dve.wait_ge(sem("wn_high"), 2)
            TT(wdt[:, :, 16:32], wdt_raw, wdt[:, :, 0:16].bitcast(F32), ALU.subtract).then_inc(sem("wn_split"), 1)
            with dve.Fori(0, 8) as i:
                for par in range(2):
                    m = 2 * i + par
                    plain_normed("conv_in", PAIR0["conv_in"] + i, par, zb(m), ADA0["conv_in"] + m, m,
                                 scale=R_squared if par else R[:, :])
            take_mod(1)
            with dve.Fori(0, 4) as i:
                for par in range(2):
                    pair, m = PAIR0["conv_mul"] + i, 2 * i + par
                    n = add_halves(pair, par, total[par])
                    split_low(pair + 1, par, 0)
                    dve.wait_ge(sem("bank_read"), n)
                    TT(total[par], total[par], zb(2 * m + 1), ALU.mult).then_inc(sem("conv_mul.u"), 1)
                    dve.wait_ge(sem("conv_mul.u"), m + 1)
                    u = total[par]
                    TS(conv[par], u, V("conv_w", 16 + m), None, ALU.mult).then_inc(sem("tap"), 1)
                    dve.wait_ge(sem("tap"), 3 * m + 1)
                    STT(conv[par][:, 1:T], u[:, 0:T - 1], V("conv_w", 8 + m), conv[par][:, 1:T], ALU.mult, ALU.add)\
                        .then_inc(sem("tap"), 1)
                    dve.wait_ge(sem("tap"), 3 * m + 2)
                    STT(conv[par][:, 2:T], u[:, 0:T - 2], V("conv_w", m), conv[par][:, 2:T], ALU.mult, ALU.add)\
                        .then_inc(sem("tap"), 1)
                    dve.wait_ge(sem("tap"), 3 * m + 3)
                    TT(wide[par], conv[par], zb(2 * m), ALU.mult).then_inc(sem("conv_mul.y"), 1)
                    split_low(pair + 1, par, 1)
                    dve.wait_ge(sem("conv_mul.high"), m + 1)
                    TT(ob(B, m, 1), wide[par], ob(B, m, 0).bitcast(F32), ALU.subtract).then_inc(sem("branch.operand"), 1)
            with dve.Fori(0, 4) as i:
                for par in range(2):
                    m = 2 * i + par
                    plain_normed("v", PAIR0["v"] + i, par, zb(32 + m))
            with dve.Fori(0, 8) as i:
                for par in range(2):
                    m = 2 * i + par
                    plain_normed("qk", PAIR0["qk"] + i, par, zb(16 + m), ADA0["qk"] + m, m)
            take_mod(2)

            def decay_operands(name, tl, h, a0, a1):
                TS(tl.dec0[h % 2], LEO, a0, None, ALU.mult).then_inc(sem(name + ".decay_ready"), 1)
                TS(tl.dec1[h % 2], LE, a1, None, ALU.mult).then_inc(sem(name + ".decay_ready"), 1)

            def attention(name, tl, decay, fill, out_sem):
                def maxes(h):
                    dve.wait_ge(sem(name + ".scores"), h + 1)
                    for b, (lo, up) in enumerate(((0, 128), (128, 384))):
                        c = 128 + 2 * h + b
                        v.tensor_reduce(small[:, c:c + 1], bank[2 + h % 2][:, lo:up], AX_X, ALU.max, negate=True)\
                            .then_inc(sem(name + ".maxes"), 1)
                    if decay and h + 2 < N_HEADS:
                        decay_operands(name, tl, h + 2, logf[:, h + 2:h + 3], logf[:, 8 + h + 2:9 + h + 2])

                def normalise(h):
                    dve.wait_ge(sem(name + ".exps"), 2 * h + 2)
                    c = 144 + 2 * h
                    link(v.reciprocal(small[:, c + 16:c + 18], small[:, c:c + 2]))
                    for b, (lo, up) in enumerate(((0, 128), (128, 384))):
                        TS(tl.prob[h % 2][:, lo:up], tl.prob[h % 2][:, lo:up], small[:, c + 16 + b:c + 17 + b], None, ALU.mult)\
                            .then_inc(sem(name + ".probs"), 1)

                def finish(h):
                    if decay:
                        dve.wait_ge(sem(name + ".high"), h + 1)
                        TT(ob(B, 8 + h, 1), bank[7][:, 0:256], ob(B, 8 + h, 0).bitcast(F32), ALU.subtract)\
                            .then_inc(sem(out_sem), 1)
                    else:
                        dve.wait_ge(sem(name + ".squared"), h + 1)
                        v.tensor_copy(zb(h), bank[7][:, 0:256]).then_inc(sem(out_sem), 1)
                        if h:
                            dve.wait_ge(sem("na.ss"), h)
                            TT(ss[:, :], ss[:, :], zb(8 + h), ALU.add).then_inc(sem("na.ss"), 1)
                        else:
                            v.tensor_copy(ss[:, :], zb(8)).then_inc(sem("na.ss"), 1)

                if decay:
                    for h in range(2):
                        decay_operands(name, tl, h, logf[:, h:h + 1], logf[:, 8 + h:9 + h])
                maxes(0)
                normalise(0)
                for h in range(N_HEADS):
                    if h:
                        finish(h - 1)
                    fill(h, 0)
                    if h + 1 < N_HEADS:
                        maxes(h + 1)
                        normalise(h + 1)
                    fill(h, 1)
                finish(N_HEADS - 1)

            dve.wait_ge(sem("con_landed"), 32)
            attention("at1", at1, True, lambda h, par: plain_normed(
                "gate", PAIR0["gate2"] + h, par, flat(G[:, 8 + h:9 + h, par, :]), total=gate_total), "branch.operand")
            dve.sem_inc(sem("branch.gated"), 4)
            with dve.Fori(0, 8) as i:
                for par in range(2):
                    pair, m = PAIR0["branch"] + i, 2 * i + par
                    dve.wait_ge(sem("halves_b"), 2 * m + 2)
                    TT(total[par], bank[par][:, 0:T], half[par], ALU.add).then_inc(sem("branch.sum"), 1)
                    TT(conv[par], bank[2 + par][:, 0:T], half2[par], ALU.add).then_inc(sem("bank_read"), 1)
                    split_low(pair + 1, par, 0)
                    dve.wait_ge(sem("gates_open"), 2 * m + 2)
                    dve.wait_ge(sem("branch.sum"), m + 1)
                    dve.wait_ge(sem("bank_read"), 2 + 2 * pair + par + 1)
                    TT(total[par], total[par], sig[par], ALU.mult).then_inc(sem("branch.gated"), 1)
                    TT(conv[par], conv[par], wide[par], ALU.mult).then_inc(sem("branch.gated"), 1)
                    dve.wait_ge(sem("branch.gated"), 4 + 2 * m + 2)
                    TT(conv[par], total[par], conv[par], ALU.add).then_inc(sem("merge"), 1)
                    split_low(pair + 1, par, 1)
                    dve.wait_ge(sem("merged_high"), m + 1)
                    TT(ob(U, m, 1), conv[par], ob(U, m, 0).bitcast(F32), ALU.subtract).then_inc(sem("merged"), 1)
            after_branch[0] = True

            def clear_ss(name):
                if name == "ff":
                    v.memset(ssg, 0.0)
                v.memset(ss[:, :], 0.0).then_inc(sem(name + ".ss"), 1)

            def add_square(name, par, local):
                dve.wait_ge(sem(name + ".squared"), local + 1)
                dve.wait_ge(sem(name + ".ss"), local + 1)
                TT(ss[:, :], ss[:, :], wide[par], ALU.add).then_inc(sem(name + ".ss"), 1)

            def signal_squares(name, source):
                dve.wait_ge(sem(source + ".ss"), 1 + NC)
                dve.sem_inc(sem("norm.squares"), 1)

            clear_ss("mix")
            with dve.Fori(0, 8) as i:
                for par in range(2):
                    pair, m = PAIR0["mix"] + i, 2 * i + par
                    add_ada(ADA0["mix"] + m, m, par)
                    n = add_halves(pair, par, total[par])
                    dve.wait_ge(sem("bank_read"), n)
                    TT(xb(m), xb(m), total[par], ALU.add).then_inc(sem("mix.x"), 1)
                    split_low(pair + 1, par, 0)
                    split_low(pair + 1, par, 1)
                    dve.wait_ge(sem("h_high"), CHUNKS["h2"] + m + 1)
                    dve.wait_ge(sem("mix.x"), m + 1)
                    STT(ob(H, m, 1), xb(m), V("g_mlp", m), ob(H, m, 0).bitcast(F32), ALU.mult, ALU.subtract)\
                        .then_inc(sem("h_ready"), 1)
                    add_square("mix", par, m)
            signal_squares("n2", "mix")
            take_mod(3)
            inverse("n2")

            def ff_group(g, final):
                pair = PAIR0["ff"] + 16 * g
                with dve.Fori(0, 8) as i:
                    for par in range(2):
                        u = 2 * i + par
                        m = 16 * g + u
                        add_ada(ADA0["ff"] + 32 * g + u, u, par)
                        n = add_halves(pair + i, par, total[par])
                        dve.wait_ge(sem("bank_read"), n)
                        STT(wide[par], total[par], 0.0, R[:, :], ALU.max, ALU.mult).then_inc(sem("ff.relu"), 1)
                        split_low(pair + i + 1, par, 0)
                        dve.wait_ge(sem("ff.u_full"), m + 1)
                        TT(ob(U, u, 1), conv[par], ob(U, u, 0).bitcast(F32), ALU.subtract).then_inc(sem("ff.u_ready"), 1)
                        split_low(pair + i + 1, par, 1)
                take_mod(2 * g + 4)
                if final:
                    clear_ss("ff")
                with dve.Fori(0, 8) as i:
                    for par in range(2):
                        u = 2 * i + par
                        m = 16 * g + u
                        add_ada(ADA0["ff"] + 32 * g + 16 + u, u, par)
                        n = add_halves(pair + 8 + i, par, total[par])
                        if not final:
                            split_low(pair + 8 + i + 1, par, 0)
                        dve.wait_ge(sem("bank_read"), n)
                        TT(xb(u), xb(u), total[par], ALU.add).then_inc(sem("ff.x"), 1)
                        if final:
                            split_low(pair + 8 + i + 1, par, 0)
                        split_low(pair + 8 + i + 1, par, 1)
                        if final:
                            add_square("ff", par, u)
                            dve.wait_ge(sem("ff.squared_g"), u + 1)
                            TT(ssg, ssg, conv[par], ALU.add).then_inc(sem("ff.ssg"), 1)
                take_mod(2 * g + 5)

            with dve.Fori(0, FF_GROUPS - 1) as g:
                ff_group(g, False)
            ff_group(FF_GROUPS - 1, True)
            signal_squares("n3", "ff")
            dve.wait_ge(sem("ff.ssg"), NC)
            dve.sem_inc(sem("norm.squares"), 1)
            dve.wait_ge(sem("rel_made"), 1)
            v.tensor_copy(relrow[:, :], bank[6][0:8, 0:REL_W]).then_inc(sem("relrow_ready"), 1)
            dve.wait_ge(sem("mod_ready"), ADA_GROUPS)
            link(STT(g1[:, :], mod[:, 16:32], 1.0, V("g_mix2", 0, 16), ALU.add, ALU.mult))
            link(TT(g1[:, :], g1[:, :], V("g_final", 0, 16), ALU.mult))
            link(STT(g2[:, :], mod[:, 64:80], 1.0, V("g_ffn", 0, 16), ALU.add, ALU.mult))
            dve.wait_ge(sem("ff.x"), FF_GROUPS * NC)

            def modulated(gain, shift, chunks, normed):
                for k in range(NC + 1):
                    if k < NC:
                        if k >= 4:
                            dve.wait_ge(sem("h_ready"), chunks + k - 3)
                        STT(work(4 + k % 4), xb(k), gain[:, k:k + 1], R[:, :], ALU.mult, ALU.mult)\
                            .then_inc(sem("normed"), 1)
                    if k:
                        j = k - 1
                        dve.wait_ge(sem("h_high"), chunks + j + 1)
                        dve.wait_ge(sem("normed"), normed + j + 1)
                        STT(H[:, j, T:2 * T], work(4 + j % 4), mod[:, shift + j:shift + j + 1], H[:, j, 0:T].bitcast(F32),
                            ALU.add, ALU.subtract).then_inc(sem("h_ready"), 1)

            inverse("n3", R2)
            TT(work(1), R2, R2, ALU.mult).then_inc(sem("n3.inverted"), 1)
            dve.wait_ge(sem("norm.summed"), NTH["n3b"])
            dve.wait_ge(sem("n3.inverted"), 1)
            TT(work(0), bank[7][:, 0:T], work(1), ALU.mult).then_inc(sem("n3.inverted"), 1)
            inverse("n3b")
            TT(R[:, :], R[:, :], R2, ALU.mult).then_inc(sem("n3.inverted"), 1)
            dve.wait_ge(sem("n3.inverted"), 3)
            modulated(g1, 0, CHUNKS["h3"], 0)

            def plain_unit(pair, par, block):
                dve.wait_ge(sem("halves"), units_with_half(pair, par))
                TT(zb(block), bank[par][:, 0:T], half[par], ALU.add).then_inc(sem("bank_read"), 1)
                split_low(pair + 1, par, 0)
                split_low(pair + 1, par, 1)

            with dve.Fori(0, 6) as i:
                for par in range(2):
                    plain_unit(PAIR0["in2"] + i, par, 2 * i + par)
            for k in range(NC):
                STT(xb(k), xb(k), V("g_final", k), R2, ALU.mult, ALU.mult).then_inc(sem("n3.x"), 1)
            dve.wait_ge(sem("soft.half"), 4)
            y, nabs, l = small[:, 320:352], small[:, 256:288], small[:, 288:320]
            dt, dta = small[:, 352:384], small[:, 384:416]
            for b in range(2):
                s = slice(16 * b, 16 * b + 16)
                link(TT(y[:, s], bank[4][:, 64 * b:64 * b + 16], small[:, 192 + 16 * b:208 + 16 * b], ALU.add))
                link(TT(y[:, s], y[:, s], V("dt_bias", 0, 16), ALU.add))
            STT(nabs, y, -1.0, y, ALU.mult, ALU.min).then_inc(sem("soft.nabs"), 1)
            dve.wait_ge(sem("soft.ln"), 2)
            link(STT(dt, y, 0.0, l, ALU.max, ALU.add))
            dve.wait_ge(sem("a_exp"), 1)
            for b in range(2):
                s = slice(16 * b, 16 * b + 16)
                link(STT(dta[:, s], dt[:, s], -1.0, small[:, 480:496], ALU.mult, ALU.mult))
            with dve.Fori(6, 12) as i:
                for par in range(2):
                    plain_unit(PAIR0["in2"] + i, par, 2 * i + par)
            dve.wait_ge(sem("bank_read"), 2 + 2 * PAIR0["in2_conv"])
            dve.sem_inc(sem("in2.out"), 24)
            dve.wait_ge(sem("relrow_stored"), 16)

            def conv_unit(pair, par, m):
                n = add_halves(pair, par, total[par])
                split_low(pair + 1, par, 0)
                dve.wait_ge(sem("bank_read"), n)
                u = total[par]
                TS(conv[par], u, V("ssm_w", 36 + m), V("ssm_b", m), ALU.mult, ALU.add).then_inc(sem("tap"), 1)
                for d in range(1, 4):
                    dve.wait_ge(sem("tap"), TAPS["in2_conv"] + 3 * m + d)
                    step = STT(conv[par][:, d:T], u[:, 0:T - d], V("ssm_w", 36 - 12 * d + m), conv[par][:, d:T],
                               ALU.mult, ALU.add)
                    step.then_inc(sem("tap" if d < 3 else "in2_conv.conv"), 1)
                split_low(pair + 1, par, 1)
                dve.wait_ge(sem("in2_conv.sig"), m + 1)
                dve.wait_ge(sem("in2_conv.conv"), m + 1)
                TT(zb(32 + m), conv[par], sig[par], ALU.mult).then_inc(sem("in2_conv.out"), 1)

            def second_fill(h, par):
                m = 2 * h + par
                if m < CONV_CH:
                    conv_unit(PAIR0["in2_conv"] + h, par, m)
                else:
                    plain_unit(PAIR0["in2_conv"] + h, par, 24 + m - CONV_CH)

            attention("at2", at2, False, second_fill, "at2.out")
            dve.wait_ge(sem("na.ss"), N_HEADS)
            dve.sem_inc(sem("norm.squares"), 1)

            def z_unit(u):
                plain_unit(PAIR0["in2_z"] + u // 2, u % 2, 24 + u)

            def ssm_decay(h):
                decay_operands("ssm", at2, h, dta[:, h:h + 1], dta[:, 16 + h:17 + h])

            def silu_z(grp):
                dve.wait_ge(sem("z_sig"), grp + 1)
                link(TT(zb(24 + 4 * grp, 4), zb(24 + 4 * grp, 4), adaf[:, 1024 * grp:1024 * grp + 1024], ALU.mult))

            def gate(j):
                ssm_y(dve, STT, j)
                dve.wait_ge(sem("ssm.y"), j + 1)
                TT(zb(32 + j), zb(32 + j), zb(24 + j), ALU.mult).then_inc(sem("ssm.gated"), 1)

            def norm_squares(first, n):
                v.tensor_reduce(ss[:, :], Z[:, first:first + n, :].rearrange("p c t -> p t c"), AX_X, ALU.add)\
                    .then_inc(sem("norm.squares"), 1)

            def normed_chunk(k):
                if k >= 4:
                    dve.wait_ge(sem("h_ready"), CHUNKS["h4"] + k - 3)
                src, gain = (zb(k), V("g_attn", k)) if k < 8 else (zb(24 + k), V("g_ssm", k - 8))
                STT(work(4 + k % 4), src, gain, R2 if 8 <= k < 12 else R[:, :], ALU.mult, ALU.mult)\
                    .then_inc(sem("normed"), 1)

            def low_chunk(k):
                dve.wait_ge(sem("h_high"), CHUNKS["h4"] + k + 1)
                dve.wait_ge(sem("normed"), NC + k + 1)
                TT(H[:, k, T:2 * T], work(4 + k % 4), H[:, k, 0:T].bitcast(F32), ALU.subtract).then_inc(sem("h_ready"), 1)

            dve.wait_ge(sem("cb_ready"), 2)
            for grp in range(2):
                TT(cbm[grp], bank[2 + grp][:, 0:384], LEOL, ALU.mult).then_inc(sem("cb_masked"), 1)
            for n in range(4):
                b, q = n // 2, n % 2
                if n == 2:
                    ssm_decay(0)
                    ssm_decay(1)
                    silu_z(0)
                    z_unit(4)
                dve.wait_ge(sem("xs_turned"), n + 1)
                out = xd[:, 1024 * b + 512 * q:1024 * b + 512 * q + 512].rearrange("p (h d) -> p h d", d=64)
                src = bank[4 + n % 2][:, :].rearrange("p (h d) -> p h d", d=64)
                d_ = dt[:, 16 * b + 8 * q:16 * b + 8 * q + 8]
                TT(out, src, d_.unsqueeze(2).to_broadcast([P, 8, 64]), ALU.mult).then_inc(sem("xdt_ready"), 1)
            dve.wait_ge(sem("cb_masked"), 2)
            for h in range(SSM_HEADS):
                dve.wait_ge(sem("ssm.exp"), h + 1)
                if h >= 2:
                    dve.wait_ge(sem("ssm.out"), h - 1)
                TT(ssm_w[h % 2], at2.prob[h % 2], cbm[h // 8], ALU.mult).then_inc(sem("ssm.weights"), 1)
                if h + 2 < SSM_HEADS:
                    ssm_decay(h + 2)
                if h in (1, 3, 5):
                    z_unit(5 + h // 2)
                if h == 1:
                    inverse("na")
                if h == 7:
                    silu_z(1)
                if h % 2 == 0 and h:
                    gate(h // 2 - 1)
                if h == 13:
                    inverse("ng0", R2)
                if h >= 6:
                    normed_chunk(h - 6)
                if h >= 8:
                    low_chunk(h - 8)
                if h == 10:
                    dve.wait_ge(sem("ssm.squared"), 1)
                    norm_squares(16, 4)
            gate(SSM_HEADS // 2 - 1)
            low_chunk(8)
            low_chunk(9)
            for k in range(10, 12):
                normed_chunk(k)
            for k in range(10, 12):
                low_chunk(k)
            dve.wait_ge(sem("ssm.squared"), 2)
            norm_squares(20, 4)
            inverse("ng1")
            for k in range(12, 16):
                normed_chunk(k)
            for k in range(12, 16):
                low_chunk(k)

            def gated(name, pair, par, m, block, gate, squares, ahead=True):
                dve.wait_ge(sem("halves"), units_with_half(pair, par))
                STT(total[par], bank[par][:, 0:T], mod[:, bass.ds(gate + block, 1)], half[par], ALU.mult, ALU.add)\
                    .then_inc(sem("bank_read"), 1)
                if ahead and not squares:
                    split_low(pair + 1, par, 0)
                dve.wait_ge(sem("bank_read"), 2 + 2 * pair + par + 1)
                TT(xb(block), xb(block), total[par], ALU.add).then_inc(sem(name + ".x"), 1)
                if ahead and squares:
                    split_low(pair + 1, par, 0)
                if ahead:
                    split_low(pair + 1, par, 1)
                if squares:
                    add_square(name, par, block)

            dve.wait_ge(sem("n3.x"), NC)
            clear_ss("out2")
            with dve.Fori(0, 8) as i:
                for par in range(2):
                    gated("out2", PAIR0["out2"] + i, par, 2 * i + par, 2 * i + par, 32, True)
            signal_squares("n4", "out2")
            dve.wait_ge(sem("out2.x"), NC)
            inverse("n4")
            modulated(g2, 48, CHUNKS["h5"], 2 * NC)

            def ffn_conv(pair, par, m, n):
                dve.wait_ge(sem("bank_read"), n)
                u = total[par]
                TS(conv[par], u, V("ffn_w", 176 + m), V("ffn_b", m), ALU.mult, ALU.add).then_inc(sem("tap"), 1)
                dve.wait_ge(sem("tap"), TAPS["up"] + 2 * m + 1)
                STT(conv[par][:, 1:T], u[:, 0:T - 1], V("ffn_w", 88 + m), conv[par][:, 1:T], ALU.mult, ALU.add)\
                    .then_inc(sem("tap"), 1)
                dve.wait_ge(sem("tap"), TAPS["up"] + 2 * m + 2)
                STT(conv[par][:, 2:T], u[:, 0:T - 2], V("ffn_w", m), conv[par][:, 2:T], ALU.mult, ALU.add)\
                    .then_inc(sem("up.conv"), 1)

            def ffn_group(g, final):
                pair = PAIR0["ffn"] + 19 * g
                with dve.Fori(0, FFN_BLOCKS) as i:
                    j = FFN_BLOCKS * g + i
                    m = 2 * FFN_BLOCKS * g + 2 * i
                    n = add_halves(pair + i, 0, total[0])
                    split_low(pair + i + 1, 0, 0)
                    ffn_conv(pair + i, 0, m, n)
                    split_low(pair + i + 1, 0, 1)
                    dve.wait_ge(sem("up.sig"), j + 1)
                    TT(wide[1], conv[0], sig[0], ALU.mult).then_inc(sem("up.silu"), 1)
                    n = add_halves(pair + i, 1, total[1])
                    ffn_conv(pair + i, 1, m + 1, n)
                    dve.wait_ge(sem("up.silu"), j + 1)
                    dve.wait_ge(sem("up.conv"), m + 2)
                    TT(wide[0], wide[1], conv[1], ALU.mult).then_inc(sem("up.act"), 1)
                    split_low(pair + i + 1, 1, 0)
                    dve.wait_ge(sem("u_high"), FF_GROUPS * FF_BLOCKS + j + 1)
                    TT(ob(U, i, 1), wide[0], ob(U, i, 0).bitcast(F32), ALU.subtract).then_inc(sem("ffn.u_ready"), 1)
                    split_low(pair + i + 1, 1, 1)
                pair = pair + FFN_BLOCKS
                if final:
                    clear_ss("down")
                with dve.Fori(0, 7 if final else 8) as i:
                    for par in range(2):
                        gated("down", pair + i, par, 16 * g + 2 * i + par, 2 * i + par, 80, final)
                if final:
                    for par in range(2):
                        gated("down", pair + 7, par, 16 * g + 14 + par, 14 + par, 80, True, ahead=False)

            with dve.Fori(0, FFN_GROUPS - 1) as g:
                ffn_group(g, False)
            ffn_group(FFN_GROUPS - 1, True)
            signal_squares("n5", "down")
            inverse("n5")
            dve.wait_ge(sem("down.gained"), NC)
            for m, size in OUT_PARTS:
                TT(Z[:, m:m + size, :], Z[:, m:m + size, :], R[:, :].unsqueeze(1).to_broadcast([P, size, T]), ALU.mult)\
                    .then_inc(sem("final.out"), 1)

        @block.gpsimd
        def _(pool):
            pool.wait_ge(sem("relrow_ready"), 1)
            pool.dma_start(t["rel_rows"], relrow[:, :]).then_inc(sem("relrow_stored"), 16)
            pool.wait_ge(sem("relrow_stored"), 16)
            for h in range(N_HEADS):
                if h >= 2:
                    pool.wait_ge(sem("at2.scores"), h - 1)
                rows = bass.AP(t["rel_rows"].tensor, h * REL_W, [[1, P], [1, 256]])
                pool.dma_start(relb[h % 2], rows).then_inc(sem("relb_landed%d" % (h % 2)), 16)


def make_constants():
    t_ = np.arange(P)
    ident = np.eye(P)
    le = (t_[:, None] <= t_[None, :]) * 1.0
    gt = (t_[:, None] > t_[None, :]) * 1.0
    one = np.ones((P, P))
    causal = np.where(t_[None, :] <= t_[:, None], 0.0, FAR)
    con = np.concatenate([ident, le, one, le, one, gt, causal, 0 * one, causal, ident[:, ::-1]], 1)
    return np.ascontiguousarray(con.astype(np.float32))


def make_onehot():
    dist = 255 - np.arange(REL_W)
    n = np.maximum(dist, 0)
    exact = REL_BUCKETS // 2
    nf = np.maximum(n, exact).astype(np.float32)
    large = exact + (np.log(nf / np.float32(exact)) / np.float32(np.log(REL_MAX_DIST / exact))
                     * np.float32(REL_BUCKETS - exact)).astype(np.int32)
    bucket = np.where(n < exact, n, np.minimum(large, REL_BUCKETS - 1))
    hot = np.zeros((REL_BUCKETS + 1, REL_W), np.float32)
    on = dist >= 0
    hot[bucket[on], np.arange(REL_W)[on]] = 1.0
    hot[REL_BUCKETS, ~on] = FAR
    return hot


def tiles(w):
    k, n = w.shape
    return np.ascontiguousarray(w.reshape(k // P, P, n // P, P).transpose(2, 1, 0, 3)).reshape(n // P, P, k)


def in_turn(a, b):
    return np.stack([tiles(a), tiles(b)], 1).reshape(-1, P, a.shape[0])


def columns(v):
    return v.reshape(-1, P).T


def layout(a):
    a = {k: np.asarray(v) for k, v in a.items()}
    w_in, w2 = a["w_in"][0], a["w_in_2"][0]
    gates = tiles(w_in[:, 6152:10248]).reshape(2, NC, P, D).transpose(1, 0, 2, 3).reshape(32, P, D)
    cb, cc, cv = w_in[:, 0:1024], w_in[:, 1024:2048], w_in[:, 2048:3072]
    ff1, ff2 = tiles(a["w_ff1"][0]), a["w_ff2"][0].reshape(FF_GROUPS, -1, D)
    up = tiles(a["w_up_2"][0]).reshape(2, FFN // P, P, D).transpose(1, 0, 2, 3).reshape(-1, P, D)
    down = a["w_down_2"][0].reshape(FFN_GROUPS, -1, D)
    by_unit = lambda v: columns(v).reshape(P, 2, FFN // P).transpose(0, 2, 1).reshape(P, -1)
    row = lambda v: np.broadcast_to(v, (P, v.shape[-1]))
    conv2 = a["conv_ffn_w_2"][0]
    vectors = {
        "g_mix": columns(a["g_mix"]), "g_mlp": columns(a["g_mlp"]), "b_gate": columns(a["b_gate"]),
        "conv_w": np.concatenate([columns(a["conv_w"][0, j]) for j in range(3)], 1),
        "b_f": row(a["b_f"]), "g_final": columns(a["g_final"]), "c": columns(a["c_2"]),
        "b_ada": columns(a["b_ada_2"]), "g_mix2": columns(a["norm_mix_g_2"]), "g_attn": columns(a["attn_norm_g_2"]),
        "ssm_w": np.concatenate([columns(a["conv_ssm_w_2"][0, j]) for j in range(4)], 1),
        "ssm_b": columns(a["conv_ssm_b_2"]), "dt_bias": row(a["dt_bias_2"]), "a_log": row(a["a_log_2"]),
        "d_skip": columns(np.repeat(a["d_skip_2"][0], SSM_DIM)), "g_ssm": columns(a["ssm_norm_g_2"]),
        "g_ffn": columns(a["norm_ffn_g_2"]),
        "ffn_w": np.concatenate([by_unit(conv2[j]) for j in range(3)], 1), "ffn_b": by_unit(a["conv_ffn_b_2"]),
        "g_out": columns(a["final_norm_g_2"]),
    }
    by_chunk = lambda w: np.ascontiguousarray(w.reshape(NC, P, -1).transpose(1, 0, 2))
    arrays = {
        "x": by_chunk(a["x"][0].T),
        "vectors": np.concatenate([vectors[n] for n, _ in VEC_SIZES], 1),
        "consts": make_constants(),
        "rel_onehot": make_onehot(),
        "rel_bias": a["rel_bias_2"],
        "w_gate": gates,
        "w_z": np.concatenate([in_turn(cb, cc), tiles(cv), tiles(w_in[:, 5120:6144]),
                               in_turn(w_in[:, 3072:4096], w_in[:, 4096:5120])]),
        "w_f": by_chunk(w_in[:, 6144:6152]),
        "w_branch": np.concatenate([tiles(a["w_conv_out"][0]), tiles(a["w_attn_out"][0])], 2),
        "w_mix": tiles(a["w_mix_out"][0]),
        "w_ff1": ff1,
        "w_ff2": np.concatenate([tiles(g) for g in ff2]),
        "w_ada": a["w_ada_2"][0].reshape(NC, P, ADA_GROUPS, ADA_COLS).transpose(2, 0, 1, 3).reshape(-1, P, ADA_COLS),
        "w_in2": np.concatenate([tiles(w) for w in (w2[:, 0:3072], w2[:, 3072:4096], w2[:, 5120:5632], w2[:, 4096:5120])]),
        "w_dt": by_chunk(w2[:, 5632:5648]),
        "w_out2": tiles(a["w_out_2"][0]),
        "w_up": up,
        "w_down": np.concatenate([tiles(g) for g in down]),
    }
    return {name: np.ascontiguousarray(array) for name, array in arrays.items()}


def kernel(**a):
    import concourse.bacc as bacc
    from concourse.bass_utils import run_bass_kernel_spmd

    arrays = layout(a)
    nc = bacc.Bacc("TRN2", target_bir_lowering=False, num_devices=1)
    t, given = {}, {}
    for name, array in arrays.items():
        given["in_" + name] = array
        t[name] = nc.dram_tensor("in_" + name, array.shape, F32, kind="ExternalInput").ap()
    t["out"] = nc.dram_tensor("out_xT", (P, NC, T), F32, kind="ExternalOutput").ap()
    t["rel_rows"] = nc.dram_tensor("rel_rows", (N_HEADS, REL_W), F32, kind="Internal").ap()
    build(nc, t)
    r = run_bass_kernel_spmd(nc, [given], core_ids=[0])
    out = r.results[0]["out_xT"]
    return np.ascontiguousarray(out.transpose(2, 1, 0)).reshape(1, T, D)
```
